# Optimizing a Trainium2 kernel written in Bass

```python
import jax
import jax.numpy as jnp
from jax import lax
import numpy as np
import math

D_MODEL = 1024
BATCH = 1
SEQ = 256
DEPTH = 1

CHUNK = 64
HG_HEADS = 8
HG_DK = 128
HG_DV = 128
HG_KEY_WIDTH = HG_HEADS * HG_DK
HG_WIDTH = HG_HEADS * HG_DV
SB_HEADS = 16
SB_DH = 64
SB_WIDTH = SB_HEADS * SB_DH
SB_BLOCK = 128
FF_HIDDEN = (8 * D_MODEL + 3 * 256 - 1) // (3 * 256) * 256
IN_SPLITS = (HG_KEY_WIDTH, HG_KEY_WIDTH, HG_WIDTH, HG_WIDTH, SB_WIDTH, SB_WIDTH, SB_WIDTH, D_MODEL, D_MODEL)
IN_WIDTH = sum(IN_SPLITS)
EPS = 1e-6


def rms_norm(x, gain):
    x32 = x.astype(jnp.float32)
    y = x32 * lax.rsqrt(jnp.mean(x32 * x32, axis=-1, keepdims=True) + EPS) * gain.astype(jnp.float32)
    return y.astype(x.dtype)

def split_cols(t, widths):
    outs, start = [], 0
    for w in widths:
        outs.append(t[..., start:start + w])
        start += w
    return outs

def hgrn2_mixer(q, f_raw, i, lb):
    b, s, _ = q.shape
    n = s // CHUNK
    lb = lb.astype(jnp.float32)
    f = lb + (1.0 - lb) * jax.nn.sigmoid(f_raw.astype(jnp.float32))
    log_f = jnp.log(f)
    k = 1.0 - f

    def chunks(t, d):
        return t.astype(jnp.float32).reshape(b, n, CHUNK, HG_HEADS, d).transpose(1, 0, 3, 2, 4)

    qc, kc, gc = chunks(q, HG_DK), chunks(k, HG_DK), chunks(log_f, HG_DK)
    vc = chunks(i, HG_DV)
    causal = jnp.tril(jnp.ones((CHUNK, CHUNK), dtype=bool))[:, :, None]

    def step(state, inp):
        q_c, k_c, v_c, g_c = inp
        cum = jnp.cumsum(g_c, axis=-2)
        diff = cum[:, :, :, None, :] - cum[:, :, None, :, :]
        decay = jnp.exp(jnp.where(causal, diff, -jnp.inf))
        scores = jnp.einsum('bhtd,bhtsd,bhsd->bhts', q_c, decay, k_c)
        o = (jnp.einsum('bhts,bhsv->bhtv', scores, v_c)
             + jnp.einsum('bhtd,bhdv->bhtv', q_c * jnp.exp(cum), state))
        last = cum[:, :, -1:, :]
        state = (jnp.exp(last[:, :, 0, :, None]) * state
                 + jnp.einsum('bhsd,bhsv->bhdv', k_c * jnp.exp(last - cum), v_c))
        return state, o

    s0 = jnp.zeros((b, HG_HEADS, HG_DK, HG_DV), jnp.float32)
    _, o = lax.scan(step, s0, (qc, kc, vc, gc))
    return o.transpose(1, 0, 3, 2, 4).reshape(b, s, HG_HEADS, HG_DV)

def stick_breaking(q, k, v):
    s_len = q.shape[2]
    scale = 1.0 / float(np.sqrt(SB_DH))
    outs = []
    for blk in range(s_len // SB_BLOCK):
        q0 = blk * SB_BLOCK
        end = q0 + SB_BLOCK
        z = jnp.einsum('bhqd,bhkd->bhqk', q[:, :, q0:end], k[:, :, :end]) * scale
        qpos = q0 + jnp.arange(SB_BLOCK)
        kpos = jnp.arange(end)
        mask = kpos[None, :] < qpos[:, None]
        log_keep = jnp.where(mask, jax.nn.log_sigmoid(-z), 0.0)
        log_w = jax.nn.log_sigmoid(z) + lax.cumsum(log_keep, axis=3, reverse=True) - log_keep
        a = jnp.where(mask, jnp.exp(log_w), 0.0)
        outs.append(jnp.einsum('bhqk,bhkd->bhqd', a, v[:, :, :end]))
    return jnp.concatenate(outs, axis=2)

def first_inputs(seed: int = 0) -> dict:
    key = jax.random.key(seed)
    ks = jax.random.split(key, 14)
    f32 = jnp.float32
    nrm = lambda k, shape, fan: jax.random.normal(k, shape, f32) * (fan ** -0.5)
    gain = lambda k, shape: 1.0 + 0.02 * jax.random.normal(k, shape, f32)
    return {
        'x': jax.random.normal(ks[0], (BATCH, SEQ, D_MODEL), f32),
        'norm1_gain': gain(ks[1], (DEPTH, D_MODEL)),
        'w_in': nrm(ks[2], (DEPTH, D_MODEL, IN_WIDTH), D_MODEL),
        'lb_logits': 0.5 * jax.random.normal(ks[3], (DEPTH + 1, HG_KEY_WIDTH), f32),
        'hg_out_norm': gain(ks[4], (DEPTH, HG_HEADS, HG_DV)),
        'sb_q_norm': gain(ks[5], (DEPTH, SB_HEADS, SB_DH)),
        'sb_k_norm': gain(ks[6], (DEPTH, SB_HEADS, SB_DH)),
        'w_hg_out': nrm(ks[7], (DEPTH, HG_WIDTH, D_MODEL), HG_WIDTH),
        'w_sb_out': nrm(ks[8], (DEPTH, SB_WIDTH, D_MODEL), SB_WIDTH),
        'w_o': nrm(ks[9], (DEPTH, D_MODEL, D_MODEL), D_MODEL),
        'norm2_gain': gain(ks[10], (DEPTH, D_MODEL)),
        'w_ffn_in': nrm(ks[11], (DEPTH, D_MODEL, 2 * FF_HIDDEN), D_MODEL),
        'w_ffn_out': nrm(ks[12], (DEPTH, FF_HIDDEN, D_MODEL), FF_HIDDEN),
    }

def first_block(x, norm1_gain, w_in, lb_logits, hg_out_norm, sb_q_norm, sb_k_norm,
              w_hg_out, w_sb_out, w_o, norm2_gain, w_ffn_in, w_ffn_out):
    b, s, _ = x.shape
    lower_bounds = jnp.cumsum(jax.nn.softmax(lb_logits.astype(jnp.float32), axis=0), axis=0)
    for layer in range(DEPTH):
        h = rms_norm(x, norm1_gain[layer])
        proj = h @ w_in[layer]
        hq, hf, hi, hg, sq, sk, sv, ga, gb = split_cols(proj, IN_SPLITS)

        o_hg = hgrn2_mixer(hq, hf, hi, lower_bounds[layer])
        o_hg = rms_norm(o_hg, hg_out_norm[layer]).reshape(b, s, HG_WIDTH)
        o_hg = o_hg * jax.nn.sigmoid(hg.astype(jnp.float32))
        y_hg = o_hg.astype(x.dtype) @ w_hg_out[layer]

        def heads(t):
            return t.astype(jnp.float32).reshape(b, s, SB_HEADS, SB_DH)
        q = rms_norm(heads(sq), sb_q_norm[layer]).transpose(0, 2, 1, 3)
        k = rms_norm(heads(sk), sb_k_norm[layer]).transpose(0, 2, 1, 3)
        v = heads(sv).transpose(0, 2, 1, 3)
        o_sb = stick_breaking(q, k, v).transpose(0, 2, 1, 3).reshape(b, s, SB_WIDTH)
        y_sb = o_sb.astype(x.dtype) @ w_sb_out[layer]

        mixed = jax.nn.sigmoid(ga) * y_hg + jax.nn.sigmoid(gb) * y_sb
        x = x + mixed @ w_o[layer]

        h2 = rms_norm(x, norm2_gain[layer])
        gate, up = split_cols(h2 @ w_ffn_in[layer], (FF_HIDDEN, FF_HIDDEN))
        x = x + (jax.nn.silu(gate) * up) @ w_ffn_out[layer]
    return x


MEM_LEN = 256
NEG_INF = -1e30
BIG = 1e30

GLA_HEADS = 4
GLA_DK = 64
GLA_DV = 128
GLA_RANK = 16
GLA_TAU = 16.0
GLA_CHUNK = 64

NSA_HEADS = 8
NSA_KV_GROUPS = 2
NSA_HPG = NSA_HEADS // NSA_KV_GROUPS
NSA_DH = 64
CMP_BLOCK = 32
CMP_STRIDE = 16
CMP_HIDDEN = 128
SLC_BLOCK = 64
SLC_TOPK = 16
WINDOW = 512
Q_BLOCK = 128

REL_BUCKETS = 32
REL_MAX_DIST = 2048

XA_HEADS = 4
XA_DH = D_MODEL // XA_HEADS

PEER_HEADS = 8
PEER_NKEYS = 128
PEER_EXPERTS = PEER_NKEYS * PEER_NKEYS
PEER_TOPK = 16
PEER_DKEY = 128
PEER_TOKEN_CHUNK = 128

IN_SIZES = (GLA_HEADS * GLA_DK, GLA_HEADS * GLA_DK, GLA_HEADS * GLA_DV, GLA_HEADS * GLA_DV, GLA_RANK,
            NSA_HEADS * NSA_DH,
            NSA_KV_GROUPS * NSA_DH, NSA_KV_GROUPS * NSA_DH,
            NSA_KV_GROUPS * NSA_DH, NSA_KV_GROUPS * NSA_DH,
            NSA_KV_GROUPS * NSA_DH, NSA_KV_GROUPS * NSA_DH,
            NSA_HEADS * 3)
IN_COLS = sum(IN_SIZES)


def rms_norm_2(x, g):
    xf = x.astype(jnp.float32)
    y = xf * lax.rsqrt(jnp.mean(xf * xf, axis=-1, keepdims=True) + EPS)
    return (y * g.astype(jnp.float32)).astype(x.dtype)

def _masked_softmax(s, mask):
    s = jnp.where(mask, s.astype(jnp.float32), NEG_INF)
    p = jax.nn.softmax(s, axis=-1)
    return p * jnp.any(mask, axis=-1, keepdims=True)

def _t5_bucket(dist):
    n = jnp.maximum(dist, 0)
    max_exact = REL_BUCKETS // 2
    nf = jnp.maximum(n, 1).astype(jnp.float32)
    log_ratio = jnp.log(nf / max_exact) / math.log(REL_MAX_DIST / max_exact)
    large = max_exact + (log_ratio * (REL_BUCKETS - max_exact)).astype(jnp.int32)
    large = jnp.minimum(large, REL_BUCKETS - 1)
    return jnp.where(n < max_exact, n, large)

def _head_bias(dist, rel_bias):
    b = jnp.moveaxis(rel_bias[_t5_bucket(dist)], -1, 0)
    return b.reshape((NSA_KV_GROUPS, NSA_HPG) + dist.shape).astype(jnp.float32)

def _split_cols(z):
    offs = np.cumsum(np.array(IN_SIZES))[:-1].tolist()
    return jnp.split(z, offs, axis=-1)

def _gla_chunked(q, k, v, log_a):
    B, T, H, dk = q.shape
    dv = v.shape[-1]
    C = GLA_CHUNK
    nc = T // C

    def to_chunks(a):
        return a.astype(jnp.float32).reshape(B, nc, C, H, a.shape[-1]).transpose(1, 0, 3, 2, 4)

    qc, kc, vc, ac = to_chunks(q), to_chunks(k), to_chunks(v), to_chunks(log_a)
    causal = jnp.tril(jnp.ones((C, C), dtype=bool))[..., None]

    def step(S, inp):
        qi, ki, vi, ai = inp
        b = jnp.cumsum(ai, axis=-2)
        diff = b[..., :, None, :] - b[..., None, :, :]
        decay = jnp.exp(jnp.where(causal, diff, NEG_INF))
        A = jnp.einsum('bhtd,bhsd,bhtsd->bhts', qi, ki, decay)
        o = jnp.einsum('bhts,bhsv->bhtv', A, vi) + jnp.einsum('bhtd,bhdv->bhtv', qi * jnp.exp(b), S)
        b_last = b[..., -1:, :]
        S_new = jnp.exp(b_last[..., 0, :])[..., None] * S + jnp.einsum(
            'bhsd,bhsv->bhdv', ki * jnp.exp(b_last - b), vi)
        return S_new, o

    S0 = jnp.zeros((B, H, dk, dv), jnp.float32)
    _, o = lax.scan(step, S0, (qc, kc, vc, ac))
    return o.transpose(1, 0, 3, 2, 4).reshape(B, T, H, dv)

def gla_mixer(gq, gk, gv, gr, glr, gate_w2, gate_b, out_norm):
    B, T, _ = gq.shape
    q = gq.reshape(B, T, GLA_HEADS, GLA_DK) * (GLA_DK ** -0.5)
    k = gk.reshape(B, T, GLA_HEADS, GLA_DK)
    v = gv.reshape(B, T, GLA_HEADS, GLA_DV)
    log_a = jax.nn.log_sigmoid((glr @ gate_w2 + gate_b).astype(jnp.float32)) / GLA_TAU
    log_a = log_a.reshape(B, T, GLA_HEADS, GLA_DK)
    o = _gla_chunked(q, k, v, log_a)
    o = rms_norm_2(o, out_norm).reshape(B, T, GLA_HEADS * GLA_DV)
    return (o * jax.nn.silu(gr.astype(jnp.float32))).astype(gq.dtype)

def _compress(kv, pos, w1, w2):
    B, T, G, dh = kv.shape
    n_cmp = (T - CMP_BLOCK) // CMP_STRIDE + 1
    idx = jnp.arange(n_cmp)[:, None] * CMP_STRIDE + jnp.arange(CMP_BLOCK)[None, :]
    blocks = kv[:, idx] + pos[None, None, :, None, :]
    blocks = blocks.transpose(0, 3, 1, 2, 4).reshape(B, G, n_cmp, CMP_BLOCK * dh)
    return jax.nn.gelu(blocks @ w1) @ w2

def _slc_importance(p_grp, n_slc):
    n_cmp = p_grp.shape[-1]
    ratio = SLC_BLOCK // CMP_STRIDE
    back = CMP_BLOCK // CMP_STRIDE - 1
    pad_end = max(ratio * n_slc - n_cmp, 0)
    pp = jnp.pad(p_grp, [(0, 0)] * (p_grp.ndim - 1) + [(back, pad_end)])
    base = jnp.arange(n_slc) * ratio + back
    imp = 0.0
    for r in range(-back, ratio):
        lo = CMP_STRIDE * r
        overlap = min(lo + CMP_BLOCK, SLC_BLOCK) - max(lo, 0)
        imp = imp + (overlap / CMP_BLOCK) * pp[..., base + r]
    return imp

def nsa_mixer(nq, kc, vc, ks, vs, kw, vw, ng, rel_bias, pos_k, pos_v, ck_w1, ck_w2, cv_w1, cv_w2):
    B, T, _ = nq.shape
    G, HPG, dh = NSA_KV_GROUPS, NSA_HPG, NSA_DH
    n_cmp = (T - CMP_BLOCK) // CMP_STRIDE + 1
    n_slc = T // SLC_BLOCK
    n_sel = min(SLC_TOPK, n_slc)
    n_qblk = T // Q_BLOCK
    kv_shape = (B, T, G, dh)

    q = (nq.reshape(B, T, G, HPG, dh) * (dh ** -0.5)).transpose(0, 2, 3, 1, 4)
    gates = jax.nn.sigmoid(ng.astype(jnp.float32)).reshape(B, T, G, HPG, 3).transpose(0, 2, 3, 1, 4)

    k_cmp = _compress(kc.reshape(kv_shape), pos_k, ck_w1, ck_w2)
    v_cmp = _compress(vc.reshape(kv_shape), pos_v, cv_w1, cv_w2)
    k_slc = ks.reshape(kv_shape).transpose(0, 2, 1, 3).reshape(B, G, n_slc, SLC_BLOCK, dh)
    v_slc = vs.reshape(kv_shape).transpose(0, 2, 1, 3).reshape(B, G, n_slc, SLC_BLOCK, dh)
    pad = ((0, 0), (0, 0), (WINDOW, 0), (0, 0))
    k_win = jnp.pad(kw.reshape(kv_shape).transpose(0, 2, 1, 3), pad)
    v_win = jnp.pad(vw.reshape(kv_shape).transpose(0, 2, 1, 3), pad)

    qi = jnp.arange(Q_BLOCK)
    kj = jnp.arange(WINDOW + Q_BLOCK)
    dist_w = qi[:, None] + WINDOW - kj[None, :]
    band = (dist_w >= 0) & (dist_w < WINDOW)
    bias_w = _head_bias(dist_w, rel_bias)
    cmp_end = jnp.arange(n_cmp) * CMP_STRIDE + (CMP_BLOCK - 1)
    slc_ids = jnp.arange(n_slc)
    bidx = jnp.arange(B)[:, None, None, None]
    gidx = jnp.arange(G)[None, :, None, None]
    table_g = rel_bias.reshape(REL_BUCKETS, G, HPG).transpose(1, 0, 2)

    def block(i):
        s0 = i * Q_BLOCK
        t = s0 + qi
        qb = lax.dynamic_slice_in_dim(q, s0, Q_BLOCK, axis=3)
        gb = lax.dynamic_slice_in_dim(gates, s0, Q_BLOCK, axis=3)

        dist_c = t[:, None] - cmp_end[None, :]
        s_c = jnp.einsum('bghqd,bgnd->bghqn', qb, k_cmp) + _head_bias(dist_c, rel_bias)
        p_c = _masked_softmax(s_c, dist_c >= 0)
        o_c = jnp.einsum('bghqn,bgnd->bghqd', p_c.astype(v_cmp.dtype), v_cmp)

        imp = _slc_importance(p_c.sum(axis=2), n_slc)
        cur = (t // SLC_BLOCK)[:, None]
        forced = (slc_ids == 0) | (slc_ids == cur) | (slc_ids == cur - 1)
        visible = (slc_ids * SLC_BLOCK)[None, :] <= t[:, None]
        imp = jnp.where(forced, BIG, jnp.where(visible, imp, NEG_INF))
        _, sel = lax.top_k(imp, n_sel)
        k_sel = k_slc[bidx, gidx, sel].reshape(B, G, Q_BLOCK, n_sel * SLC_BLOCK, dh)
        v_sel = v_slc[bidx, gidx, sel].reshape(B, G, Q_BLOCK, n_sel * SLC_BLOCK, dh)
        kpos = (sel[..., None] * SLC_BLOCK + jnp.arange(SLC_BLOCK)).reshape(B, G, Q_BLOCK, -1)
        dist_s = t[:, None] - kpos
        bias_s = jnp.moveaxis(table_g[gidx, _t5_bucket(dist_s)], -1, 2).astype(jnp.float32)
        s_s = jnp.einsum('bghqd,bgqkd->bghqk', qb, k_sel) + bias_s
        p_s = _masked_softmax(s_s, (dist_s >= 0)[:, :, None])
        o_s = jnp.einsum('bghqk,bgqkd->bghqd', p_s.astype(v_sel.dtype), v_sel)

        k_w = lax.dynamic_slice_in_dim(k_win, s0, WINDOW + Q_BLOCK, axis=2)
        v_w = lax.dynamic_slice_in_dim(v_win, s0, WINDOW + Q_BLOCK, axis=2)
        valid_w = band & ((s0 - WINDOW + kj) >= 0)[None, :]
        s_w = jnp.einsum('bghqd,bgkd->bghqk', qb, k_w) + bias_w
        p_w = _masked_softmax(s_w, valid_w)
        o_w = jnp.einsum('bghqk,bgkd->bghqd', p_w.astype(v_w.dtype), v_w)

        o = gb[..., 0:1] * o_c + gb[..., 1:2] * o_s + gb[..., 2:3] * o_w
        return o.astype(nq.dtype)

    o = lax.map(block, jnp.arange(n_qblk))
    return o.transpose(1, 0, 4, 2, 3, 5).reshape(B, T, NSA_HEADS * dh)

def cross_attn(hn, memn, wq, wk, wv, wo):
    B, T, _ = hn.shape
    M = memn.shape[1]
    q = (hn @ wq).reshape(B, T, XA_HEADS, XA_DH) * (XA_DH ** -0.5)
    k = (memn @ wk).reshape(B, M, XA_HEADS, XA_DH)
    v = (memn @ wv).reshape(B, M, XA_HEADS, XA_DH)
    s = jnp.einsum('bqhd,bmhd->bhqm', q, k).astype(jnp.float32)
    p = jax.nn.softmax(s, axis=-1).astype(v.dtype)
    o = jnp.einsum('bhqm,bmhd->bqhd', p, v).reshape(B, T, XA_HEADS * XA_DH)
    return o @ wo

def peer_ffn(hn, wq, subkeys, down, up):
    B, T, D = hn.shape
    N = B * T
    H, K = PEER_HEADS, PEER_TOPK
    xt = hn.reshape(N, D)
    q = (xt @ wq).reshape(N, H, 2, PEER_DKEY // 2)
    s = jnp.einsum('nhpd,hpkd->nhpk', q, subkeys).astype(jnp.float32)
    s_half, i_half = lax.top_k(s, K)
    cand_s = (s_half[:, :, 0, :, None] + s_half[:, :, 1, None, :]).reshape(N, H, K * K)
    cand_i = (i_half[:, :, 0, :, None] * PEER_NKEYS + i_half[:, :, 1, None, :]).reshape(N, H, K * K)
    top_s, pos = lax.top_k(cand_s, K)
    eidx = jnp.take_along_axis(cand_i, pos, axis=-1)
    gate = jax.nn.softmax(top_s, axis=-1)
    n_chunks = N // PEER_TOKEN_CHUNK

    def chunk(args):
        xc, ec, gc = args
        u = down[ec]
        act = jax.nn.gelu(jnp.einsum('cd,chkd->chk', xc, u).astype(jnp.float32)) * gc
        return jnp.einsum('chk,chkd->cd', act.astype(up.dtype), up[ec])

    y = lax.map(chunk, (xt.reshape(n_chunks, PEER_TOKEN_CHUNK, D),
                        eidx.reshape(n_chunks, PEER_TOKEN_CHUNK, H, K),
                        gate.reshape(n_chunks, PEER_TOKEN_CHUNK, H, K)))
    return y.reshape(B, T, D).astype(hn.dtype)

def second_inputs(seed: int = 0) -> dict:
    key = jax.random.key(seed)
    ks = jax.random.split(key, 32)
    f32 = jnp.float32
    L, D = DEPTH, D_MODEL

    def nrm(k, shape, scale):
        return jax.random.normal(k, shape, f32) * scale

    def gain(k, shape):
        return 1.0 + 0.02 * jax.random.normal(k, shape, f32)

    return {
        'x': nrm(ks[0], (BATCH, SEQ, D), 1.0),
        'mem': nrm(ks[1], (BATCH, MEM_LEN, D), 1.0),
        'rel_bias': nrm(ks[2], (REL_BUCKETS, NSA_HEADS), 0.5),
        'norm_mix': gain(ks[3], (L, D)),
        'w_in': nrm(ks[4], (L, D, IN_COLS), D ** -0.5),
        'gla_gate_w2': nrm(ks[5], (L, GLA_RANK, GLA_HEADS * GLA_DK), GLA_RANK ** -0.5),
        'gla_gate_b': nrm(ks[6], (L, GLA_HEADS * GLA_DK), 0.1),
        'gla_out_norm': gain(ks[7], (L, GLA_DV)),
        'cmp_pos_k': nrm(ks[8], (L, CMP_BLOCK, NSA_DH), 0.1),
        'cmp_pos_v': nrm(ks[9], (L, CMP_BLOCK, NSA_DH), 0.1),
        'cmp_k_w1': nrm(ks[10], (L, CMP_BLOCK * NSA_DH, CMP_HIDDEN), (CMP_BLOCK * NSA_DH) ** -0.5),
        'cmp_k_w2': nrm(ks[11], (L, CMP_HIDDEN, NSA_DH), CMP_HIDDEN ** -0.5),
        'cmp_v_w1': nrm(ks[12], (L, CMP_BLOCK * NSA_DH, CMP_HIDDEN), (CMP_BLOCK * NSA_DH) ** -0.5),
        'cmp_v_w2': nrm(ks[13], (L, CMP_HIDDEN, NSA_DH), CMP_HIDDEN ** -0.5),
        'w_out': nrm(ks[14], (L, D, D), D ** -0.5),
        'norm_xattn': gain(ks[15], (L, D)),
        'norm_mem': gain(ks[16], (L, D)),
        'xa_wq': nrm(ks[17], (L, D, D), D ** -0.5),
        'xa_wk': nrm(ks[18], (L, D, D), D ** -0.5),
        'xa_wv': nrm(ks[19], (L, D, D), D ** -0.5),
        'xa_wo': nrm(ks[20], (L, D, D), D ** -0.5),
        'norm_ffn': gain(ks[21], (L, D)),
        'peer_wq': nrm(ks[22], (L, D, PEER_HEADS * PEER_DKEY), D ** -0.5),
        'peer_subkeys': nrm(ks[23], (L, PEER_HEADS, 2, PEER_NKEYS, PEER_DKEY // 2), (PEER_DKEY // 2) ** -0.5),
        'peer_down': nrm(ks[24], (L, PEER_EXPERTS, D), D ** -0.5),
        'peer_up': nrm(ks[25], (L, PEER_EXPERTS, D), PEER_HEADS ** -0.5),
        'norm_final': gain(ks[26], (D,)),
    }

def second_block(x, mem, rel_bias, norm_mix, w_in, gla_gate_w2, gla_gate_b, gla_out_norm,
              cmp_pos_k, cmp_pos_v, cmp_k_w1, cmp_k_w2, cmp_v_w1, cmp_v_w2, w_out,
              norm_xattn, norm_mem, xa_wq, xa_wk, xa_wv, xa_wo,
              norm_ffn, peer_wq, peer_subkeys, peer_down, peer_up, norm_final):
    h = x
    for l in range(DEPTH):
        hn = rms_norm_2(h, norm_mix[l])
        (gq, gk, gv, gr, glr, nq, kc, vc, ks_, vs_, kw, vw, ng) = _split_cols(hn @ w_in[l])
        o_gla = gla_mixer(gq, gk, gv, gr, glr, gla_gate_w2[l], gla_gate_b[l], gla_out_norm[l])
        o_nsa = nsa_mixer(nq, kc, vc, ks_, vs_, kw, vw, ng, rel_bias,
                          cmp_pos_k[l], cmp_pos_v[l], cmp_k_w1[l], cmp_k_w2[l], cmp_v_w1[l], cmp_v_w2[l])
        h = h + jnp.concatenate([o_gla, o_nsa], axis=-1) @ w_out[l]
        h = h + cross_attn(rms_norm_2(h, norm_xattn[l]), rms_norm_2(mem, norm_mem[l]),
                           xa_wq[l], xa_wk[l], xa_wv[l], xa_wo[l])
        h = h + peer_ffn(rms_norm_2(h, norm_ffn[l]), peer_wq[l], peer_subkeys[l], peer_down[l], peer_up[l])
    return rms_norm_2(h, norm_final)


def setup_inputs(seed=0):
    out = dict(first_inputs(seed))
    for name, value in second_inputs(seed + 1).items():
        if name != "x":
            out[name + "_2"] = value
    return out


def reference(
    x, norm1_gain, w_in, lb_logits, hg_out_norm, sb_q_norm, sb_k_norm, w_hg_out, w_sb_out, w_o,
    norm2_gain, w_ffn_in, w_ffn_out, mem_2, rel_bias_2, norm_mix_2, w_in_2, gla_gate_w2_2,
    gla_gate_b_2, gla_out_norm_2, cmp_pos_k_2, cmp_pos_v_2, cmp_k_w1_2, cmp_k_w2_2, cmp_v_w1_2,
    cmp_v_w2_2, w_out_2, norm_xattn_2, norm_mem_2, xa_wq_2, xa_wk_2, xa_wv_2, xa_wo_2,
    norm_ffn_2, peer_wq_2, peer_subkeys_2, peer_down_2, peer_up_2, norm_final_2,
):
    x = first_block(
        x, norm1_gain, w_in, lb_logits, hg_out_norm, sb_q_norm, sb_k_norm, w_hg_out, w_sb_out,
        w_o, norm2_gain, w_ffn_in, w_ffn_out,
    )
    return second_block(
        x, mem_2, rel_bias_2, norm_mix_2, w_in_2, gla_gate_w2_2, gla_gate_b_2, gla_out_norm_2,
        cmp_pos_k_2, cmp_pos_v_2, cmp_k_w1_2, cmp_k_w2_2, cmp_v_w1_2, cmp_v_w2_2, w_out_2,
        norm_xattn_2, norm_mem_2, xa_wq_2, xa_wk_2, xa_wv_2, xa_wo_2, norm_ffn_2, peer_wq_2,
        peer_subkeys_2, peer_down_2, peer_up_2, norm_final_2,
    )


_drawn_inputs = setup_inputs


def setup_inputs(seed=0):
    import zlib

    import numpy as np

    out = dict(_drawn_inputs(seed))
    spreads = {}
    factors = {'hg_out_norm': 4.233,
     'sb_q_norm': 5.503,
     'sb_k_norm': 5.913,
     'norm_mix_2': 2.675,
     'gla_out_norm_2': 4.57,
     'cmp_pos_k_2': 7.872,
     'norm_xattn_2': 8.0,
     'norm_mem_2': 6.848,
     'norm_ffn_2': 22.84,
     'norm_final_2': 7.576}
    for name, (base, spread) in spreads.items():
        noise = np.random.default_rng([zlib.crc32(name.encode()), seed]).standard_normal(out[name].shape)
        drawn = base * np.exp(spread * noise) if base else spread * noise
        out[name] = jnp.asarray(drawn.astype(out[name].dtype))
    for name, factor in factors.items():
        out[name] = (out[name] * factor).astype(out[name].dtype)
    return out
```

```python
from contextlib import ExitStack

import concourse.bass as bass
import numpy as np
from concourse import mybir

F32 = mybir.dt.float32
U32 = mybir.dt.uint32
ALU = mybir.AluOpType
ACT = mybir.ActivationFunctionType
AX = mybir.AxisListType

P = 128
T = 256
NT = T // P
D = 1024
KD = D // P
EPS = 1e-6
RING = 4
SLAB = 2048
FF = 2816
FT = FF // P
MASKED = -1e30
EXPO_CAP = 80.0

HH, HD, HCHUNK = 8, 128, 64
SH, SD = 16, 64
GH, GD, GV, GRANK, GTAU = 4, 64, 128, 16, 16.0
NH, NG, ND = 8, 2, 64
CB, CS = 32, 16
NCMP = (T - CB) // CS + 1
BUCKETS, MAX_DIST = 32, 2048
XH, XD = 4, 256
PH, PK, PTOP = 8, 128, 16

N_WIN_TURNED, N_WIN_NATURAL = 20, 16
N_FFN_IN, N_FFN_OUT = FT, FT // 2
STREAM = [("win_turned", 20), ("win_natural", 16), ("hg_out", 4), ("sb_out", 4), ("w_o", 4),
          ("ffn_in", FT), ("ffn_out", FT // 2),
          ("win2_turned", 8), ("win2_natural", 3), ("win2_small", 1), ("w_out", 4),
          ("xa_wk", 4), ("xa_wv", 4), ("xa_wq", 4), ("xa_wo", 4), ("peer_wq", 4),
          ("peer", PK)]
FIRST_SLAB = {}
_at = 0
for _name, _n in STREAM:
    FIRST_SLAB[_name] = _at
    _at += _n
N_SLABS = _at


def build(nc, ins, out, stop=None):
    top = ExitStack()
    with top:
        def sb(name, shape, dt=F32, ctx=top):
            return ctx.enter_context(nc.sbuf_tensor(name, shape, dt))

        def sem(name):
            return top.enter_context(nc.semaphore(name))

        psum = top.enter_context(nc.psum_tensor("psum", [P, 8, 512], F32))

        ring = sb("ring", [P, RING, SLAB])
        x = sb("x", [P, NT, D])
        hT = sb("hT", [P, KD, T])
        ident = sb("ident", [P, P])
        causal = sb("causal", [P, P])
        mean_sq = sb("mean_sq", [P, 4])
        rstd = sb("rstd", [P, 4])
        gains = sb("gains", [P, 9, KD])
        scr = sb("scr", [P, NT, D])
        minus_half = sb("minus_half", [P, 32])

        slab_landed = [sem(f"slab_landed{i}") for i in range(RING)]
        slab_used = sem("slab_used")
        bank_read = sem("bank_read")
        w_stream = ins["w_stream"]
        state = {"fed": 0, "banks": 0}

        def feed(sp, end):
            upto = N_SLABS if end >= N_SLABS - RING else (end + RING) // RING * RING
            g0, g1 = state["fed"] // RING, -(-upto // RING)
            state["fed"] = min(g1 * RING, N_SLABS)
            if g1 <= g0:
                return

            def one(s, j, wait):
                if wait is not None:
                    sp.wait_ge(slab_used, wait)
                sp.dma_start(ring[:, j, :], w_stream[s, :, :]).then_inc(slab_landed[j], 16)

            if g0 == 0:
                for j in range(RING):
                    one(j, j, None)
                g0 = 1
            whole = N_SLABS // RING
            if min(g1, whole) - g0 > 0:
                with sp.Fori(g0, min(g1, whole)) as g:
                    for j in range(RING):
                        sp.wait_ge(slab_used, g * RING + (j - RING + 1))
                        sp.dma_start(ring[:, j, :], w_stream[bass.ds(g * RING + j, 1), :, :]
                                     .rearrange("a p n -> p (a n)")).then_inc(slab_landed[j], 16)
            for s in range(whole * RING, state["fed"] if g1 > whole else 0):
                one(s, s % RING, s - RING + 1)

        def turned_slab(pe, slot, bank, src):
            w = ring[:, slot, :].rearrange("p (k c) -> p k c", k=KD)
            for c in range(2):
                for k in range(KD):
                    mm = pe.matmul(psum[:, bank, c * T:(c + 1) * T], w[:, k, c * P:(c + 1) * P],
                                   src[:, k, :], start=(k == 0), stop=(k == KD - 1))
            return mm

        def natural_slab(pe, slot, bank, src):
            w = ring[:, slot, :].rearrange("p (k c) -> p k c", k=KD)
            for n in range(NT):
                for k in range(KD):
                    mm = pe.matmul(psum[:, bank, n * 256:(n + 1) * 256], src[:, k, n * P:(n + 1) * P],
                                   w[:, k, :], start=(k == 0), stop=(k == KD - 1))
            return mm

        def slabs(pe, name, n, one_slab, src, i0=0, banks0=None):
            s0 = FIRST_SLAB[name] + i0
            b0 = state["banks"] if banks0 is None else banks0

            def step(s, j, it, first):
                slot = (s0 + j) % RING
                landed = 16 * ((s0 + j) // RING + 1)
                pe.wait_ge(slab_landed[slot], landed if it is None else it * 16 + landed)
                if not first:
                    free = b0 + j - RING + 1
                    pe.wait_ge(bank_read, free if it is None else it * RING + free)
                one_slab(pe, slot, slot, src).then_inc(slab_used, 1)

            for j in range(min(n, RING)):
                step(s0 + j, j, None, True)
            groups = n // RING
            if groups > 1:
                with pe.Fori(1, groups) as it:
                    for j in range(RING):
                        step(None, j, it, False)
            for j in range(max(groups, 1) * RING, n):
                step(s0 + j, j, None, False)

        def banks_out(eng, name, n, read, i0=0):
            s0 = FIRST_SLAB[name] + i0

            def step(i, j, it):
                used = s0 + j + 1
                eng.wait_ge(slab_used, used if it is None else it * RING + used)
                read(j if it is None else it * RING + j, (s0 + j) % RING).then_inc(bank_read, 1)

            groups = n // RING
            if groups > 1:
                with eng.Fori(0, groups) as it:
                    for j in range(RING):
                        step(None, j, it)
            else:
                groups = 0
            for j in range(groups * RING, n):
                step(None, j, None)

        def end_slabs(n):
            state["banks"] += n

        class Chain:

            def __init__(self, name):
                self.sem, self.n = sem(name), 0

            def step(self, eng, ins_):
                self.n += 1
                ins_.then_inc(self.sem, 1)
                eng.wait_ge(self.sem, self.n)

        dve_chain, act_chain, pool_chain = Chain("dve_step"), Chain("act_step"), Chain("pool_step")

        dma_in = sem("dma_in")
        small = {"n": 0}

        with nc.Block(no_gpsimd_drain=True) as block:
            @block.sync
            def _(sp):
                sp.dma_start(x[:, :, :], ins["x"].rearrange("b (t p) d -> p (b t) d", p=P)).then_inc(dma_in, 16)
                sp.dma_start(gains[:, :, :], ins["gains"]).then_inc(dma_in, 16)
                feed(sp, 0)
                sp.wait_ge(dma_in, 32)
            small["n"] = 32

            @block.gpsimd
            def _(pool):
                pool_chain.step(pool, pool.memset(ident[:, :], 0.0))
                pool.affine_select(out=ident[:, :], in_=ident[:, :], compare_op=ALU.not_equal, fill=1.0,
                                   base=0, pattern=[[-1, P]], channel_multiplier=1)
                pool_chain.step(pool, pool.memset(causal[:, :], 1.0))
                pool_chain.step(pool, pool.affine_select(
                    out=causal[:, :], in_=causal[:, :], compare_op=ALU.is_ge, fill=0.0,
                    base=0, pattern=[[1, P]], channel_multiplier=-1))

            @block.vector
            def _(dve):
                dve.memset(minus_half[:, :], -0.5)
        if stop == "const":
            return

        norm_ready, norm_scaled, norm_turned = sem("norm_ready"), sem("norm_scaled"), sem("norm_turned")
        norms = {"n": 0}
        rstd_ready = sem("rstd_ready")
        rstds = {"n": 0}

        def inv_sqrt(pool, dst, src):
            pool_chain.step(pool, pool.tensor_scalar(dst, src, EPS, None, ALU.add))
            rstds["n"] += 1
            pool.tensor_tensor(dst, dst, minus_half[:, 0:dst.shape[1]], ALU.pow).then_inc(rstd_ready, 1)

        def norm_turn(src, dst, gain_at, last_slab):
            n = norms["n"]
            norms["n"] += 1
            with nc.Block(no_gpsimd_drain=True) as block:
                @block.sync
                def _(sp):
                    feed(sp, last_slab)

                @block.scalar
                def _(act):
                    for t in range(NT):
                        act.activation(scr[:, t, :], src[:, t, :], ACT.Square, scale=D ** -0.5,
                                       accum_out=mean_sq[:, t:t + 1]).then_inc(norm_ready, 1)

                @block.gpsimd
                def _(pool):
                    pool.wait_ge(norm_ready, NT * (n + 1))
                    inv_sqrt(pool, rstd[:, 0:NT], mean_sq[:, 0:NT])

                @block.vector
                def _(dve):
                    dve.wait_ge(rstd_ready, rstds["n"])
                    for t in range(NT):
                        dve.tensor_scalar(scr[:, t, :], src[:, t, :], rstd[:, t:t + 1], None,
                                          ALU.mult).then_inc(norm_scaled, 1)
                    for b in range(4):
                        dve.wait_ge(norm_turned, 4 * n + b + 1)
                        dve.tensor_tensor(
                            dst[:, 2 * b:2 * b + 2, :],
                            psum[:, b, :].rearrange("p (k t) -> p k t", k=2),
                            gains[:, gain_at, 2 * b:2 * b + 2].unsqueeze(2).to_broadcast([P, 2, T]),
                            ALU.mult)

                @block.tensor
                def _(pe):
                    pe.wait_ge(norm_scaled, NT * (n + 1))
                    for b in range(4):
                        for k in (2 * b, 2 * b + 1):
                            for t in range(NT):
                                mm = pe.transpose(psum[:, b, (k % 2) * T + t * P:(k % 2) * T + (t + 1) * P],
                                                  scr[:, t, k * P:(k + 1) * P], ident[:, :])
                        mm.then_inc(norm_turned, 1)

        norm_turn(x, hT, 0, 0)
        if stop == "norm1":
            return

        first = ExitStack()
        n_win = N_WIN_TURNED + N_WIN_NATURAL
        proj = sb("proj", [P, n_win, 512], ctx=first)
        SIG_HG, SIG_GA, SIG_GB = 8, 12, 16

        with nc.Block(no_gpsimd_drain=True) as block:
            @block.sync
            def _(sp):
                feed(sp, FIRST_SLAB["hg_out"])

            @block.tensor
            def _(pe):
                slabs(pe, "win_turned", N_WIN_TURNED, turned_slab, hT)
                s0 = FIRST_SLAB["win_natural"]
                with pe.Fori(0, N_WIN_NATURAL // RING) as it:
                    for j in range(RING):
                        slot = (s0 + j) % RING
                        pe.wait_ge(slab_landed[slot], it * 16 + 16 * ((s0 + j) // RING + 1))
                        pe.wait_ge(bank_read, it * RING + s0 + j - RING + 1)
                        natural_slab(pe, slot, slot, hT).then_inc(slab_used, 1)

            @block.scalar
            def _(act):
                banks_out(act, "win_turned", n_win, lambda i, bank: act.activation(
                    proj[:, bass.ds(i, 1), :].rearrange("p a n -> p (a n)"), psum[:, bank, :], ACT.Copy))
        end_slabs(n_win)
        NCH = HH * T // HCHUNK
        ohT = sb("ohT", [P, HH, T], ctx=first)
        hg = ExitStack()
        lbl = sb("lbl", [P, 2, KD], ctx=hg)
        lbw = sb("lbw", [P, 4, KD], ctx=hg)
        oml = sb("oml", [P, KD], ctx=hg)
        LG = sb("LG", [P, HH * T], ctx=hg)
        CUM = sb("CUM", [P, HH * T], ctx=hg)
        E1 = sb("E1", [P, HH * T], ctx=hg)
        dec = sb("dec", [P, 3, NCH], ctx=hg)
        hmask = sb("hmask", [P, P], ctx=hg)
        scT = sb("scT", [P, NT * HH, P], ctx=hg)
        qe = proj[:, 0:4, :].rearrange("p a n -> p (a n)")
        fk = proj[:, 4:8, :].rearrange("p a n -> p (a n)")
        chunks = lambda v: v.rearrange("p (c s) -> p c s", s=HCHUNK)
        win_mask = sb("reset", [P, HH * T], ctx=hg)
        lb_ready, sig_ready, f_ready, log_ready, mid_ready, d_ready, e_ready = (
            sem(n) for n in ("lb_ready", "sig_ready", "f_ready", "log_ready", "mid_ready", "d_ready", "e_ready"))
        reset_ready = sem("hg_reset_ready")
        with nc.Block(no_gpsimd_drain=True) as block:
            @block.sync
            def _(sp):
                sp.dma_start(lbl[:, :, :], ins["lb_logits"]).then_inc(dma_in, 16)
                sp.wait_ge(dma_in, small["n"] + 16)
            small["n"] += 16

            @block.gpsimd
            def _(pool):
                pool_chain.step(pool, pool.memset(win_mask[:, :], 1.0))
                pool.memset(chunks(win_mask[:, :])[:, :, 0:1], 0.0).then_inc(reset_ready, 1)
                pool_chain.step(pool, pool.memset(scT[:, :, :], 0.0))
                pool_chain.step(pool, pool.tensor_copy(hmask[:, :], causal[:, :]))
                pool_chain.step(pool, pool.memset(hmask[0:HCHUNK, HCHUNK:P], 0.0))

            @block.scalar
            def _(act):
                act.activation(fk, fk, ACT.Sigmoid).then_inc(sig_ready, 1)
                gates = proj[:, SIG_HG:SIG_GB + 4, :].rearrange("p a n -> p (a n)")
                act.activation(gates, gates, ACT.Sigmoid)
                act.wait_ge(lb_ready, 1)
                act.activation(lbw[:, 1:3, :], lbw[:, 1:3, :], ACT.Exp).then_inc(lb_ready, 1)
                act.wait_ge(f_ready, 1)
                act.activation(LG[:, :], fk, ACT.Ln).then_inc(log_ready, 1)
                act.wait_ge(mid_ready, 1)
                act.activation(dec[:, :, :], dec[:, :, :], ACT.Exp)
                act.wait_ge(d_ready, 1)
                act.activation(E1[:, :], LG[:, :], ACT.Exp).then_inc(e_ready, 1)
                act.activation(CUM[:, :], LG[:, :], ACT.Exp, scale=-1.0).then_inc(e_ready, 1)

            @block.vector
            def _(dve):
                dve.wait_ge(dma_in, small["n"])
                dve_chain.step(dve, dve.tensor_tensor(lbw[:, 0, :], lbl[:, 0, :], lbl[:, 1, :], ALU.max))
                dve.tensor_tensor(lbw[:, 1:3, :], lbl[:, :, :],
                                  lbw[:, 0:1, :].to_broadcast([P, 2, KD]), ALU.subtract).then_inc(lb_ready, 1)
                dve.wait_ge(lb_ready, 2)
                dve_chain.step(dve, dve.tensor_tensor(lbw[:, 0, :], lbw[:, 1, :], lbw[:, 2, :], ALU.add))
                dve_chain.step(dve, dve.reciprocal(lbw[:, 3, :], lbw[:, 0, :]))
                dve_chain.step(dve, dve.tensor_tensor(oml[:, :], lbw[:, 2, :], lbw[:, 3, :], ALU.mult))
                dve_chain.step(dve, dve.tensor_tensor(lbw[:, 3, :], lbw[:, 1, :], lbw[:, 3, :], ALU.mult))
                dve.wait_ge(sig_ready, 1)
                for h in range(HH):
                    fh = fk[:, h * T:(h + 1) * T]
                    o = dve.tensor_scalar(fh, fh, oml[:, h:h + 1], lbw[:, 3, h:h + 1], ALU.mult, ALU.add)
                o.then_inc(f_ready, 1)
                dve.wait_ge(log_ready, 1)
                dve_chain.step(dve, dve.tensor_scalar(fk, fk, -1.0, 1.0, ALU.mult, ALU.add))
                dve.wait_ge(reset_ready, 1)
                dve_chain.step(dve, dve.tensor_tensor_scan(CUM[:, :], win_mask[:, :], LG[:, :], 0.0,
                                                           ALU.mult, ALU.add))
                mid = chunks(CUM[:, :])[:, :, HCHUNK // 2 - 1:HCHUNK // 2]
                last = chunks(CUM[:, :])[:, :, HCHUNK - 1:HCHUNK]
                dve.tensor_copy(dec[:, 0, :].unsqueeze(2), mid)
                dve.tensor_copy(dec[:, 1, :].unsqueeze(2), last)
                dve.tensor_tensor(dec[:, 2, :].unsqueeze(2), last, mid, ALU.subtract).then_inc(mid_ready, 1)
                dve_chain.step(dve, dve.tensor_tensor(chunks(LG[:, :]), chunks(CUM[:, :]),
                                                      mid.to_broadcast([P, NCH, HCHUNK]), ALU.subtract))
                dve.tensor_scalar(LG[:, :], LG[:, :], EXPO_CAP, -EXPO_CAP, ALU.min, ALU.max).then_inc(d_ready, 1)
                dve.wait_ge(e_ready, 1)
                dve.tensor_tensor(qe, qe, E1[:, :], ALU.mult)
                dve.wait_ge(e_ready, 2)
                dve.tensor_tensor(fk, fk, CUM[:, :], ALU.mult)

        keN = E1[:, :].rearrange("p (i d) -> p i d", d=HD)
        hS = CUM[:, 0:HH * P].rearrange("p (h v) -> p h v", h=HH)
        hSp = sb("hSp", [P, 3, HH, P], ctx=hg)
        hO = LG[:, :].rearrange("p (i v) -> p i v", v=P)
        hSq = E1[:, :].rearrange("p (i v) -> p i v", v=P)
        hms = sb("hms", [P, NT * HH], ctx=hg)
        V = lambda t, h: proj[:, 20 + h // 2, t * 256 + (h % 2) * P:t * 256 + (h % 2) * P + P]
        by4 = lambda b, n: psum[:, b:b + n, :].rearrange("p b (j c) -> p (b j) c", c=P)
        ke_turned, sc_done, keN_ready, scT_ready, dS_done, Sp_ready, o_done, o_copied, o_scaled, o_turned = (
            sem(n) for n in ("hg_ke_turned", "hg_scores_done", "hg_keN_ready", "hg_scT_ready", "hg_dS_done",
                             "hg_state_ready", "hg_o_done", "hg_o_copied", "hg_o_scaled", "hg_o_turned"))
        sq_ready = sem("hg_squares_ready")
        with nc.Block(no_gpsimd_drain=True) as block:
            @block.tensor
            def _(pe):
                for t in range(NT):
                    for h in range(HH):
                        i = t * HH + h
                        mm = pe.transpose(by4(0, 4)[:, i, :], fk[:, h * T + t * P:h * T + (t + 1) * P], ident[:, :])
                mm.then_inc(ke_turned, 1)
                for t in range(NT):
                    for h in range(HH):
                        at = slice(h * T + t * P, h * T + (t + 1) * P)
                        mm = pe.matmul(by4(4, 4)[:, t * HH + h, :], fk[:, at], qe[:, at], start=True, stop=True)
                mm.then_inc(sc_done, 1)
                pe.wait_ge(keN_ready, 1)
                for c in range(3):
                    if c == 2:
                        pe.wait_ge(scT_ready, 1)
                    t, b = c // 2, (c % 2) * HCHUNK
                    for h in range(HH):
                        mm = pe.matmul(by4(2 * c, 2)[:, h, :], keN[b:b + HCHUNK, t * HH + h, :],
                                       V(t, h)[b:b + HCHUNK, :], start=True, stop=True)
                    mm.then_inc(dS_done, 1)
                pe.wait_ge(scT_ready, 1)
                for t in range(NT):
                    if t == 0:
                        pe.wait_ge(Sp_ready, 1)
                    else:
                        pe.wait_ge(Sp_ready, 3)
                    for h in range(HH):
                        o = by4(6 if t == 0 else 0, 2)[:, h, :]
                        pe.matmul(o, scT[:, t * HH + h, :], V(t, h), start=True, stop=True)
                        for c in ((1,) if t == 0 else (2, 3)):
                            b = (c % 2) * HCHUNK
                            mm = pe.matmul(o[b:b + HCHUNK, :],
                                           qe[:, h * T + c * HCHUNK:h * T + (c + 1) * HCHUNK],
                                           hSp[:, c - 1, h, :], start=False, stop=True, skip_group_check=True)
                    mm.then_inc(o_done, 1)
                pe.wait_ge(o_scaled, 1)
                for h in range(HH):
                    for t in range(NT):
                        mm = pe.transpose(by4(2, 4)[:, h * 2 + t, :], hO[:, t * HH + h, :], ident[:, :])
                mm.then_inc(o_turned, 1)

            @block.scalar
            def _(act):
                act.wait_ge(ke_turned, 1)
                act.activation(keN, by4(0, 4), ACT.Copy).then_inc(keN_ready, 1)
                for t in range(NT):
                    act.wait_ge(o_done, t + 1)
                    o = by4(6 if t == 0 else 0, 2)
                    act.activation(hSq[:, t * HH:(t + 1) * HH, :], o, ACT.Square,
                                   scale=HD ** -0.5).then_inc(sq_ready, 1)
                    act.activation(hO[:, t * HH:(t + 1) * HH, :], o, ACT.Copy).then_inc(o_copied, 1)

            @block.gpsimd
            def _(pool):
                pool.wait_ge(sq_ready, 3)
                inv_sqrt(pool, hms[:, :], hms[:, :])

            @block.vector
            def _(dve):
                dve.wait_ge(sc_done, 1)
                dve.copy_predicated(scT[:, :, :], hmask[:, :].bitcast(U32).unsqueeze(1).to_broadcast([P, NT * HH, P]),
                                    by4(4, 4)).then_inc(scT_ready, 1)
                wide = lambda k, c: dec[:, k, :].rearrange("p (h c) -> p h c", c=4)[:, :, c:c + 1] \
                    .to_broadcast([P, HH, P])
                tmp = hSp[:, 2, :, :]
                for c in range(3):
                    dve.wait_ge(dS_done, c + 1)
                    if c == 0:
                        dve_chain.step(dve, dve.tensor_tensor(hS, by4(0, 2), wide(2, 0), ALU.mult))
                    else:
                        dve.tensor_tensor(tmp, by4(2 * c, 2), wide(2, c), ALU.mult)
                        dve_chain.step(dve, dve.tensor_tensor(hS, hS, wide(1, c), ALU.mult))
                        dve_chain.step(dve, dve.tensor_tensor(hS, hS, tmp, ALU.add))
                    dve.tensor_tensor(hSp[:, c, :, :], hS, wide(0, c + 1), ALU.mult).then_inc(Sp_ready, 1)
                dve.wait_ge(sq_ready, 2)
                dve.tensor_reduce(hms[:, :], hSq, AX.X, ALU.add).then_inc(sq_ready, 1)
                dve.wait_ge(rstd_ready, rstds["n"])
                dve.wait_ge(o_copied, 2)
                dve.tensor_tensor(hO, hO, hms[:, :].unsqueeze(2).to_broadcast([P, NT * HH, P]),
                                  ALU.mult).then_inc(o_scaled, 1)
                dve.wait_ge(o_turned, 1)
                for h in range(HH):
                    dve.scalar_tensor_tensor(
                        out=ohT[:, h, :], in0=psum[:, 2 + h // 2, (h % 2) * T:(h % 2 + 1) * T],
                        scalar=gains[:, 8, h:h + 1],
                        in1=proj[:, SIG_HG + h // 2, (h % 2) * T:(h % 2 + 1) * T], op0=ALU.mult, op1=ALU.mult)
        hg.close()
        if stop == "hgrn":
            first.close()
            return

        NQK = NT * SH
        sbx = ExitStack()
        sbq = ExitStack()
        osT = sb("osT", [P, SH // 2, T], ctx=sbx)
        qT = sb("qT", [P, SH // 2, T], ctx=sbx)
        kT = sb("kT", [P, SH // 2, T], ctx=sbx)
        strict = sb("strict", [P, 3 * P], ctx=sbx)
        strict_add = sb("strict_add", [P, 3 * P], ctx=sbx)
        neg_upper = sb("neg_upper", [P, P], ctx=sbx)
        neg_ones = sb("neg_ones", [P, P], ctx=sbx)
        qkms = sb("qkms", [P, 2 * NQK], ctx=sbx)
        q_gain = sb("q_gain", [P, KD], ctx=sbx)
        half64 = sb("half64", [P, 2 * NQK], ctx=sbx)
        qk_sq = sb("qk_sq", [P, 2 * NQK, SD], ctx=sbq)
        qk = proj[:, 24:32, :].rearrange("p a n -> p (a n)").rearrange("p (i d) -> p i d", d=SD)
        qk_sq_ready, qk_ms_ready, qk_scaled, qk_turned = (
            sem(n) for n in ("qk_sq_ready", "qk_ms_ready", "qk_scaled", "qk_turned"))
        with nc.Block(no_gpsimd_drain=True) as block:
            @block.scalar
            def _(act):
                act.activation(qk_sq[:, :, :], qk, ACT.Square, scale=SD ** -0.5).then_inc(qk_sq_ready, 1)

            @block.gpsimd
            def _(pool):
                pool_chain.step(pool, pool.memset(half64[:, :], -0.5))
                pool.wait_ge(qk_ms_ready, 1)
                pool_chain.step(pool, pool.tensor_scalar(qkms[:, :], qkms[:, :], EPS, None, ALU.add))
                rstds["n"] += 1
                pool.tensor_tensor(qkms[:, :], qkms[:, :], half64[:, :], ALU.pow).then_inc(rstd_ready, 1)
                pool_chain.step(pool, pool.memset(strict[:, :], 1.0))
                pool_chain.step(pool, pool.memset(neg_upper[:, :], -1.0))
                pool_chain.step(pool, pool.memset(neg_ones[:, :], -1.0))
                for m in (strict[:, 0:P], strict[:, 2 * P:3 * P]):
                    pool_chain.step(pool, pool.affine_select(
                        out=m, in_=m, compare_op=ALU.is_gt, fill=0.0, base=0, pattern=[[1, P]],
                        channel_multiplier=-1))
                pool_chain.step(pool, pool.affine_select(
                    out=neg_upper[:, :], in_=neg_upper[:, :], compare_op=ALU.is_ge, fill=0.0, base=0,
                    pattern=[[-1, P]], channel_multiplier=1))
                pool_chain.step(pool, pool.tensor_scalar(strict_add[:, :], strict[:, :], 1.0, -MASKED,
                                                         ALU.subtract, ALU.mult))

            @block.vector
            def _(dve):
                dve_chain.step(dve, dve.tensor_scalar(q_gain[:, :], gains[:, 6, :], SD ** -0.5, None, ALU.mult))
                dve.wait_ge(qk_sq_ready, 1)
                dve.tensor_reduce(qkms[:, :], qk_sq[:, :, :], AX.X, ALU.add).then_inc(qk_ms_ready, 1)
                dve.wait_ge(rstd_ready, rstds["n"])
                for i in range(2):
                    part = slice(i * NQK, (i + 1) * NQK)
                    dve.tensor_tensor(qk[:, part, :], qk[:, part, :],
                                      qkms[:, part].unsqueeze(2).to_broadcast([P, NQK, SD]),
                                      ALU.mult).then_inc(qk_scaled, 1)
                for i, (dst, g) in enumerate(((qT, q_gain[:, :]), (kT, gains[:, 7, :]))):
                    dve.wait_ge(qk_turned, i + 1)
                    dve.tensor_tensor(dst[:, :, :], psum[:, 4 * i:4 * i + 4, :].rearrange("p b (j t) -> p (b j) t", t=T),
                                      g.unsqueeze(2).to_broadcast([P, KD, T]), ALU.mult)

            @block.tensor
            def _(pe):
                for i in range(2):
                    pe.wait_ge(qk_scaled, i + 1)
                    for ft in range(KD):
                        for t in range(NT):
                            mm = pe.transpose(
                                psum[:, 4 * i + ft // 2, (ft % 2) * T + t * P:(ft % 2) * T + (t + 1) * P],
                                proj[:, 24 + 4 * i + ft // 2, t * 256 + (ft % 2) * P:t * 256 + (ft % 2 + 1) * P],
                                ident[:, :])
                    mm.then_inc(qk_turned, 1)
        sbq.close()

        sba = ExitStack()
        C3 = 3 * P
        za = sb("za", [P, 2, 4, C3], ctx=sba)
        three = lambda v: v.rearrange("p a n -> p (a n)").rearrange("p (g h c) -> p g h c", g=2, h=4)
        sp_m = three(proj[:, 24:30, :])
        wa = three(proj[:, 0:6, :])
        z_done, l_ready, spm_ready, r_done, w_ready, a_ready, so_done, so_out = (
            sem(n) for n in ("sb_z_done", "sb_log_ready", "sb_softplus_ready", "sb_logw_done", "sb_logw_ready",
                             "sb_weights_ready", "sb_o_done", "sb_o_out"))
        NGRP = SH // 4
        with nc.Block(no_gpsimd_drain=True) as block:
            @block.tensor
            def _(pe):
                def z(g):
                    if g >= 2:
                        pe.wait_ge(so_out, g - 1)
                    for j in range(4):
                        h = 4 * g + j
                        b, r = 4 * (g % 2) + j, slice((h % 2) * SD, (h % 2 + 1) * SD)
                        pe.matmul(psum[:, b, 0:T], kT[r, h // 2, 0:P], qT[r, h // 2, :], start=True, stop=True)
                        mm = pe.matmul(psum[:, b, T:C3], kT[r, h // 2, P:T], qT[r, h // 2, P:T],
                                       start=False, stop=True, skip_group_check=True)
                    mm.then_inc(z_done, 1)

                def r(g):
                    pe.wait_ge(spm_ready, g + 1)
                    for j in range(4):
                        b, m = 4 * (g % 2) + j, sp_m[:, g % 2, j, :]
                        pe.matmul(psum[:, b, 0:C3], neg_upper[:, :], m, start=False, stop=True,
                                  skip_group_check=True)
                        mm = pe.matmul(psum[:, b, P:T], neg_ones[:, :], m[:, T:C3], start=False, stop=True,
                                       skip_group_check=True)
                    mm.then_inc(r_done, 1)

                def o(g):
                    pe.wait_ge(a_ready, g + 1)
                    for j in range(4):
                        h = 4 * g + j
                        ob = psum[(h % 2) * SD:(h % 2 + 1) * SD, 4 * (g % 2) + j // 2, 0:T]
                        v = lambda kt: proj[:, 32 + h // 4, kt * 256 + (h % 4) * SD:kt * 256 + (h % 4 + 1) * SD]
                        pe.matmul(ob, v(0), wa[:, g % 2, j, 0:T], start=True, stop=True)
                        mm = pe.matmul(ob[:, P:T], v(1), wa[:, g % 2, j, T:C3], start=False, stop=True,
                                       skip_group_check=True)
                    mm.then_inc(so_done, 1)

                z(0)
                for g in range(NGRP):
                    if g + 1 < NGRP:
                        z(g + 1)
                    r(g)
                    o(g)

            @block.scalar
            def _(act):
                def logs(g):
                    act.wait_ge(z_done, g + 1)
                    a, zz = za[:, g % 2, :, :], psum[:, 4 * (g % 2):4 * (g % 2) + 4, 0:C3]
                    if g >= 2:
                        act.wait_ge(spm_ready, g - 1)
                    act_chain.step(act, act.activation(a, zz, ACT.Abs))
                    act_chain.step(act, act.activation(a, a, ACT.Exp, scale=-1.0))
                    act.activation(a, a, ACT.Ln, bias=1.0).then_inc(l_ready, 1)

                def weights(g):
                    act.wait_ge(w_ready, g + 1)
                    a = wa[:, g % 2, :, :]
                    act.activation(a, a, ACT.Exp).then_inc(a_ready, 1)
                    act.wait_ge(so_done, g + 1)
                    act.activation(osT[:, 2 * g:2 * g + 2, :], psum[:, 4 * (g % 2):4 * (g % 2) + 2, 0:T],
                                   ACT.Copy).then_inc(so_out, 1)

                logs(0)
                for g in range(NGRP):
                    if g + 1 < NGRP:
                        logs(g + 1)
                    weights(g)

            @block.vector
            def _(dve):
                def soft(g):
                    dve.wait_ge(l_ready, g + 1)
                    m, zz = sp_m[:, g % 2, :, :], psum[:, 4 * (g % 2):4 * (g % 2) + 4, 0:C3]
                    if g >= 2:
                        dve.wait_ge(r_done, g - 1)
                    dve_chain.step(dve, dve.scalar_tensor_tensor(
                        out=m, in0=zz, scalar=0.0, in1=za[:, g % 2, :, :], op0=ALU.max, op1=ALU.add))
                    dve.tensor_tensor(m, m, strict[:, :].unsqueeze(1).to_broadcast([P, 4, C3]),
                                      ALU.mult).then_inc(spm_ready, 1)

                def masked(g):
                    dve.wait_ge(r_done, g + 1)
                    if g >= 2:
                        dve.wait_ge(so_done, g - 1)
                    dve.tensor_tensor(wa[:, g % 2, :, :], psum[:, 4 * (g % 2):4 * (g % 2) + 4, 0:C3],
                                      strict_add[:, :].unsqueeze(1).to_broadcast([P, 4, C3]),
                                      ALU.add).then_inc(w_ready, 1)

                soft(0)
                for g in range(NGRP):
                    masked(g)
                    if g + 1 < NGRP:
                        soft(g + 1)
        sba.close()
        if stop == "sb":
            sbx.close(); first.close()
            return

        mx = ExitStack()
        mix = sb("mix", [P, KD, T], ctx=mx)
        part = sb("part", [P, 512], ctx=mx)
        mix_ready = sem("mix_ready")
        s_hg, s_sb, s_wo = FIRST_SLAB["hg_out"], FIRST_SLAB["sb_out"], FIRST_SLAB["w_o"]
        flat = lambda t, i: t[:, 2 * i:2 * i + 2, :].rearrange("p a t -> p (a t)")
        nat_cols = lambda t, i: t[:, :, 256 * i:256 * (i + 1)]
        bank_nat = lambda b: psum[:, b, :].rearrange("p (n c) -> p n c", n=NT)
        b0 = state["banks"]
        with nc.Block(no_gpsimd_drain=True) as block:
            @block.sync
            def _(sp):
                feed(sp, s_wo + 4)

            @block.tensor
            def _(pe):
                slabs(pe, "hg_out", 4, turned_slab, ohT)
                for j in range(4):
                    s = s_sb + j
                    pe.wait_ge(slab_landed[s % RING], 16 * (s // RING + 1))
                    pe.wait_ge(bank_read, b0 + j + 1)
                    turned_slab(pe, s % RING, s % RING, osT).then_inc(slab_used, 1)
                pe.wait_ge(mix_ready, 1)
                slabs(pe, "w_o", 4, natural_slab, mix)

            @block.vector
            def _(dve):
                for i in range(4):
                    dve.wait_ge(slab_used, s_hg + i + 1)
                    dve.tensor_tensor(flat(mix, i), psum[:, (s_hg + i) % RING, :], proj[:, SIG_GA + i, :],
                                      ALU.mult).then_inc(bank_read, 1)
                for i in range(4):
                    dve.wait_ge(slab_used, s_sb + i + 1)
                    dve_chain.step(dve, dve.tensor_tensor(part[:, :], psum[:, (s_sb + i) % RING, :],
                                                          proj[:, SIG_GB + i, :], ALU.mult))
                    o = dve.tensor_tensor(flat(mix, i), flat(mix, i), part[:, :], ALU.add)
                    if i < 3:
                        dve_chain.step(dve, o)
                o.then_inc(mix_ready, 1)
                for i in range(4):
                    dve.wait_ge(slab_used, s_wo + i + 1)
                    dve.tensor_tensor(nat_cols(x, i), nat_cols(x, i), bank_nat((s_wo + i) % RING), ALU.add)
        end_slabs(4)
        mx.close()
        sbx.close()
        first.close()
        if stop == "mix":
            return

        norm_turn(x, hT, 1, FIRST_SLAB["ffn_in"])
        ff = ExitStack()
        act_T = sb("act_T", [P, FT, T], ctx=ff)
        gate = sb("gate", [P, RING, T], ctx=ff)
        silu_ready = sem("silu_ready")
        s_in, s_out = FIRST_SLAB["ffn_in"], FIRST_SLAB["ffn_out"]
        at = lambda it, c: c if it is None else it * RING + c
        with nc.Block(no_gpsimd_drain=True) as block:
            @block.sync
            def _(sp):
                feed(sp, s_out + N_FFN_OUT)

            @block.tensor
            def _(pe):
                slabs(pe, "ffn_in", N_FFN_IN, turned_slab, hT)
                for i in range(N_FFN_OUT):
                    s = s_out + i
                    pe.wait_ge(slab_landed[s % RING], 16 * (s // RING + 1))
                    pe.wait_ge(bank_read, state["banks"] + min(2 * i + 2, FT))
                    w = ring[:, s % RING, :].rearrange("p (k c) -> p k c", k=2)
                    for kk in range(2):
                        for n in range(NT):
                            for c in range(2):
                                mm = pe.matmul(psum[:, 4 + 2 * n + c, :], act_T[:, 2 * i + kk, n * P:(n + 1) * P],
                                               w[:, kk, c * 512:(c + 1) * 512],
                                               start=(i == 0 and kk == 0), stop=(i == N_FFN_OUT - 1 and kk == 1))
                    mm.then_inc(slab_used, 1)

            def each_tile(eng, body):
                groups = FT // RING
                with eng.Fori(0, groups) as it:
                    for j in range(RING):
                        body(j, it)
                for j in range(groups * RING, FT):
                    body(j, None)

            @block.scalar
            def _(act):
                def one(j, it):
                    act.wait_ge(slab_used, at(it, s_in + j + 1))
                    act.wait_ge(bank_read, at(it, state["banks"] - RING + 1 + j))
                    act.activation(gate[:, j % RING, :], psum[:, (s_in + j) % RING, 0:T],
                                   ACT.Silu).then_inc(silu_ready, 1)
                each_tile(act, one)

            @block.vector
            def _(dve):
                def one(j, it):
                    dve.wait_ge(silu_ready, at(it, j + 1))
                    dve.tensor_tensor(act_T[:, bass.ds(at(it, j), 1), :].rearrange("p a t -> p (a t)"),
                                      gate[:, j % RING, :], psum[:, (s_in + j) % RING, T:2 * T],
                                      ALU.mult).then_inc(bank_read, 1)
                each_tile(dve, one)
                dve.wait_ge(slab_used, s_out + N_FFN_OUT)
                for n in range(NT):
                    dve.tensor_tensor(x[:, n, :], x[:, n, :],
                                      psum[:, 4 + 2 * n:6 + 2 * n, :].rearrange("p b c -> p (b c)"), ALU.add)
        end_slabs(FT)
        ff.close()
        if stop == "ffn":
            return

        norm_turn(x, hT, 2, FIRST_SLAB["win2_turned"])
        N_WIN2 = 12
        SL_GQ, SL_GK, SL_GR, SL_NQ, SL_C, SL_SW, SL_GV, SL_V, SL_SMALL = 0, 1, 2, 4, 6, 7, 8, 10, 11
        second = ExitStack()
        catT = sb("catT", [P, KD, T], ctx=second)
        proj2 = sb("proj2", [P, N_WIN2, 512], ctx=second)
        nsx = ExitStack()
        w1 = sb("w1", [P, 2, CB // 2, P], ctx=nsx)
        w2k = sb("w2k", [P, 2, ND], ctx=nsx)
        w2v = sb("w2v", [P, ND], ctx=nsx)
        pos = sb("pos", [P, 2, CB // 2], ctx=nsx)
        relx = sb("relx", [BUCKETS + 1, NH], ctx=nsx)
        buckets = sb("buckets", [BUCKETS + 1, 2, 2 * T - 1], ctx=nsx)
        gla_w2 = sb("gla_w2", [GRANK, T], ctx=nsx)
        gla_vec = sb("gla_vec", [P, 3], ctx=nsx)
        N_SMALL2 = 8
        small2 = sem("small_weights_landed")

        def more_slabs(pe, name, n, i0, one_slab, src):
            for j in range(n):
                s = FIRST_SLAB[name] + j
                pe.wait_ge(slab_landed[s % RING], 16 * (s // RING + 1))
                if i0 + j >= RING:
                    pe.wait_ge(bank_read, state["banks"] + i0 + j - RING + 1)
                one_slab(pe, s % RING, s % RING, src).then_inc(slab_used, 1)

        def small_slab(pe, slot, bank, src):
            w = ring[:, slot, :].rearrange("p (k c) -> p k c", k=KD)
            for k in range(KD):
                pe.matmul(psum[0:GRANK, bank, 0:T], w[:, k, 0:GRANK], src[:, k, :],
                          start=(k == 0), stop=(k == KD - 1))
            for n in range(NT):
                for k in range(KD):
                    mm = pe.matmul(psum[:, bank, T + 24 * n:T + 24 * (n + 1)], src[:, k, n * P:(n + 1) * P],
                                   w[:, k, GRANK:GRANK + 24], start=(k == 0), stop=(k == KD - 1))
            return mm

        with nc.Block(no_gpsimd_drain=True) as block:
            @block.sync
            def _(sp):
                sp.dma_start(w1[:, :, :, :], ins["cmp_w1"]).then_inc(small2, 16)
                for h in range(2):
                    sp.dma_start(w2k[:, h, :], ins["cmp_k_w2"]).then_inc(small2, 16)
                sp.dma_start(w2v[:, :], ins["cmp_v_w2"]).then_inc(small2, 16)
                sp.dma_start(pos[:, :, :], ins["cmp_pos"]).then_inc(small2, 16)
                sp.dma_start(relx[0:BUCKETS, :], ins["rel_bias"]).then_inc(small2, 16)
                sp.dma_start(buckets[:, :, :], ins["buckets"]).then_inc(small2, 16)
                sp.dma_start(gla_w2[:, :], ins["gla_w2"]).then_inc(small2, 16)
                sp.dma_start(gla_vec[:, :], ins["gla_vec"]).then_inc(small2, 16)
                feed(sp, FIRST_SLAB["w_out"])
                sp.wait_ge(small2, 16 * (N_SMALL2 + 1))

            @block.gpsimd
            def _(pool):
                pool_chain.step(pool, pool.memset(relx[BUCKETS:BUCKETS + 1, :], MASKED))

            @block.tensor
            def _(pe):
                slabs(pe, "win2_turned", 8, turned_slab, hT)
                more_slabs(pe, "win2_natural", 3, 8, natural_slab, hT)
                more_slabs(pe, "win2_small", 1, 11, small_slab, hT)

            @block.scalar
            def _(act):
                banks_out(act, "win2_turned", 11, lambda i, bank: act.activation(
                    proj2[:, bass.ds(i, 1), :].rearrange("p a n -> p (a n)"), psum[:, bank, :], ACT.Copy))
                s = FIRST_SLAB["win2_small"]
                act.wait_ge(slab_used, s + 1)
                act.activation(proj2[0:GRANK, SL_SMALL, 0:T], psum[0:GRANK, s % RING, 0:T], ACT.Copy)
                act.activation(proj2[:, SL_SMALL, T:T + 48], psum[:, s % RING, T:T + 48],
                               ACT.Copy).then_inc(bank_read, 1)
        end_slabs(N_WIN2)

        gl = ExitStack()
        GP = GH // 2
        CH = GP * NT
        gu = sb("gu", [P, GP * T], ctx=gl)
        ga_ = sb("ga_", [P, GP * T], ctx=gl)
        gcum = sb("gcum", [P, GP * T], ctx=gl)
        gmask = sb("gmask", [P, GP * T], ctx=gl)
        gdec = sb("gdec", [P, 3, CH], ctx=gl)
        gfac = sb("gfac", [P, GP], ctx=gl)
        gscT = sb("gscT", [P, NT * GH, P], ctx=gl)
        gkeN = sb("gkeN", [P, GP * P], ctx=gl)
        gS = sb("gS", [P, GP, GV], ctx=gl)
        gO = sb("gO", [P, NT * GH, GV], ctx=gl)
        gSq = sb("gSq", [P, NT * GH, GV], ctx=gl)
        gms = sb("gms", [P, NT * GH], ctx=gl)
        gq = proj2[:, SL_GQ, :]
        gk = proj2[:, SL_GK, :]
        g_names = ("u_done", "u_ready", "l_ready", "mid_ready", "d_ready", "e_ready", "q_ready", "sc_done",
                   "turned", "keN_ready", "dS_done", "S_ready", "scT_ready", "o_done", "sq_ready", "ms_ready",
                   "o_scaled", "o_turned", "masks_ready")
        G = {n: sem("gla_" + n) for n in g_names}
        pairs_of = lambda v, s=P: v.rearrange("p (c s) -> p c s", s=s)
        gV = lambda t, h: proj2[:, SL_GV + h // 2, t * 256 + (h % 2) * GV:t * 256 + (h % 2 + 1) * GV]
        g_at = lambda c, h: (h % 2) * 4 + c * GP + h // 2
        rows = lambda h: slice((h % 2) * GD, (h % 2 + 1) * GD)
        with nc.Block(no_gpsimd_drain=True) as block:
            @block.tensor
            def _(pe):
                for f in range(GP):
                    mm = pe.matmul(psum[:, 0, f * T:(f + 1) * T], gla_w2[:, f * P:(f + 1) * P],
                                   proj2[0:GRANK, SL_SMALL, 0:T], start=True, stop=True)
                mm.then_inc(G["u_done"], 1)
                pe.wait_ge(G["q_ready"], 1)
                for f in range(GP):
                    mm = pe.transpose(psum[:, 3, f * P:(f + 1) * P], gk[:, f * T:f * T + P], ident[:, :])
                mm.then_inc(G["turned"], 1)
                for c in range(NT):
                    for h in range(GH):
                        at_ = slice((h // 2) * T + c * P, (h // 2) * T + (c + 1) * P)
                        mm = pe.matmul(by4(1, 2)[:, g_at(c, h), :], gk[rows(h), at_], gq[rows(h), at_],
                                       start=True, stop=True)
                mm.then_inc(G["sc_done"], 1)
                pe.wait_ge(G["keN_ready"], 1)
                for h in range(GH):
                    mm = pe.matmul(psum[rows(h), 0, (h // 2) * GV:(h // 2 + 1) * GV], gkeN[:, h * GD:(h + 1) * GD],
                                   gV(0, h), start=True, stop=True)
                mm.then_inc(G["dS_done"], 1)
                pe.wait_ge(G["scT_ready"], 1)
                pe.wait_ge(G["S_ready"], 1)
                for c in range(NT):
                    for h in range(GH):
                        o = by4(4, 2)[:, g_at(c, h), :]
                        mm = pe.matmul(o, gscT[:, g_at(c, h), :], gV(c, h), start=True, stop=(c == 0))
                        if c == 1:
                            mm = pe.matmul(o, gq[rows(h), (h // 2) * T + P:(h // 2 + 1) * T], gS[rows(h), h // 2, :],
                                           start=False, stop=True)
                mm.then_inc(G["o_done"], 1)
                pe.wait_ge(G["o_scaled"], 1)
                for h in range(GH):
                    for c in range(NT):
                        mm = pe.transpose(by4(6, 2)[:, h * 2 + c, :], gO[:, g_at(c, h), :], ident[:, :])
                mm.then_inc(G["o_turned"], 1)

            @block.gpsimd
            def _(pool):
                pool_chain.step(pool, pool.memset(gmask[:, :], 1.0))
                pool_chain.step(pool, pool.memset(pairs_of(gmask[:, :])[:, :, 0:1], 0.0))
                pool.memset(gscT[:, :, :], 0.0).then_inc(G["masks_ready"], 1)
                pool.wait_ge(G["ms_ready"], 1)
                inv_sqrt(pool, gms[:, :], gms[:, :])


            @block.scalar
            def _(act):
                act.wait_ge(G["u_ready"], 1)
                act_chain.step(act, act.activation(ga_[:, :], gu[:, :], ACT.Abs))
                act_chain.step(act, act.activation(ga_[:, :], ga_[:, :], ACT.Exp, scale=-1.0))
                act.activation(ga_[:, :], ga_[:, :], ACT.Ln, bias=1.0).then_inc(G["l_ready"], 1)
                act.wait_ge(G["mid_ready"], 1)
                act.activation(gdec[:, :, :], gdec[:, :, :], ACT.Exp, scale=1 / GTAU).then_inc(G["e_ready"], 1)
                act.wait_ge(G["d_ready"], 1)
                act.activation(ga_[:, :], gu[:, :], ACT.Exp, scale=1 / GTAU).then_inc(G["e_ready"], 1)
                act.activation(gcum[:, :], gu[:, :], ACT.Exp, scale=-1 / GTAU).then_inc(G["e_ready"], 1)
                act.wait_ge(G["turned"], 1)
                act.activation(gkeN[:, :], psum[:, 3, 0:GP * P], ACT.Copy).then_inc(G["keN_ready"], 1)
                silu = proj2[:, SL_GR:SL_GR + 2, :]
                act_chain.step(act, act.activation(silu, silu, ACT.Silu))
                act.wait_ge(G["o_done"], 1)
                act.activation(gSq[:, :, :], by4(4, 2), ACT.Square, scale=GV ** -0.5).then_inc(G["sq_ready"], 1)
                act.activation(gO[:, :, :], by4(4, 2), ACT.Copy).then_inc(G["sq_ready"], 1)

            @block.vector
            def _(dve):
                dve.wait_ge(G["u_done"], 1)
                for f in range(GP):
                    o = dve.tensor_scalar(gu[:, f * T:(f + 1) * T], psum[:, 0, f * T:(f + 1) * T],
                                          gla_vec[:, f:f + 1], None, ALU.add)
                o.then_inc(G["u_ready"], 1)
                dve.wait_ge(G["l_ready"], 1)
                dve_chain.step(dve, dve.scalar_tensor_tensor(out=gu[:, :], in0=gu[:, :], scalar=0.0, in1=ga_[:, :],
                                                             op0=ALU.min, op1=ALU.subtract))
                dve.wait_ge(G["masks_ready"], 1)
                dve_chain.step(dve, dve.tensor_tensor_scan(gcum[:, :], gmask[:, :], gu[:, :], 0.0,
                                                           ALU.mult, ALU.add))
                mid = pairs_of(gcum[:, :])[:, :, P // 2 - 1:P // 2]
                last = pairs_of(gcum[:, :])[:, :, P - 1:P]
                dve.tensor_copy(gdec[:, 0, :].unsqueeze(2), mid)
                dve.tensor_copy(gdec[:, 1, :].unsqueeze(2), last)
                dve.tensor_tensor(gdec[:, 2, :].unsqueeze(2), last, mid, ALU.subtract).then_inc(G["mid_ready"], 1)
                dve_chain.step(dve, dve.tensor_tensor(pairs_of(gu[:, :]), pairs_of(gcum[:, :]),
                                                      mid.to_broadcast([P, CH, P]), ALU.subtract))
                dve.tensor_scalar(gu[:, :], gu[:, :], EXPO_CAP * GTAU, -EXPO_CAP * GTAU, ALU.min,
                                  ALU.max).then_inc(G["d_ready"], 1)
                dve.wait_ge(G["e_ready"], 3)
                dve.scalar_tensor_tensor(out=gq, in0=gq, scalar=GD ** -0.5, in1=ga_[:, :], op0=ALU.mult,
                                         op1=ALU.mult)
                dve.tensor_tensor(gk, gk, gcum[:, :], ALU.mult).then_inc(G["q_ready"], 1)
                dve_chain.step(dve, dve.tensor_tensor(gfac[:, :].unsqueeze(2),
                                                      gdec[:, 2, :].rearrange("p (f c) -> p f c", c=NT)[:, :, 0:1],
                                                      gdec[:, 0, :].rearrange("p (f c) -> p f c", c=NT)[:, :, 1:2],
                                                      ALU.mult))
                dve.wait_ge(G["sc_done"], 1)
                dve.copy_predicated(gscT[:, :, :], causal[:, :].bitcast(U32).unsqueeze(1).to_broadcast([P, NT * GH, P]),
                                    by4(1, 2)).then_inc(G["scT_ready"], 1)
                dve.wait_ge(G["dS_done"], 1)
                dve.tensor_tensor(gS[:, :, :], psum[:, 0, 0:GP * GV].rearrange("p (f v) -> p f v", f=GP),
                                  gfac[:, :].unsqueeze(2).to_broadcast([P, GP, GV]), ALU.mult).then_inc(G["S_ready"], 1)
                dve.wait_ge(G["sq_ready"], 1)
                dve.tensor_reduce(gms[:, :], gSq[:, :, :], AX.X, ALU.add).then_inc(G["ms_ready"], 1)
                dve.wait_ge(rstd_ready, rstds["n"])
                dve.wait_ge(G["sq_ready"], 2)
                dve.tensor_tensor(gO[:, :, :], gO[:, :, :], gms[:, :].unsqueeze(2).to_broadcast([P, NT * GH, GV]),
                                  ALU.mult).then_inc(G["o_scaled"], 1)
                dve.wait_ge(G["o_turned"], 1)
                for h in range(GH):
                    dve.scalar_tensor_tensor(
                        out=catT[:, h, :], in0=psum[:, 6 + h // 2, (h % 2) * T:(h % 2 + 1) * T],
                        scalar=gla_vec[:, 2:3], in1=proj2[:, SL_GR + h // 2, (h % 2) * T:(h % 2 + 1) * T],
                        op0=ALU.mult, op1=ALU.mult)
        gl.close()
        if stop == "gla":
            nsx.close(); second.close()
            return

        nb = ExitStack()
        bias = sb("bias", [P, NH, T], ctx=nsx)
        bias_c = sb("bias_c", [P, NT, NCMP, NH], ctx=nsx)
        kdup = sb("kdup", [P, 2, NG, T], ctx=nsx)
        kcmp = sb("kcmp", [P, NG, NCMP], ctx=nsx)
        vcmp = sb("vcmp", [NCMP, NG, ND], ctx=nsx)
        ngate = sb("ngate", [P, NT, 3 * NH], ctx=nsx)
        gsel = sb("gsel", [P, NH, 6], ctx=nsx)
        seen = sb("seen", [P, 1], ctx=nsx)
        kc2 = sb("kc2", [P, 2, NG, T], ctx=nb)
        hid = sb("hid", [P, 2, NG * NCMP], ctx=nb)
        posb = sb("posb", [P, 2], ctx=nb)
        bias_up = sb("bias_up", [P, NH, T], ctx=nb)
        turn_over = sb("turn_over", [P, P], ctx=nb)
        line = sb("line", [NH, 2 * T], ctx=nb)
        bias_line = nc.dram_tensor("bias_line", [NH, 2 * T], F32, kind="Internal").ap()
        N_ = {n: sem("nsa_" + n) for n in (
            "line_done", "line_ready", "line_stored", "bias_landed", "cmp_bias_done", "cmp_bias_ready", "kc_ready",
            "hid_done", "pos_ready", "hid_ready", "cmp_done", "gate_ready", "seen_ready", "over_ready",
            "bias_done")}
        with nc.Block(no_gpsimd_drain=True) as block:
            @block.sync
            def _(sp):
                sp.wait_ge(N_["line_ready"], 1)
                sp.dma_start(bias_line[:, 0:2 * T - 1], line[:, 0:2 * T - 1]).then_inc(N_["line_stored"], 16)
                sp.wait_ge(N_["line_stored"], 16)
                toeplitz = bass.AP(bias_line.tensor, 0, [[1, P], [2 * T, NH], [1, T]])
                sp.dma_start(bias_up[:, :, :], toeplitz).then_inc(N_["bias_landed"], 16)
                sp.wait_ge(N_["bias_landed"], 16)

            @block.tensor
            def _(pe):
                pe.matmul(psum[0:NH, 0, 0:2 * T - 1], relx[:, :], buckets[:, 1, :], start=True,
                          stop=True).then_inc(N_["line_done"], 1)
                for t in range(NT):
                    for n in range(NCMP):
                        at_ = T - 1 + t * P - CS * n - (CB - 1)
                        i = (t * NCMP + n) * NH
                        mm = pe.matmul(psum[:, 1, i:i + NH], buckets[:, 0, at_:at_ + P], relx[:, :],
                                       start=True, stop=True)
                mm.then_inc(N_["cmp_bias_done"], 1)
                pe.wait_ge(N_["kc_ready"], 1)
                for kv in range(2):
                    for j in range(CB // 2):
                        src = kc2[:, kv, :, :].rearrange("p g (b s) -> p g b s", s=CS)
                        pe.matmul(psum[:, 2 + kv, 0:NG * NCMP], w1[:, kv, j, :],
                                  src[:, :, 2 * j // CS:2 * j // CS + NCMP, 2 * j % CS],
                                  start=(j == 0), stop=(j == CB // 2 - 1))
                        mm = pe.matmul(psum[:, 4 + kv, 0:1], w1[:, kv, j, :], pos[:, kv, j:j + 1],
                                       start=(j == 0), stop=(j == CB // 2 - 1))
                    mm.then_inc(N_["hid_done"], 1)
                pe.wait_ge(N_["hid_ready"], 2)
                pe.matmul(psum[:, 6, 0:NG * NCMP], w2k[:, :, :].rearrange("p a d -> p (a d)"), hid[:, 0, :],
                          start=True, stop=True).then_inc(N_["cmp_done"], 1)
                for g in range(NG):
                    mm = pe.matmul(psum[0:NCMP, 7, g * ND:(g + 1) * ND], hid[:, 1, g * NCMP:(g + 1) * NCMP],
                                   w2v[:, :], start=True, stop=True)
                mm.then_inc(N_["cmp_done"], 1)
                pe.wait_ge(N_["over_ready"], 1)
                pe.wait_ge(N_["bias_landed"], 16)
                pe.wait_ge(N_["cmp_bias_ready"], 1)
                pe.wait_ge(N_["line_ready"], 1)
                for b in range(4):
                    mm = pe.matmul(psum[:, b, :], turn_over[:, :],
                                   bias_up[:, 2 * b:2 * b + 2, :].rearrange("p h c -> p (h c)"),
                                   start=True, stop=True)
                mm.then_inc(N_["bias_done"], 1)

            @block.scalar
            def _(act):
                act.wait_ge(N_["line_done"], 1)
                act.activation(line[:, 0:2 * T - 1], psum[0:NH, 0, 0:2 * T - 1], ACT.Copy).then_inc(N_["line_ready"], 1)
                act.activation(ngate[:, :, :].rearrange("p n c -> p (n c)"), proj2[:, SL_SMALL, T:T + 3 * NT * NH],
                               ACT.Sigmoid).then_inc(N_["gate_ready"], 1)
                for kv in range(2):
                    act.wait_ge(N_["hid_done"], kv + 1)
                    act_chain.step(act, act.activation(posb[:, kv:kv + 1], psum[:, 4 + kv, 0:1], ACT.Copy))
                    act.activation(hid[:, kv, :], psum[:, 2 + kv, 0:NG * NCMP], ACT.Gelu_apprx_tanh,
                                   bias=posb[:, kv:kv + 1]).then_inc(N_["hid_ready"], 1)
                act.wait_ge(N_["cmp_done"], 2)
                act.activation(kcmp[:, :, :].rearrange("p g n -> p (g n)"), psum[:, 6, 0:NG * NCMP], ACT.Copy)
                act.activation(vcmp[:, :, :].rearrange("p g d -> p (g d)"), psum[0:NCMP, 7, 0:NG * ND], ACT.Copy)

            @block.gpsimd
            def _(pool):
                pool_chain.step(pool, pool.memset(seen[:, :], 1.0))
                pool_chain.step(pool, pool.memset(turn_over[:, :], 0.0))
                pool.affine_select(out=turn_over[:, :], in_=turn_over[:, :], compare_op=ALU.not_equal, fill=1.0,
                                   base=-(P - 1), pattern=[[1, P]], channel_multiplier=1).then_inc(N_["over_ready"], 1)
                pool.affine_select(out=seen[:, :], in_=seen[:, :], compare_op=ALU.is_ge, fill=0.0,
                                   base=-(CB - 1), pattern=[[1, 1]],
                                   channel_multiplier=1).then_inc(N_["seen_ready"], 1)

            @block.vector
            def _(dve):
                two = lambda r, sl: proj2[r, sl, :].rearrange("p (a t) -> p a t", a=2)
                for g in range(NG):
                    r = slice(g * ND, (g + 1) * ND)
                    dve.tensor_copy(kc2[0:ND, :, g, :], two(r, SL_C))
                    o = dve.tensor_copy(kc2[ND:P, :, g, 0:T - 1], two(r, SL_C)[:, :, 1:T])
                o.then_inc(N_["kc_ready"], 1)
                for g in range(NG):
                    r = slice(g * ND, (g + 1) * ND)
                    for half in range(2):
                        dve.tensor_copy(kdup[half * ND:(half + 1) * ND, :, g, :], two(r, SL_SW))
                dve.wait_ge(N_["cmp_bias_done"], 1)
                dve.tensor_copy(bias_c[:, :, :, :].rearrange("p t n h -> p (t n h)"), psum[:, 1, 0:NT * NCMP * NH])\
                   .then_inc(N_["cmp_bias_ready"], 1)
                dve.wait_ge(N_["gate_ready"], 1)
                ng3 = lambda t: ngate[:, t, :].rearrange("p (h i) -> p h i", i=3)
                dve.tensor_copy(gsel[:, :, 0:2], ng3(1)[:, :, 1:3])
                dve.tensor_copy(gsel[:, :, 2:4], ng3(0)[:, :, 1:3])
                dve.wait_ge(N_["seen_ready"], 1)
                dve.tensor_scalar(gsel[:, :, 4:5], ng3(0)[:, :, 0:1], seen[:, 0:1], None, ALU.mult)
                dve.tensor_copy(gsel[:, :, 5:6], ng3(1)[:, :, 0:1])
                dve.wait_ge(N_["bias_done"], 1)
                dve.tensor_copy(bias[:, :, :].rearrange("p (b h) c -> p b (h c)", b=4), psum[:, 0:4, :])
        nb.close()

        na = ExitStack()
        SC = 512 + 256 + NT * NCMP
        sc = sb("sc", [P, 2, SC + 2], ctx=na)
        negm = sb("negm", [P, 2, 6], ctx=na)
        den = sb("den", [P, 2, 6], ctx=na)
        coef = sb("coef", [P, 2, 6], ctx=na)
        pT = sb("pT", [P, 2, 2, 3 * P], ctx=na)
        pTc = sb("pTc", [NCMP, 2, T], ctx=na)
        A_ = {n: sem("na_" + n) for n in ("s_done", "scored", "max_ready", "exp_ready", "scaled", "t_done",
                                          "pT_ready", "o_done", "o_out")}
        SPANS = [(0, 256), (256, 512), (512, 640), (640, 768), (768, 768 + NCMP), (768 + NCMP, 768 + 2 * NCMP)]
        nqT = lambda h: proj2[(h % 2) * ND:(h % 2 + 1) * ND, SL_NQ + h // 4, ((h // 2) % 2) * T:((h // 2) % 2 + 1) * T]
        half = lambda h: slice((h % 2) * ND, (h % 2 + 1) * ND)
        with nc.Block(no_gpsimd_drain=True) as block:
            @block.tensor
            def _(pe):
                def scores(h):
                    g, bA, bB = h // (NH // NG), 2 * (h % 2), 2 * (h % 2) + 1
                    if h >= 2:
                        pe.wait_ge(A_["scored"], h - 1)
                    q = nqT(h)
                    for i in range(2):
                        pe.matmul(psum[:, bA, i * T:(i + 1) * T], q[:, P:T], kdup[half(h), i, g, :],
                                  start=True, stop=True)
                    for i in range(2):
                        pe.matmul(psum[:, bB, i * P:(i + 1) * P], q[:, 0:P], kdup[half(h), i, g, 0:P],
                                  start=True, stop=True)
                    for t in range(NT):
                        mm = pe.matmul(psum[:, bB, T + t * NCMP:T + (t + 1) * NCMP], q[:, t * P:(t + 1) * P],
                                       kcmp[half(h), g, :], start=True, stop=True)
                    mm.then_inc(A_["s_done"], 1)

                def turn(h):
                    pe.wait_ge(A_["scaled"], h + 1)
                    if h >= 1:
                        pe.wait_ge(A_["pT_ready"], h)
                    s = sc[:, h % 2, :]
                    for i in range(2):
                        b = 4 + i
                        pe.transpose(psum[:, b, 0:P], s[:, 512 + i * P:512 + (i + 1) * P], ident[:, :])
                        pe.transpose(psum[:, b, P:T], s[:, i * T:i * T + P], ident[:, :])
                        pe.transpose(psum[:, b, T:3 * P], s[:, i * T + P:(i + 1) * T], ident[:, :])
                        mm = pe.transpose(psum[0:NCMP, b, 3 * P:4 * P], s[:, 768 + i * NCMP:768 + (i + 1) * NCMP],
                                          ident[:, :])
                    mm.then_inc(A_["t_done"], 1)

                def outputs(h):
                    g = h // (NH // NG)
                    pe.wait_ge(A_["pT_ready"], h + 1)
                    if h % 2 == 0 and h >= 4:
                        pe.wait_ge(A_["o_out"], h // 2 - 1)
                    o = psum[half(h), 6 + (h // 2) % 2, 0:T]
                    for i in range(2):
                        v = lambda kt: proj2[:, SL_V, kt * 256 + i * P + g * ND:kt * 256 + i * P + (g + 1) * ND]
                        pe.matmul(o, v(0), pT[:, h % 2, i, 0:T], start=(i == 0), stop=True, skip_group_check=True)
                        pe.matmul(o[:, P:T], v(1), pT[:, h % 2, i, T:3 * P], start=False, stop=True,
                                  skip_group_check=True)
                    mm = pe.matmul(o, vcmp[:, g, :], pTc[:, h % 2, :], start=False, stop=True,
                                   skip_group_check=True)
                    mm.then_inc(A_["o_done"], 1)

                scores(0)
                for h in range(NH):
                    if h + 1 < NH:
                        scores(h + 1)
                    turn(h)
                    outputs(h)

            @block.scalar
            def _(act):
                def exps(h):
                    act.wait_ge(A_["max_ready"], h + 1)
                    for i, (a, b) in enumerate(SPANS):
                        e = act.activation(sc[:, h % 2, a:b], sc[:, h % 2, a:b], ACT.Exp,
                                           bias=negm[:, h % 2, i:i + 1], accum_out=den[:, h % 2, i:i + 1])
                    e.then_inc(A_["exp_ready"], 1)

                exps(0)
                for h in range(NH):
                    act.wait_ge(A_["t_done"], h + 1)
                    if h >= 2:
                        act.wait_ge(A_["o_done"], h - 1)
                    act.activation(pT[:, h % 2, :, :], psum[:, 4:6, 0:3 * P], ACT.Copy)
                    act.activation(pTc[:, h % 2, :].rearrange("p (t q) -> p t q", t=NT), psum[0:NCMP, 4:6, 3 * P:4 * P],
                                   ACT.Copy).then_inc(A_["pT_ready"], 1)
                    if h + 1 < NH:
                        exps(h + 1)
                    if h % 2 == 1:
                        act.wait_ge(A_["o_done"], h + 1)
                        act.activation(catT[:, 4 + h // 2, :], psum[:, 6 + (h // 2) % 2, 0:T],
                                       ACT.Copy).then_inc(A_["o_out"], 1)

            @block.vector
            def _(dve):
                SCALE = ND ** -0.5

                def score(h):
                    dve.wait_ge(A_["s_done"], h + 1)
                    if h >= 2:
                        dve.wait_ge(A_["t_done"], h - 1)
                    s, bA, bB = sc[:, h % 2, :], 2 * (h % 2), 2 * (h % 2) + 1
                    wide = lambda v, n: v.rearrange("p (a c) -> p a c", a=n)
                    dve.scalar_tensor_tensor(out=wide(s[:, 0:512], 2), in0=wide(psum[:, bA, :], 2), scalar=SCALE,
                                             in1=bias[:, h:h + 1, :].to_broadcast([P, 2, T]),
                                             op0=ALU.mult, op1=ALU.add)
                    dve.scalar_tensor_tensor(out=wide(s[:, 512:768], 2), in0=wide(psum[:, bB, 0:256], 2), scalar=SCALE,
                                             in1=bias[:, h:h + 1, P:T].to_broadcast([P, 2, P]),
                                             op0=ALU.mult, op1=ALU.add)
                    o = dve.scalar_tensor_tensor(
                        out=s[:, 768:768 + 2 * NCMP], in0=psum[:, bB, T:T + 2 * NCMP], scalar=SCALE,
                        in1=bias_c[:, :, :, h].rearrange("p t n -> p (t n)"), op0=ALU.mult, op1=ALU.add)
                    o.then_inc(A_["scored"], 1)
                    dve.wait_ge(A_["scored"], h + 1)
                    nm = negm[:, h % 2, :]
                    dve.tensor_reduce(nm[:, 0:2], wide(s[:, 0:512], 2), AX.X, ALU.max, negate=True)
                    dve.tensor_reduce(nm[:, 2:4], wide(s[:, 512:768], 2), AX.X, ALU.max, negate=True)
                    dve.tensor_reduce(nm[:, 4:6], wide(s[:, 768:768 + 2 * NCMP], 2), AX.X, ALU.max,
                                      negate=True).then_inc(A_["max_ready"], 1)

                def scale(h):
                    dve.wait_ge(A_["exp_ready"], h + 1)
                    c = coef[:, h % 2, :]
                    dve_chain.step(dve, dve.reciprocal(c, den[:, h % 2, :]))
                    dve_chain.step(dve, dve.tensor_tensor(c, c, gsel[:, h, :], ALU.mult))
                    for i, (a, b) in enumerate(SPANS):
                        o = dve.tensor_scalar(sc[:, h % 2, a:b], sc[:, h % 2, a:b], c[:, i:i + 1], None, ALU.mult)
                    o.then_inc(A_["scaled"], 1)

                score(0)
                for h in range(NH):
                    if h + 1 < NH:
                        score(h + 1)
                    scale(h)
        na.close()
        nsx.close()
        if stop == "nsa":
            second.close()
            return

        def onto_residual(name, src):
            s0 = FIRST_SLAB[name]
            with nc.Block(no_gpsimd_drain=True) as block:
                @block.sync
                def _(sp):
                    feed(sp, s0 + 4)

                @block.tensor
                def _(pe):
                    more_slabs(pe, name, 4, 0, natural_slab, src)

                @block.vector
                def _(dve):
                    for i in range(4):
                        dve.wait_ge(slab_used, s0 + i + 1)
                        dve.tensor_tensor(nat_cols(x, i), nat_cols(x, i), bank_nat((s0 + i) % RING), ALU.add)

        onto_residual("w_out", catT)
        second.close()
        if stop == "wout":
            return

        xa = ExitStack()
        memT = sb("memT", [P, KD, T], ctx=xa)
        xp = sb("xp", [P, 12, 512], ctx=xa)
        xoT = sb("xoT", [P, KD, T], ctx=xa)
        xs = sb("xs", [P, NT * XH, T], ctx=xa)
        xpT = sb("xpT", [P, XH, NT, T], ctx=xa)
        xneg = sb("xneg", [P, NT * XH], ctx=xa)
        xden = sb("xden", [P, NT * XH], ctx=xa)
        mem = xs[:, :, :].rearrange("p (n a) t -> p n (a t)", n=NT)
        X_ = {n: sem("xa_" + n) for n in ("mem_landed", "s_done", "max_ready", "exp_ready", "scaled", "t_done",
                                          "pT_ready", "o_done")}
        with nc.Block(no_gpsimd_drain=True) as block:
            @block.sync
            def _(sp):
                sp.dma_start(mem, ins["mem"].rearrange("b (t p) d -> p (b t) d", p=P)).then_inc(X_["mem_landed"], 16)
                sp.wait_ge(X_["mem_landed"], 16)
        norm_turn(mem, memT, 4, FIRST_SLAB["xa_wk"])
        norm_turn(x, hT, 3, FIRST_SLAB["xa_wk"])
        with nc.Block(no_gpsimd_drain=True) as block:
            @block.sync
            def _(sp):
                feed(sp, FIRST_SLAB["xa_wo"])

            @block.tensor
            def _(pe):
                more_slabs(pe, "xa_wk", 4, 0, turned_slab, memT)
                more_slabs(pe, "xa_wv", 4, 4, natural_slab, memT)
                more_slabs(pe, "xa_wq", 4, 8, turned_slab, hT)

            @block.scalar
            def _(act):
                banks_out(act, "xa_wk", 12, lambda i, bank: act.activation(
                    xp[:, bass.ds(i, 1), :].rearrange("p a n -> p (a n)"), psum[:, bank, :], ACT.Copy))
        end_slabs(12)
        tile_of = lambda s0, f: xp[:, s0 + f // 2, (f % 2) * T:(f % 2 + 1) * T]
        by2 = lambda b, n: psum[:, b:b + n, :].rearrange("p b (j c) -> p (b j) c", c=T)
        XT = XD // P
        with nc.Block(no_gpsimd_drain=True) as block:
            @block.tensor
            def _(pe):
                for h in range(XH):
                    for t in range(NT):
                        for j in range(XT):
                            mm = pe.matmul(by2(0, 4)[:, h * NT + t, :], tile_of(8, XT * h + j)[:, t * P:(t + 1) * P],
                                           tile_of(0, XT * h + j), start=(j == 0), stop=(j == XT - 1))
                mm.then_inc(X_["s_done"], 1)
                for h in range(XH):
                    pe.wait_ge(X_["scaled"], h + 1)
                    for m in range(NT):
                        for t in range(NT):
                            mm = pe.transpose(by2(4, 4)[:, h * NT + m, t * P:(t + 1) * P],
                                              xs[:, h * NT + t, m * P:(m + 1) * P], ident[:, :])
                    mm.then_inc(X_["t_done"], 1)
                for h in range(XH):
                    pe.wait_ge(X_["pT_ready"], h + 1)
                    for j in range(XT):
                        for m in range(NT):
                            v = xp[:, 4 + h, m * 256 + j * P:m * 256 + (j + 1) * P]
                            mm = pe.matmul(by2(0, 4)[:, XT * h + j, :], v, xpT[:, h, m, :],
                                           start=(m == 0), stop=(m == NT - 1))
                mm.then_inc(X_["o_done"], 1)

            @block.scalar
            def _(act):
                act.wait_ge(X_["max_ready"], 1)
                for i in range(NT * XH):
                    act.activation(xs[:, i, :], by2(0, 4)[:, i, :], ACT.Exp, bias=xneg[:, i:i + 1], scale=XD ** -0.5,
                                   accum_out=xden[:, i:i + 1]).then_inc(X_["exp_ready"], 1)
                for h in range(XH):
                    act.wait_ge(X_["t_done"], h + 1)
                    act.activation(xpT[:, h, :, :], by2(4, 4)[:, h * NT:(h + 1) * NT, :],
                                   ACT.Copy).then_inc(X_["pT_ready"], 1)
                act.wait_ge(X_["o_done"], 1)
                act.activation(xoT[:, :, :], by2(0, 4), ACT.Copy)

            @block.vector
            def _(dve):
                dve.wait_ge(X_["s_done"], 1)
                dve_chain.step(dve, dve.tensor_reduce(xneg[:, :], by2(0, 4), AX.X, ALU.max, negate=True))
                dve.tensor_scalar(xneg[:, :], xneg[:, :], XD ** -0.5, None, ALU.mult).then_inc(X_["max_ready"], 1)
                dve.wait_ge(X_["exp_ready"], NT * XH)
                dve_chain.step(dve, dve.reciprocal(xden[:, :], xden[:, :]))
                for h in range(XH):
                    for t in range(NT):
                        i = h * NT + t
                        o = dve.tensor_scalar(xs[:, i, :], xs[:, i, :], xden[:, i:i + 1], None, ALU.mult)
                    o.then_inc(X_["scaled"], 1)
        onto_residual("xa_wo", xoT)
        xa.close()
        if stop == "xa":
            return

        norm_turn(x, hT, 5, FIRST_SLAB["peer_wq"])
        KH = PH * PTOP
        assert KH == P and PK == P
        pr = ExitStack()
        IT, JT, GT = (sb(n, [P, T], ctx=pr) for n in ("IT", "JT", "GT"))
        iota_e = sb("iota_e", [P, P], ctx=pr)
        fin_gain = sb("fin_gain", [P, D], ctx=pr)
        pa = ExitStack()
        pqT = sb("pqT", [P, PH, T], ctx=pa)
        subk = sb("subk", [P, PH, PK], ctx=pa)
        R_ = {n: sem("peer_" + n) for n in (
            "loads", "iota_ready", "scored", "exp_in", "exp_out", "table_ready", "turned", "turned_out", "ab_ready",
            "g_done", "g_out", "hid_done", "gelu_done", "weighted")}
        with nc.Block(no_gpsimd_drain=True) as block:
            @block.sync
            def _(sp):
                sp.dma_start(subk[:, :, :], ins["subkeys"]).then_inc(R_["loads"], 16)
                sp.dma_start(fin_gain[:, :], ins["norm_final"].partition_broadcast(P)).then_inc(R_["loads"], 16)
                feed(sp, FIRST_SLAB["peer"])
                sp.wait_ge(R_["loads"], 32)

            @block.gpsimd
            def _(pool):
                pool.iota(iota_e[:, :], pattern=[[1, P]], base=0, channel_multiplier=0,
                          allow_small_or_imprecise_dtypes=True).then_inc(R_["iota_ready"], 1)

            @block.tensor
            def _(pe):
                more_slabs(pe, "peer_wq", 4, 0, turned_slab, hT)

            @block.scalar
            def _(act):
                banks_out(act, "peer_wq", 4, lambda i, bank: act.activation(
                    pqT[:, 2 * i:2 * i + 2, :].rearrange("p a t -> p (a t)"), psum[:, bank, :], ACT.Copy))
        end_slabs(4)

        NHALF = 2 * PH
        work = sb("work", [P, NHALF, PK], ctx=pa)
        vals = sb("vals", [P, NHALF, PTOP], ctx=pa)
        idx_u = sb("idx_u", [P, NHALF, PTOP], U32, ctx=pa)
        idx_f = sb("idx_f", [P, NHALF, PTOP], ctx=pa)
        cand = sb("cand", [P, PH, PTOP * PTOP], ctx=pa)
        cwork = sb("cwork", [P, PH, PTOP * PTOP], ctx=pa)
        ts_ = sb("ts_", [P, PH, PTOP], ctx=pa)
        tpos = sb("tpos", [P, PH, PTOP], U32, ctx=pa)
        ab_u = sb("ab_u", [P, 2, PH, PTOP], U32, ctx=pa)
        ab_f = sb("ab_f", [P, 2, PH, PTOP], ctx=pa)
        zsum = sb("zsum", [P, PH], ctx=pa)
        tables = sb("tables", [P, 3, NT, KH], ctx=pa)
        LOWEST = -3.0e38
        with nc.Block(no_gpsimd_drain=True) as block:
            @block.tensor
            def _(pe):
                for t in range(NT):
                    for half_ in range(2):
                        r = slice(half_ * 64, (half_ + 1) * 64)
                        for h in range(PH):
                            mm = pe.matmul(by4(4 * t, 4)[:, half_ * PH + h, :], pqT[r, h, t * P:(t + 1) * P],
                                           subk[r, h, :], start=True, stop=True)
                    mm.then_inc(R_["scored"], 1)
                pe.wait_ge(R_["table_ready"], NT)
                for c in range(3):
                    for t in range(NT):
                        mm = pe.transpose(psum[:, c, t * P:(t + 1) * P], tables[:, c, t, :], ident[:, :])
                mm.then_inc(R_["turned"], 1)

            @block.scalar
            def _(act):
                for t in range(NT):
                    act.wait_ge(R_["exp_in"], t + 1)
                    act.activation(ts_[:, :, :], ts_[:, :, :], ACT.Exp).then_inc(R_["exp_out"], 1)

            @block.vector
            def _(dve):
                dve.wait_ge(R_["iota_ready"], 1)
                for t in range(NT):
                    dve.wait_ge(R_["scored"], t + 1)
                    s = by4(4 * t, 4)

                    def each_row(n, op):
                        for i in range(n):
                            o = op(i)
                        dve_chain.step(dve, o)

                    each_row(NHALF, lambda i: dve.max(vals[:, i, 0:8], s[:, i, :]))
                    each_row(NHALF, lambda i: dve.max_index(idx_u[:, i, 0:8], vals[:, i, 0:8], s[:, i, :]))
                    each_row(NHALF, lambda i: dve.match_replace(work[:, i, :], vals[:, i, 0:8], s[:, i, :], LOWEST))
                    each_row(NHALF, lambda i: dve.max(vals[:, i, 8:16], work[:, i, :]))
                    each_row(NHALF, lambda i: dve.max_index(idx_u[:, i, 8:16], vals[:, i, 8:16], work[:, i, :]))
                    dve.tensor_copy(idx_f[:, :, :], idx_u[:, :, :])
                    dve_chain.step(dve, dve.tensor_tensor(
                        cand[:, :, :].rearrange("p h (a b) -> p h a b", a=PTOP),
                        vals[:, 0:PH, :].unsqueeze(3).to_broadcast([P, PH, PTOP, PTOP]),
                        vals[:, PH:NHALF, :].unsqueeze(2).to_broadcast([P, PH, PTOP, PTOP]), ALU.add))
                    each_row(PH, lambda h: dve.max(ts_[:, h, 0:8], cand[:, h, :]))
                    each_row(PH, lambda h: dve.max_index(tpos[:, h, 0:8], ts_[:, h, 0:8], cand[:, h, :]))
                    each_row(PH, lambda h: dve.match_replace(cwork[:, h, :], ts_[:, h, 0:8], cand[:, h, :], LOWEST))
                    each_row(PH, lambda h: dve.max(ts_[:, h, 8:16], cwork[:, h, :]))
                    each_row(PH, lambda h: dve.max_index(tpos[:, h, 8:16], ts_[:, h, 8:16], cwork[:, h, :]))
                    dve_chain.step(dve, dve.tensor_copy(zsum[:, :].unsqueeze(2), ts_[:, :, 0:1]))
                    dve.tensor_tensor(ts_[:, :, :], ts_[:, :, :],
                                      zsum[:, :].unsqueeze(2).to_broadcast([P, PH, PTOP]),
                                      ALU.subtract).then_inc(R_["exp_in"], 1)
                    dve.tensor_single_scalar(ab_u[:, 0, :, :], tpos[:, :, :], 4, ALU.logical_shift_right)
                    dve_chain.step(dve, dve.tensor_single_scalar(ab_u[:, 1, :, :], tpos[:, :, :], 15,
                                                                 ALU.bitwise_and))
                    dve_chain.step(dve, dve.tensor_copy(ab_f[:, :, :, :], ab_u[:, :, :, :]))
                    wide = lambda v: v.rearrange("p h (k a) -> p h k a", k=PTOP)
                    for c, eq in enumerate((cand, cwork)):
                        dve_chain.step(dve, dve.tensor_tensor(
                            wide(eq[:, :, :]), ab_f[:, c, :, :].unsqueeze(3).to_broadcast([P, PH, PTOP, PTOP]),
                            iota_e[:, 0:PTOP].unsqueeze(1).unsqueeze(1).to_broadcast([P, PH, PTOP, PTOP]),
                            ALU.is_equal))
                        dve_chain.step(dve, dve.tensor_tensor(
                            wide(eq[:, :, :]), wide(eq[:, :, :]),
                            idx_f[:, c * PH:(c + 1) * PH, :].unsqueeze(2).to_broadcast([P, PH, PTOP, PTOP]),
                            ALU.mult))
                        dve_chain.step(dve, dve.tensor_reduce(
                            tables[:, c, t, :], eq[:, :, :].rearrange("p h (k a) -> p (h k) a", k=PTOP),
                            AX.X, ALU.add))
                    dve.wait_ge(R_["exp_out"], t + 1)
                    dve_chain.step(dve, dve.tensor_reduce(zsum[:, :], ts_[:, :, :], AX.X, ALU.add))
                    dve_chain.step(dve, dve.reciprocal(zsum[:, :], zsum[:, :]))
                    dve_chain.step(dve, dve.tensor_tensor(
                        tables[:, 2, t, :].rearrange("p (h k) -> p h k", k=PTOP), ts_[:, :, :],
                        zsum[:, :].unsqueeze(2).to_broadcast([P, PH, PTOP]), ALU.mult))
                    dve.sem_inc(R_["table_ready"], 1)
                dve.wait_ge(R_["turned"], 1)
                for c, dst in enumerate((IT, JT, GT)):
                    dve.tensor_copy(dst[:, :], psum[:, c, 0:T])
        pa.close()

        ALLG = sb("all_gates", [P, T, PK], ctx=pr)
        gbx = ExitStack()
        hot = sb("hot", [P, 2, 4, 2, P], ctx=gbx)
        NQ = T // 4
        with nc.Block(no_gpsimd_drain=True) as block:
            def quads(eng, body):
                for q in range(2):
                    body(q, None)
                with eng.Fori(1, NQ // 2) as it:
                    for q in range(2):
                        body(q, it)

            at2 = lambda it, c, k=2: c if it is None else it * k + c

            @block.vector
            def _(dve):
                def body(q, it):
                    if it is not None:
                        dve.wait_ge(R_["g_done"], at2(it, q - 1))
                    for k in range(4):
                        n = at2(it, 4 * q + k, 8)
                        dve.tensor_scalar(hot[:, q, k, 0, :], iota_e[:, :], JT[:, bass.ds(n, 1)], None, ALU.is_equal)
                        o = dve.tensor_scalar(hot[:, q, k, 1, :], iota_e[:, :], IT[:, bass.ds(n, 1)],
                                              GT[:, bass.ds(n, 1)], ALU.is_equal, ALU.mult)
                    o.then_inc(R_["ab_ready"], 1)
                quads(dve, body)

            @block.tensor
            def _(pe):
                def body(q, it):
                    pe.wait_ge(R_["ab_ready"], at2(it, q + 1))
                    if it is not None:
                        pe.wait_ge(R_["g_out"], at2(it, q - 1))
                    for k in range(4):
                        mm = pe.matmul(psum[:, q, k * P:(k + 1) * P], hot[:, q, k, 0, :], hot[:, q, k, 1, :],
                                       start=True, stop=True)
                    mm.then_inc(R_["g_done"], 1)
                quads(pe, body)

            @block.scalar
            def _(act):
                def body(q, it):
                    act.wait_ge(R_["g_done"], at2(it, q + 1))
                    act.activation(ALLG[:, bass.ds(at2(it, 4 * q, 8), 4), :], psum[:, q, :].rearrange(
                        "p (k i) -> p k i", k=4), ACT.Copy).then_inc(R_["g_out"], 1)
                quads(act, body)
        gbx.close()

        pm = ExitStack()
        gel = sb("gel", [P, 2, T], ctx=pm)
        wgt = sb("wgt", [P, 2, T], ctx=pm)
        sE = FIRST_SLAB["peer"]
        LASTG = PK // RING - 1
        with nc.Block(no_gpsimd_drain=True) as block:
            at4 = lambda it, c: c if it is None else it * RING + c

            def groups(eng, body):
                for j in range(RING):
                    body(j, None, 0)
                with eng.Fori(1, LASTG) as it:
                    for j in range(RING):
                        body(j, it, None)
                for j in range(RING):
                    body(LASTG * RING + j, None, LASTG)

            @block.sync
            def _(sp):
                feed(sp, N_SLABS)

            @block.tensor
            def _(pe):
                def hidden(j, it):
                    slot = (sE + j) % RING
                    landed = 16 * ((sE + j) // RING + 1)
                    pe.wait_ge(slab_landed[slot], landed if it is None else it * 16 + landed)
                    if it is not None or j >= 2:
                        pe.wait_ge(R_["gelu_done"], at4(it, j - 1))
                    w = ring[:, slot, 0:D].rearrange("p (k e) -> p k e", k=KD)
                    for k in range(KD):
                        mm = pe.matmul(psum[:, j % 2, 0:T], w[:, k, :], hT[:, k, :], start=(k == 0), stop=(k == KD - 1))
                    mm.then_inc(R_["hid_done"], 1)

                def body(j, it, g):
                    if g != LASTG or j % RING != RING - 1:
                        hidden(j + 1, it)
                    slot = (sE + j) % RING
                    pe.wait_ge(R_["weighted"], at4(it, j + 1))
                    for n in range(NT):
                        for c in range(2):
                            mm = pe.matmul(psum[:, 4 + 2 * n + c, :], wgt[:, j % 2, n * P:(n + 1) * P],
                                           ring[:, slot, D + c * 512:D + (c + 1) * 512],
                                           start=(g == 0 and j == 0), stop=(g == LASTG and j % RING == RING - 1))
                    mm.then_inc(slab_used, 1)

                hidden(0, None)
                groups(pe, body)

            @block.scalar
            def _(act):
                def body(j, it, g):
                    act.wait_ge(R_["hid_done"], at4(it, j + 1))
                    if it is not None or j >= 2:
                        act.wait_ge(R_["weighted"], at4(it, j - 1))
                    act.activation(gel[:, j % 2, :], psum[:, j % 2, 0:T], ACT.Gelu_apprx_tanh)\
                       .then_inc(R_["gelu_done"], 1)
                groups(act, body)

            @block.vector
            def _(dve):
                def body(j, it, g):
                    dve.wait_ge(R_["gelu_done"], at4(it, j + 1))
                    if it is not None or j >= 2:
                        dve.wait_ge(slab_used, at4(it, sE + j - 1))
                    gates = ALLG[:, :, bass.ds(at4(it, j), 1)].rearrange("p n a -> p (n a)")
                    dve.tensor_tensor(wgt[:, j % 2, :], gel[:, j % 2, :], gates, ALU.mult)\
                       .then_inc(R_["weighted"], 1)
                groups(dve, body)
                dve.wait_ge(slab_used, N_SLABS)
                for n in range(NT):
                    dve.tensor_tensor(x[:, n, :], x[:, n, :],
                                      psum[:, 4 + 2 * n:6 + 2 * n, :].rearrange("p b c -> p (b c)"), ALU.add)
        pm.close()

        fin_sq, fin_ready, out_stored = sem("final_squares"), sem("final_ready"), sem("out_stored")
        with nc.Block(no_gpsimd_drain=True) as block:
            @block.scalar
            def _(act):
                for t in range(NT):
                    act.activation(scr[:, t, :], x[:, t, :], ACT.Square, scale=D ** -0.5,
                                   accum_out=mean_sq[:, t:t + 1]).then_inc(fin_sq, 1)

            @block.gpsimd
            def _(pool):
                pool.wait_ge(fin_sq, NT)
                inv_sqrt(pool, rstd[:, 0:NT], mean_sq[:, 0:NT])

            @block.vector
            def _(dve):
                dve.wait_ge(rstd_ready, rstds["n"])
                for t in range(NT):
                    dve.scalar_tensor_tensor(out=x[:, t, :], in0=x[:, t, :], scalar=rstd[:, t:t + 1],
                                             in1=fin_gain[:, :], op0=ALU.mult, op1=ALU.mult).then_inc(fin_ready, 1)

            @block.sync
            def _(sp):
                for t in range(NT):
                    sp.wait_ge(fin_ready, t + 1)
                    sp.dma_start(out[0, t * P:(t + 1) * P, :], x[:, t, :]).then_inc(out_stored, 16)
                sp.wait_ge(out_stored, 16 * NT)
        pr.close()



def lay_out(inputs):
    a = {k: np.asarray(v) for k, v in inputs.items()}

    def cols(w, order=None):
        w = w.reshape(KD, P, -1, 256)
        return w.transpose(2, 1, 0, 3).reshape(-1, P, SLAB)

    def vec(v):
        return v.reshape(KD, P).T

    w_in = a["w_in"][0]
    sec = lambda *n: np.concatenate([w_in[:, D * i:D * (i + 1)] for i in n], axis=1)
    parts = [cols(sec(0, 1, 3, 7, 8)), cols(sec(2, 4, 5, 6)),
             cols(a["w_hg_out"][0]), cols(a["w_sb_out"][0]), cols(a["w_o"][0])]
    fi = a["w_ffn_in"][0].reshape(KD, P, 2, FT, P)
    parts.append(fi.transpose(3, 1, 0, 2, 4).reshape(FT, P, SLAB))
    fo = a["w_ffn_out"][0].reshape(FT // 2, 2, P, D)
    parts.append(fo.transpose(0, 2, 1, 3).reshape(FT // 2, P, SLAB))
    w2 = a["w_in_2"][0]
    o = np.cumsum([0, 256, 256, 512, 512, 16, 512, 128, 128, 128, 128, 128, 128, 24])
    gq, gk, gv, gr, glr, nq, kc, vc, ks, vs, kw, vw, ng = (w2[:, o[i]:o[i + 1]] for i in range(13))
    pad = np.zeros((D, 256 - 40), np.float32)
    parts.append(cols(np.concatenate([gq, gk, gr, nq, kc, vc, ks, kw, gv, vs, vw, glr, ng, pad], axis=1)))
    for n in ("w_out_2", "xa_wk_2", "xa_wv_2", "xa_wq_2", "xa_wo_2", "peer_wq_2"):
        parts.append(cols(a[n][0]))
    down = a["peer_down_2"][0].reshape(PK, P, KD, P).transpose(0, 3, 2, 1).reshape(PK, P, D)
    up = a["peer_up_2"][0].reshape(PK, P, D)
    parts.append(np.concatenate([down, up], axis=2))
    w_stream = np.concatenate(parts, axis=0)
    assert w_stream.shape == (N_SLABS, P, SLAB)

    gains = np.stack([vec(a["norm1_gain"][0]), vec(a["norm2_gain"][0]), vec(a["norm_mix_2"][0]),
                      vec(a["norm_xattn_2"][0]), vec(a["norm_mem_2"][0]), vec(a["norm_ffn_2"][0]),
                      vec(a["sb_q_norm"][0]), vec(a["sb_k_norm"][0]), vec(a["hg_out_norm"][0])], axis=1)
    lb_logits = a["lb_logits"].reshape(2, KD, P).transpose(2, 0, 1)

    paired = lambda v: v.reshape(CB // 2, 2 * ND, -1).transpose(1, 0, 2)
    cmp_w1 = np.stack([paired(a["cmp_k_w1_2"][0]), paired(a["cmp_v_w1_2"][0])], axis=1)
    cmp_pos = np.stack([paired(a["cmp_pos_k_2"][0])[:, :, 0], paired(a["cmp_pos_v_2"][0])[:, :, 0]], axis=1)
    gla_vec = np.concatenate([a["gla_gate_b_2"][0].reshape(2, P).T, a["gla_out_norm_2"][0].reshape(P, 1)], axis=1)
    return {
        "x": a["x"], "w_stream": w_stream, "gains": gains, "lb_logits": lb_logits,
        "cmp_w1": cmp_w1, "cmp_pos": cmp_pos, "cmp_k_w2": a["cmp_k_w2_2"][0], "cmp_v_w2": a["cmp_v_w2_2"][0],
        "rel_bias": a["rel_bias_2"], "buckets": bucket_rows(), "gla_w2": a["gla_gate_w2_2"][0], "gla_vec": gla_vec,
        "mem": a["mem_2"], "norm_final": a["norm_final_2"],
        "subkeys": a["peer_subkeys_2"][0].transpose(1, 3, 0, 2).reshape(P, PH, PK),
    }


def bucket_rows():
    n = np.arange(T)
    exact = BUCKETS // 2
    log_ratio = np.log(np.maximum(n, 1).astype(np.float32) / np.float32(exact)) / np.float32(
        np.log(MAX_DIST / exact))
    large = np.minimum(exact + (log_ratio * (BUCKETS - exact)).astype(np.int32), BUCKETS - 1)
    bucket = np.where(n < exact, n, large)
    up = np.zeros((BUCKETS + 1, 2 * T - 1), np.float32)
    up[BUCKETS, :T - 1] = 1
    up[bucket, T - 1 + n] = 1
    return np.stack([up, up[:, ::-1]], axis=1)


_OUT = (1, T, D)


def kernel(**inputs):
    import concourse.bacc as _bacc
    from concourse.bass_utils import run_bass_kernel_spmd as _run

    nc = _bacc.Bacc("TRN2", target_bir_lowering=False, num_devices=1)
    arrays, args = {}, {}
    for name, v in lay_out(inputs).items():
        v = np.ascontiguousarray(v)
        arrays[f"in_{name}"] = v
        args[name] = nc.dram_tensor(f"in_{name}", v.shape, mybir.dt.from_np(v.dtype), kind="ExternalInput").ap()
    out = nc.dram_tensor("out_0", _OUT, F32, kind="ExternalOutput").ap()
    build(nc, args, out)
    r = _run(nc, [arrays], core_ids=[0])
    return r.results[0]["out_0"]
```

```python
from contextlib import ExitStack

import concourse.bass as bass
import numpy as np
from concourse import mybir

F32 = mybir.dt.float32
F32R = mybir.dt.float32r
U32 = mybir.dt.uint32
ALU = mybir.AluOpType
ACT = mybir.ActivationFunctionType
AX = mybir.AxisListType

P = 128
T = 256
NT = T // P
D = 1024
KD = D // P
EPS = 1e-6
RING = 2
BANKS = 4
GROUP = 4
SLAB = 2048
FF = 2816
FT = FF // P
MASKED = -1e30
EXPO_CAP = 80.0

HH, HD, HCHUNK = 8, 128, 64
SH, SD = 16, 64
GH, GD, GV, GRANK, GTAU = 4, 64, 128, 16, 16.0
NH, NG, ND = 8, 2, 64
CB, CS = 32, 16
NCMP = (T - CB) // CS + 1
BUCKETS, MAX_DIST = 32, 2048
XH, XD = 4, 256
PH, PK, PTOP = 8, 128, 16

N_WIN_TURNED, N_WIN_NATURAL = 20, 16
N_FFN_IN, N_FFN_OUT = FT, FT // 2
STREAM = [("win_turned", 20), ("win_natural", 16), ("hg_out", 4), ("sb_out", 4), ("w_o", 4),
          ("ffn_in", FT), ("ffn_out", FT // 2),
          ("win2_turned", 8), ("win2_natural", 3), ("win2_small", 1), ("w_out", 4),
          ("xa_wk", 4), ("xa_wv", 4), ("xa_wq", 4), ("xa_wo", 4), ("peer_wq", 4),
          ("peer_down", PK // 2), ("peer_up", PK // 2)]
FIRST_SLAB = {}
_at = 0
for _name, _n in STREAM:
    FIRST_SLAB[_name] = _at
    _at += _n
N_SLABS = _at


def build(nc, ins, out, stop=None):
    top = ExitStack()
    with top:
        def sb(name, shape, dt=F32, ctx=top):
            return ctx.enter_context(nc.sbuf_tensor(name, shape, dt))

        def sem(name):
            return top.enter_context(nc.semaphore(name))

        psum = top.enter_context(nc.psum_tensor("psum", [P, 8, 512], F32))

        ring = sb("ring", [P, RING, SLAB])
        wH = sb("wH", [P, RING, SLAB], F32R)
        wL = sb("wL", [P, RING, SLAB], F32R)
        x = sb("x", [P, NT, D])
        inH = sb("inH", [P, KD, T], F32R)
        inL = sb("inL", [P, KD, T], F32R)
        src_in = (inH, inL)
        ident = sb("ident", [P, P])
        causal = sb("causal", [P, P])
        mean_sq = sb("mean_sq", [P, 4])
        rstd = sb("rstd", [P, 4])
        gains = sb("gains", [P, 9, KD])
        minus_half = sb("minus_half", [P, 32])

        slab_landed = [sem(f"slab_landed{i}") for i in range(RING)]
        hi_ready = sem("hi_ready")
        split_ready = sem("split_ready")
        slab_used = sem("slab_used")
        bank_read = sem("bank_read")
        w_stream = ins["w_stream"]
        state = {"fed": 0, "banks": 0}

        def at(it, c, k=GROUP):
            return c if it is None else it * k + c

        def feed(sp, end):
            upto = min(N_SLABS, (end + 2 + RING) // RING * RING)
            first_, state["fed"] = state["fed"], max(upto, state["fed"])

            def one(s, it=None):
                if it is not None or s >= RING:
                    sp.wait_ge(split_ready, at(it, s - RING + 1, RING))
                src = w_stream[s, :, :] if it is None else w_stream[bass.ds(at(it, s, RING), 1), :, :] \
                    .rearrange("a p n -> p (a n)")
                sp.dma_start(ring[:, s % RING, :], src).then_inc(slab_landed[s % RING], 16)

            g0, g1 = -(-first_ // RING), upto // RING
            if first_ == 0:
                for s in range(RING):
                    one(s)
                g0 = 1
            if g1 > g0:
                with sp.Fori(g0, g1) as it:
                    for j in range(RING):
                        one(j, it)
            for s in range(max(g1 * RING, first_), upto):
                one(s)

        def split_hi(act, s, it=None):
            if it is None and s >= N_SLABS:
                return
            slot = s % RING
            act.wait_ge(slab_landed[slot], at(it, 16 * (s // RING + 1), 16 * GROUP // RING))
            if it is not None or s >= RING:
                act.wait_ge(slab_used, at(it, s - RING + 1))
            act.activation(wH[:, slot, :], ring[:, slot, :], ACT.Copy).then_inc(hi_ready, 1)

        def split_lo(dve, s, it=None):
            if it is None and s >= N_SLABS:
                return
            slot = s % RING
            dve.wait_ge(hi_ready, at(it, s + 1))
            dve.tensor_tensor(wL[:, slot, :], ring[:, slot, :], wH[:, slot, :].bitcast(F32),
                              ALU.subtract).then_inc(split_ready, 1)

        def per_slab(eng, s0, n, body, peel=0):
            rounds = n // GROUP
            if rounds - peel < 2:
                peel = rounds
            for j in range(peel * GROUP):
                body(s0 + j, None)
            if rounds > peel:
                with eng.Fori(peel, rounds) as it:
                    for j in range(GROUP):
                        body(s0 + j, it)
            for j in range(rounds * GROUP, n):
                body(s0 + j, None)

        def three(pe, out_, lhs, rhs, start, stop):
            pe.matmul(out_, lhs[0], rhs[0], start=start, stop=False)
            pe.matmul(out_, lhs[0], rhs[1], start=False, stop=False)
            return pe.matmul(out_, lhs[1], rhs[0], start=False, stop=stop)

        def weights_of(slot, k):
            return [w[:, slot, :].rearrange("p (k c) -> p k c", k=k) for w in (wH, wL)]

        def turned_slab(pe, slot, bank, src):
            w = weights_of(slot, KD)
            for c in range(2):
                for k in range(KD):
                    mm = three(pe, psum[:, bank, c * T:(c + 1) * T], [v[:, k, c * P:(c + 1) * P] for v in w],
                               [v[:, k, :] for v in src], k == 0, k == KD - 1)
            return mm

        def natural_slab(pe, slot, bank, src):
            w = weights_of(slot, KD)
            for n in range(NT):
                for k in range(KD):
                    mm = three(pe, psum[:, bank, n * 256:(n + 1) * 256], [v[:, k, n * P:(n + 1) * P] for v in src],
                               [v[:, k, :] for v in w], k == 0, k == KD - 1)
            return mm

        def project(pe, s0, n, one_slab, src, before=0):
            base = state["banks"] + before - BANKS + 1

            def body(s, it):
                pe.wait_ge(split_ready, at(it, s + 1))
                if it is not None or before + s - s0 >= BANKS:
                    pe.wait_ge(bank_read, at(it, base + s - s0))
                one_slab(pe, s % RING, s % BANKS, src).then_inc(slab_used, 1)

            per_slab(pe, s0, n, body, peel=0 if before >= BANKS else 1)

        def end_slabs(n):
            state["banks"] += n

        class Chain:

            def __init__(self, name):
                self.sem, self.n = sem(name), 0

            def step(self, eng, ins_):
                self.n += 1
                ins_.then_inc(self.sem, 1)
                eng.wait_ge(self.sem, self.n)

        dve_chain, act_chain, pool_chain = Chain("dve_step"), Chain("act_step"), Chain("pool_step")

        dma_in = sem("dma_in")

        with nc.Block(no_gpsimd_drain=True) as block:
            @block.sync
            def _(sp):
                sp.dma_start(x[:, :, :], ins["x"].rearrange("b (t p) d -> p (b t) d", p=P)).then_inc(dma_in, 16)
                sp.dma_start(gains[:, :, :], ins["gains"]).then_inc(dma_in, 16)
                feed(sp, 0)
                sp.wait_ge(dma_in, 32)

            @block.scalar
            def _(act):
                for s in range(RING):
                    split_hi(act, s)

            @block.gpsimd
            def _(pool):
                pool_chain.step(pool, pool.memset(ident[:, :], 0.0))
                pool.affine_select(out=ident[:, :], in_=ident[:, :], compare_op=ALU.not_equal, fill=1.0,
                                   base=0, pattern=[[-1, P]], channel_multiplier=1)
                pool_chain.step(pool, pool.memset(causal[:, :], 1.0))
                pool_chain.step(pool, pool.affine_select(
                    out=causal[:, :], in_=causal[:, :], compare_op=ALU.is_ge, fill=0.0,
                    base=0, pattern=[[1, P]], channel_multiplier=-1))

            @block.vector
            def _(dve):
                dve.memset(minus_half[:, :], -0.5)
                for s in range(RING):
                    split_lo(dve, s)
        if stop == "const":
            return

        norm_ready, norm_scaled, norm_turned, norm_hi = (
            sem(n) for n in ("norm_ready", "norm_scaled", "norm_turned", "norm_hi"))
        norms = {"n": 0}
        rstd_ready = sem("rstd_ready")
        rstds = {"n": 0}

        def inv_sqrt(pool, dst, src):
            pool_chain.step(pool, pool.tensor_scalar(dst, src, EPS, None, ALU.add))
            rstds["n"] += 1
            pool.tensor_tensor(dst, dst, minus_half[:, 0:dst.shape[1]], ALU.pow).then_inc(rstd_ready, 1)

        split_sem = sem("input_rounded")
        splits = {"n": 0}

        def split_input(src, dst):
            n = splits["n"]
            splits["n"] += 1
            with nc.Block(no_gpsimd_drain=True) as block:
                @block.scalar
                def _(act):
                    for k in range(0, KD, 2):
                        act.activation(dst[0][:, k:k + 2, :], src[:, k:k + 2, :], ACT.Copy).then_inc(split_sem, 1)

                @block.vector
                def _(dve):
                    for k in range(0, KD, 2):
                        dve.wait_ge(split_sem, (n * KD + k) // 2 + 1)
                        dve.tensor_tensor(dst[1][:, k:k + 2, :], src[:, k:k + 2, :],
                                          dst[0][:, k:k + 2, :].bitcast(F32), ALU.subtract)

        def norm_turn(src, dst, gain_at):
            n = norms["n"]
            norms["n"] += 1
            own = ExitStack()
            scr = sb(f"normed{n}", [P, NT, D], ctx=own)
            tile = lambda k: psum[:, k // 2, (k % 2) * T:(k % 2 + 1) * T]
            with nc.Block(no_gpsimd_drain=True) as block:
                @block.scalar
                def _(act):
                    for t in range(NT):
                        act.activation(scr[:, t, :], src[:, t, :], ACT.Square, scale=D ** -0.5,
                                       accum_out=mean_sq[:, t:t + 1]).then_inc(norm_ready, 1)
                    for k in range(KD):
                        act.wait_ge(norm_turned, 4 * n + k // 2 + 1)
                        act.activation(dst[0][:, k, :], tile(k), ACT.Copy,
                                       scale=gains[:, gain_at, k:k + 1]).then_inc(norm_hi, 1)

                @block.gpsimd
                def _(pool):
                    pool.wait_ge(norm_ready, NT * (n + 1))
                    inv_sqrt(pool, rstd[:, 0:NT], mean_sq[:, 0:NT])

                @block.vector
                def _(dve):
                    dve.wait_ge(rstd_ready, rstds["n"])
                    for t in range(NT):
                        dve.tensor_scalar(scr[:, t, :], src[:, t, :], rstd[:, t:t + 1], None,
                                          ALU.mult).then_inc(norm_scaled, 1)
                    for k in range(KD):
                        dve.wait_ge(norm_hi, KD * n + 2 * (k // 2) + 2)
                        dve.scalar_tensor_tensor(out=dst[1][:, k, :], in0=tile(k), scalar=gains[:, gain_at, k:k + 1],
                                                 in1=dst[0][:, k, :].bitcast(F32), op0=ALU.mult, op1=ALU.subtract)

                @block.tensor
                def _(pe):
                    for t in range(NT):
                        pe.wait_ge(norm_scaled, NT * n + t + 1)
                        for k in range(KD):
                            mm = pe.transpose(tile(k)[:, t * P:(t + 1) * P], scr[:, t, k * P:(k + 1) * P],
                                              ident[:, :])
                            if t == NT - 1 and k % 2 == 1:
                                mm.then_inc(norm_turned, 1)
            own.close()

        norm_turn(x, src_in, 0)
        if stop == "norm1":
            return

        first = ExitStack()
        n_win = N_WIN_TURNED + N_WIN_NATURAL
        proj = sb("proj", [P, n_win, 512], ctx=first)
        SIG_HG, SIG_GA, SIG_GB, QK_AT, V_AT, SV_AT = 8, 12, 16, 20, 28, 32
        QK_ROOT = rstds["n"] + 1

        def copy_out(dst, s0, n):
            def act_step(act):
                per_slab(act, s0, n, lambda s, it: copy_step(act, dst, s0, s, it))
            return act_step, lambda dve: per_slab(dve, s0, n, lambda s, it: split_lo(dve, s + RING, it))

        def copy_step(act, dst, s0, s, it=None):
            act.wait_ge(slab_used, at(it, s + 1))
            act.activation(dst[:, bass.ds(at(it, s - s0), 1), :].rearrange("p a n -> p (a n)"),
                           psum[:, s % BANKS, :], ACT.Copy).then_inc(bank_read, 1)
            split_hi(act, s + RING, it)

        NCH = HH * T // HCHUNK
        NQK = NT * SH
        ohT = sb("ohT", [P, HH, T], ctx=first)
        qkms = sb("qkms", [P, 2 * NQK], ctx=first)
        half64 = sb("half64", [P, 2 * NQK], ctx=first)
        strict = sb("strict", [P, 3 * P], ctx=first)
        strict_add = sb("strict_add", [P, 3 * P], ctx=first)
        neg_upper = sb("neg_upper", [P, P], ctx=first)
        neg_ones = sb("neg_ones", [P, P], ctx=first)
        hg = ExitStack()
        lbl = sb("lbl", [P, 2, KD], ctx=hg)
        lbw = sb("lbw", [P, 4, KD], ctx=hg)
        oml = sb("oml", [P, KD], ctx=hg)
        LG = sb("LG", [P, HH * T], ctx=hg)
        CUM = sb("CUM", [P, HH * T], ctx=hg)
        E1 = sb("E1", [P, HH * T], ctx=hg)
        dec = sb("dec", [P, 3, NCH], ctx=hg)
        hmask = sb("hmask", [P, P], ctx=hg)
        scT = sb("scT", [P, NT * HH, P], ctx=hg)
        qe = proj[:, 0:4, :].rearrange("p a n -> p (a n)")
        fk = proj[:, 4:8, :].rearrange("p a n -> p (a n)")
        gates = lambda j: proj[:, SIG_HG + 4 * j:SIG_HG + 4 * j + 4, :]
        qk = proj[:, QK_AT:QK_AT + 8, :].rearrange("p a n -> p (a n)").rearrange("p (i d) -> p i d", d=SD)
        qk_part = [slice(i * NQK, (i + 1) * NQK) for i in range(2)]
        qk_sq = scT[:, :, :].rearrange("p i (a d) -> p (i a) d", d=SD)
        chunks = lambda v: v.rearrange("p (c s) -> p c s", s=HCHUNK)
        mid = chunks(CUM[:, :])[:, :, HCHUNK // 2 - 1:HCHUNK // 2]
        last = chunks(CUM[:, :])[:, :, HCHUNK - 1:HCHUNK]
        resets = sb("resets", [P, HH * T], ctx=hg)
        (lb_ready, sig_ready, f_ready, log_ready, mid_ready, d_ready, e_ready, resets_ready, qk_sq_ready,
         qk_ms_ready) = (sem(n) for n in (
             "lb_ready", "sig_ready", "f_ready", "log_ready", "mid_ready", "d_ready", "e_ready", "hg_resets_ready",
             "qk_sq_ready", "qk_ms_ready"))
        with nc.Block(no_gpsimd_drain=True) as block:
            @block.sync
            def _(sp):
                sp.dma_start(lbl[:, :, :], ins["lb_logits"]).then_inc(dma_in, 16)
                feed(sp, n_win)
                sp.wait_ge(dma_in, 48)

            @block.tensor
            def _(pe):
                project(pe, 0, N_WIN_TURNED, turned_slab, src_in)
                project(pe, N_WIN_TURNED, N_WIN_NATURAL, natural_slab, src_in, before=N_WIN_TURNED)

            @block.gpsimd
            def _(pool):
                pool_chain.step(pool, pool.memset(resets[:, :], 1.0))
                pool.memset(chunks(resets[:, :])[:, :, 0:1], 0.0).then_inc(resets_ready, 1)
                pool_chain.step(pool, pool.memset(half64[:, :], -0.5))
                pool_chain.step(pool, pool.tensor_copy(hmask[:, :], causal[:, :]))
                pool_chain.step(pool, pool.memset(hmask[0:HCHUNK, HCHUNK:P], 0.0))
                pool_chain.step(pool, pool.memset(strict[:, :], 1.0))
                pool_chain.step(pool, pool.memset(neg_upper[:, :], -1.0))
                pool_chain.step(pool, pool.memset(neg_ones[:, :], -1.0))
                for m in (strict[:, 0:P], strict[:, 2 * P:3 * P]):
                    pool_chain.step(pool, pool.affine_select(
                        out=m, in_=m, compare_op=ALU.is_gt, fill=0.0, base=0, pattern=[[1, P]],
                        channel_multiplier=-1))
                pool_chain.step(pool, pool.affine_select(
                    out=neg_upper[:, :], in_=neg_upper[:, :], compare_op=ALU.is_ge, fill=0.0, base=0,
                    pattern=[[-1, P]], channel_multiplier=1))
                pool_chain.step(pool, pool.tensor_scalar(strict_add[:, :], strict[:, :], 1.0, -MASKED,
                                                         ALU.subtract, ALU.mult))
                pool.wait_ge(qk_ms_ready, 2)
                pool_chain.step(pool, pool.tensor_scalar(qkms[:, :], qkms[:, :], EPS, None, ALU.add))
                rstds["n"] += 1
                pool.tensor_tensor(qkms[:, :], qkms[:, :], half64[:, :], ALU.pow).then_inc(rstd_ready, 1)
                pool_chain.step(pool, pool.memset(scT[:, :, :], 0.0))

            @block.scalar
            def _(act):
                act_step, _ = copy_out(proj, 0, N_WIN_TURNED)
                act_step(act)
                for s in range(N_WIN_TURNED, n_win):
                    copy_step(act, proj, 0, s)
                    step = s - N_WIN_TURNED
                    if step == 0:
                        act.activation(fk, fk, ACT.Sigmoid).then_inc(sig_ready, 1)
                    elif step == 1:
                        act.wait_ge(lb_ready, 1)
                        act.activation(lbw[:, 1:3, :], lbw[:, 1:3, :], ACT.Exp).then_inc(lb_ready, 1)
                    elif step == 3:
                        act.wait_ge(f_ready, 1)
                        act.activation(LG[:, :], fk, ACT.Ln).then_inc(log_ready, 1)
                    elif step in (2, 5, 8):
                        g = gates((2, 5, 8).index(step))
                        act.activation(g, g, ACT.Sigmoid)
                    elif step == 6:
                        act.wait_ge(mid_ready, 1)
                        act.activation(dec[:, :, :], dec[:, :, :], ACT.Exp)
                    elif step in (7, 9):
                        i = (7, 9).index(step)
                        if i == 1:
                            act.wait_ge(qk_ms_ready, 1)
                        act.activation(qk_sq, qk[:, qk_part[i], :], ACT.Square, scale=SD ** -0.5)\
                           .then_inc(qk_sq_ready, 1)
                    elif step == 10:
                        act.wait_ge(d_ready, 1)
                        act.activation(E1[:, :], LG[:, :], ACT.Exp).then_inc(e_ready, 1)
                    elif step == 11:
                        act.activation(CUM[:, :], LG[:, :], ACT.Exp, scale=-1.0).then_inc(e_ready, 1)

            @block.vector
            def _(dve):
                per_slab(dve, 0, N_WIN_TURNED, lambda s, it: split_lo(dve, s + RING, it))
                for s in range(N_WIN_TURNED, n_win):
                    split_lo(dve, s + RING)
                    step = s - N_WIN_TURNED
                    if step == 0:
                        dve.wait_ge(dma_in, 48)
                        dve_chain.step(dve, dve.tensor_tensor(lbw[:, 0, :], lbl[:, 0, :], lbl[:, 1, :], ALU.max))
                        dve.tensor_tensor(lbw[:, 1:3, :], lbl[:, :, :],
                                          lbw[:, 0:1, :].to_broadcast([P, 2, KD]), ALU.subtract).then_inc(lb_ready, 1)
                    elif step == 1:
                        dve.wait_ge(lb_ready, 2)
                        dve_chain.step(dve, dve.tensor_tensor(lbw[:, 0, :], lbw[:, 1, :], lbw[:, 2, :], ALU.add))
                        dve_chain.step(dve, dve.reciprocal(lbw[:, 3, :], lbw[:, 0, :]))
                        dve_chain.step(dve, dve.tensor_tensor(oml[:, :], lbw[:, 2, :], lbw[:, 3, :], ALU.mult))
                        dve_chain.step(dve, dve.tensor_tensor(lbw[:, 3, :], lbw[:, 1, :], lbw[:, 3, :], ALU.mult))
                    elif step == 2:
                        dve.wait_ge(sig_ready, 1)
                        for h in range(HH):
                            fh = fk[:, h * T:(h + 1) * T]
                            o = dve.tensor_scalar(fh, fh, oml[:, h:h + 1], lbw[:, 3, h:h + 1], ALU.mult, ALU.add)
                        o.then_inc(f_ready, 1)
                    elif step == 4:
                        dve.wait_ge(log_ready, 1)
                        dve_chain.step(dve, dve.tensor_scalar(fk, fk, -1.0, 1.0, ALU.mult, ALU.add))
                    elif step == 5:
                        dve.wait_ge(resets_ready, 1)
                        dve_chain.step(dve, dve.tensor_tensor_scan(CUM[:, :], resets[:, :], LG[:, :], 0.0,
                                                                   ALU.mult, ALU.add))
                    elif step == 6:
                        dve.tensor_copy(dec[:, 0, :].unsqueeze(2), mid)
                        dve.tensor_copy(dec[:, 1, :].unsqueeze(2), last)
                        dve.tensor_tensor(dec[:, 2, :].unsqueeze(2), last, mid, ALU.subtract).then_inc(mid_ready, 1)
                        dve_chain.step(dve, dve.tensor_tensor(chunks(LG[:, :]), chunks(CUM[:, :]),
                                                              mid.to_broadcast([P, NCH, HCHUNK]), ALU.subtract))
                    elif step == 7:
                        dve.tensor_scalar(LG[:, :], LG[:, :], EXPO_CAP, -EXPO_CAP, ALU.min, ALU.max)\
                           .then_inc(d_ready, 1)
                    elif step in (8, 9):
                        i = step - 8
                        dve.wait_ge(qk_sq_ready, i + 1)
                        dve.tensor_reduce(qkms[:, qk_part[i]], qk_sq, AX.X, ALU.add).then_inc(qk_ms_ready, 1)
                    elif step == 10:
                        dve.wait_ge(e_ready, 1)
                        dve.tensor_tensor(qe, qe, E1[:, :], ALU.mult)
                    elif step == 11:
                        dve.wait_ge(e_ready, 2)
                        dve.tensor_tensor(fk, fk, CUM[:, :], ALU.mult)
                    elif step in (12, 13):
                        i = step - 12
                        dve.wait_ge(rstd_ready, QK_ROOT)
                        dve.tensor_tensor(qk[:, qk_part[i], :], qk[:, qk_part[i], :],
                                          qkms[:, qk_part[i]].unsqueeze(2).to_broadcast([P, NQK, SD]), ALU.mult)
        end_slabs(n_win)

        keN = E1[:, :].rearrange("p (i d) -> p i d", d=HD)
        hS = CUM[:, 0:HH * P].rearrange("p (h v) -> p h v", h=HH)
        hSp2 = sb("hSp2", [P, D], ctx=hg)
        hSp = [v.rearrange("p (h v) -> p h v", v=P) for v in
               (resets[:, 0:D], resets[:, D:2 * D], hSp2[:, :])]
        hO = LG[:, :].rearrange("p (i v) -> p i v", v=P)
        hSq = E1[:, :].rearrange("p (i v) -> p i v", v=P)
        hms = sb("hms", [P, NT * HH], ctx=hg)
        V = lambda t, h: proj[:, V_AT + h // 2, t * 256 + (h % 2) * P:t * 256 + (h % 2) * P + P]
        by4 = lambda b, n: psum[:, b:b + n, :].rearrange("p b (j c) -> p (b j) c", c=P)
        ke_turned, sc_done, keN_ready, scT_ready, dS_done, Sp_ready, o_done, o_copied, o_scaled, o_turned = (
            sem(n) for n in ("hg_ke_turned", "hg_scores_done", "hg_keN_ready", "hg_scT_ready", "hg_dS_done",
                             "hg_state_ready", "hg_o_done", "hg_o_copied", "hg_o_scaled", "hg_o_turned"))
        sq_ready = sem("hg_squares_ready")
        with nc.Block(no_gpsimd_drain=True) as block:
            @block.tensor
            def _(pe):
                for t in range(NT):
                    for h in range(HH):
                        i = t * HH + h
                        mm = pe.transpose(by4(0, 4)[:, i, :], fk[:, h * T + t * P:h * T + (t + 1) * P], ident[:, :])
                mm.then_inc(ke_turned, 1)
                for t in range(NT):
                    for h in range(HH):
                        at = slice(h * T + t * P, h * T + (t + 1) * P)
                        mm = pe.matmul(by4(4, 4)[:, t * HH + h, :], fk[:, at], qe[:, at], start=True, stop=True)
                mm.then_inc(sc_done, 1)
                pe.wait_ge(keN_ready, 1)
                for c in range(3):
                    if c == 2:
                        pe.wait_ge(scT_ready, 1)
                    t, b = c // 2, (c % 2) * HCHUNK
                    for h in range(HH):
                        mm = pe.matmul(by4(2 * c, 2)[:, h, :], keN[b:b + HCHUNK, t * HH + h, :],
                                       V(t, h)[b:b + HCHUNK, :], start=True, stop=True)
                    mm.then_inc(dS_done, 1)
                pe.wait_ge(scT_ready, 1)
                for t in range(NT):
                    if t == 0:
                        pe.wait_ge(Sp_ready, 1)
                    else:
                        pe.wait_ge(Sp_ready, 3)
                    for h in range(HH):
                        o = by4(6 if t == 0 else 0, 2)[:, h, :]
                        pe.matmul(o, scT[:, t * HH + h, :], V(t, h), start=True, stop=True)
                        for c in ((1,) if t == 0 else (2, 3)):
                            b = (c % 2) * HCHUNK
                            mm = pe.matmul(o[b:b + HCHUNK, :],
                                           qe[:, h * T + c * HCHUNK:h * T + (c + 1) * HCHUNK],
                                           hSp[c - 1][:, h, :], start=False, stop=True, skip_group_check=True)
                    mm.then_inc(o_done, 1)
                pe.wait_ge(o_scaled, 1)
                for h in range(HH):
                    for t in range(NT):
                        mm = pe.transpose(by4(2, 4)[:, h * 2 + t, :], hO[:, t * HH + h, :], ident[:, :])
                mm.then_inc(o_turned, 1)

            @block.scalar
            def _(act):
                act.wait_ge(ke_turned, 1)
                act.activation(keN, by4(0, 4), ACT.Copy).then_inc(keN_ready, 1)
                for t in range(NT):
                    act.wait_ge(o_done, t + 1)
                    o = by4(6 if t == 0 else 0, 2)
                    act.activation(hSq[:, t * HH:(t + 1) * HH, :], o, ACT.Square,
                                   scale=HD ** -0.5).then_inc(sq_ready, 1)
                    act.activation(hO[:, t * HH:(t + 1) * HH, :], o, ACT.Copy).then_inc(o_copied, 1)

            @block.gpsimd
            def _(pool):
                pool.wait_ge(sq_ready, 3)
                inv_sqrt(pool, hms[:, :], hms[:, :])

            @block.vector
            def _(dve):
                dve.wait_ge(sc_done, 1)
                dve.copy_predicated(scT[:, :, :], hmask[:, :].bitcast(U32).unsqueeze(1).to_broadcast([P, NT * HH, P]),
                                    by4(4, 4)).then_inc(scT_ready, 1)
                wide = lambda k, c: dec[:, k, :].rearrange("p (h c) -> p h c", c=4)[:, :, c:c + 1] \
                    .to_broadcast([P, HH, P])
                tmp = hSp[2]
                for c in range(3):
                    dve.wait_ge(dS_done, c + 1)
                    if c == 0:
                        dve_chain.step(dve, dve.tensor_tensor(hS, by4(0, 2), wide(2, 0), ALU.mult))
                    else:
                        dve.tensor_tensor(tmp, by4(2 * c, 2), wide(2, c), ALU.mult)
                        dve_chain.step(dve, dve.tensor_tensor(hS, hS, wide(1, c), ALU.mult))
                        dve_chain.step(dve, dve.tensor_tensor(hS, hS, tmp, ALU.add))
                    dve.tensor_tensor(hSp[c], hS, wide(0, c + 1), ALU.mult).then_inc(Sp_ready, 1)
                dve.wait_ge(sq_ready, 2)
                dve.tensor_reduce(hms[:, :], hSq, AX.X, ALU.add).then_inc(sq_ready, 1)
                dve.wait_ge(rstd_ready, rstds["n"])
                dve.wait_ge(o_copied, 2)
                dve.tensor_tensor(hO, hO, hms[:, :].unsqueeze(2).to_broadcast([P, NT * HH, P]),
                                  ALU.mult).then_inc(o_scaled, 1)
                dve.wait_ge(o_turned, 1)
                for h in range(HH):
                    dve.scalar_tensor_tensor(
                        out=ohT[:, h, :], in0=psum[:, 2 + h // 2, (h % 2) * T:(h % 2 + 1) * T],
                        scalar=gains[:, 8, h:h + 1],
                        in1=proj[:, SIG_HG + h // 2, (h % 2) * T:(h % 2 + 1) * T], op0=ALU.mult, op1=ALU.mult)
        hg.close()
        if stop == "hgrn":
            first.close()
            return

        sbx = ExitStack()
        osT = sb("osT", [P, SH // 2, T], ctx=sbx)
        sbk = ExitStack()
        qT = sb("qT", [P, SH // 2, T], ctx=sbk)
        kT = sb("kT", [P, SH // 2, T], ctx=sbk)
        q_gain = sb("q_gain", [P, KD], ctx=sbk)
        qk_turned = sem("qk_turned")
        with nc.Block(no_gpsimd_drain=True) as block:
            @block.vector
            def _(dve):
                dve_chain.step(dve, dve.tensor_scalar(q_gain[:, :], gains[:, 6, :], SD ** -0.5, None, ALU.mult))
                for i, (dst, g) in enumerate(((qT, q_gain[:, :]), (kT, gains[:, 7, :]))):
                    dve.wait_ge(qk_turned, i + 1)
                    dve.tensor_tensor(dst[:, :, :], psum[:, 4 * i:4 * i + 4, :].rearrange("p b (j t) -> p (b j) t", t=T),
                                      g.unsqueeze(2).to_broadcast([P, KD, T]), ALU.mult)

            @block.tensor
            def _(pe):
                for i in range(2):
                    for ft in range(KD):
                        for t in range(NT):
                            mm = pe.transpose(
                                psum[:, 4 * i + ft // 2, (ft % 2) * T + t * P:(ft % 2) * T + (t + 1) * P],
                                proj[:, QK_AT + 4 * i + ft // 2, t * 256 + (ft % 2) * P:t * 256 + (ft % 2 + 1) * P],
                                ident[:, :])
                    mm.then_inc(qk_turned, 1)

        sba = ExitStack()
        C3 = 3 * P
        za = sb("za", [P, 2, 4, C3], ctx=sba)
        by_group = lambda v: v.rearrange("p a n -> p (a n)").rearrange("p (g h c) -> p g h c", g=2, h=4)
        sp_m = by_group(proj[:, QK_AT:QK_AT + 6, :])
        wa = by_group(proj[:, 0:6, :])
        z_done, l_ready, spm_ready, r_done, w_ready, a_ready, so_done, so_out = (
            sem(n) for n in ("sb_z_done", "sb_log_ready", "sb_softplus_ready", "sb_logw_done", "sb_logw_ready",
                             "sb_weights_ready", "sb_o_done", "sb_o_out"))
        NGRP = SH // 4
        with nc.Block(no_gpsimd_drain=True) as block:
            @block.tensor
            def _(pe):
                def z(g):
                    if g >= 2:
                        pe.wait_ge(so_out, g - 1)
                    for j in range(4):
                        h = 4 * g + j
                        b, r = 4 * (g % 2) + j, slice((h % 2) * SD, (h % 2 + 1) * SD)
                        pe.matmul(psum[:, b, 0:T], kT[r, h // 2, 0:P], qT[r, h // 2, :], start=True, stop=True)
                        mm = pe.matmul(psum[:, b, T:C3], kT[r, h // 2, P:T], qT[r, h // 2, P:T],
                                       start=False, stop=True, skip_group_check=True)
                    mm.then_inc(z_done, 1)

                def r(g):
                    pe.wait_ge(spm_ready, g + 1)
                    for j in range(4):
                        b, m = 4 * (g % 2) + j, sp_m[:, g % 2, j, :]
                        pe.matmul(psum[:, b, 0:C3], neg_upper[:, :], m, start=False, stop=True,
                                  skip_group_check=True)
                        mm = pe.matmul(psum[:, b, P:T], neg_ones[:, :], m[:, T:C3], start=False, stop=True,
                                       skip_group_check=True)
                    mm.then_inc(r_done, 1)

                def o(g):
                    pe.wait_ge(a_ready, g + 1)
                    for j in range(4):
                        h = 4 * g + j
                        ob = psum[(h % 2) * SD:(h % 2 + 1) * SD, 4 * (g % 2) + j // 2, 0:T]
                        v = lambda kt: proj[:, SV_AT + h // 4, kt * 256 + (h % 4) * SD:kt * 256 + (h % 4 + 1) * SD]
                        pe.matmul(ob, v(0), wa[:, g % 2, j, 0:T], start=True, stop=True)
                        mm = pe.matmul(ob[:, P:T], v(1), wa[:, g % 2, j, T:C3], start=False, stop=True,
                                       skip_group_check=True)
                    mm.then_inc(so_done, 1)

                z(0)
                for g in range(NGRP):
                    if g + 1 < NGRP:
                        z(g + 1)
                    r(g)
                    o(g)

            @block.scalar
            def _(act):
                def logs(g):
                    act.wait_ge(z_done, g + 1)
                    a, zz = za[:, g % 2, :, :], psum[:, 4 * (g % 2):4 * (g % 2) + 4, 0:C3]
                    if g >= 2:
                        act.wait_ge(spm_ready, g - 1)
                    act_chain.step(act, act.activation(a, zz, ACT.Abs))
                    act_chain.step(act, act.activation(a, a, ACT.Exp, scale=-1.0))
                    act.activation(a, a, ACT.Ln, bias=1.0).then_inc(l_ready, 1)

                def weights(g):
                    act.wait_ge(w_ready, g + 1)
                    a = wa[:, g % 2, :, :]
                    act.activation(a, a, ACT.Exp).then_inc(a_ready, 1)
                    act.wait_ge(so_done, g + 1)
                    act.activation(osT[:, 2 * g:2 * g + 2, :], psum[:, 4 * (g % 2):4 * (g % 2) + 2, 0:T],
                                   ACT.Copy).then_inc(so_out, 1)

                logs(0)
                for g in range(NGRP):
                    if g + 1 < NGRP:
                        logs(g + 1)
                    weights(g)

            @block.vector
            def _(dve):
                def soft(g):
                    dve.wait_ge(l_ready, g + 1)
                    m, zz = sp_m[:, g % 2, :, :], psum[:, 4 * (g % 2):4 * (g % 2) + 4, 0:C3]
                    if g >= 2:
                        dve.wait_ge(r_done, g - 1)
                    dve_chain.step(dve, dve.scalar_tensor_tensor(
                        out=m, in0=zz, scalar=0.0, in1=za[:, g % 2, :, :], op0=ALU.max, op1=ALU.add))
                    dve.tensor_tensor(m, m, strict[:, :].unsqueeze(1).to_broadcast([P, 4, C3]),
                                      ALU.mult).then_inc(spm_ready, 1)

                def masked(g):
                    dve.wait_ge(r_done, g + 1)
                    if g >= 2:
                        dve.wait_ge(so_done, g - 1)
                    dve.tensor_tensor(wa[:, g % 2, :, :], psum[:, 4 * (g % 2):4 * (g % 2) + 4, 0:C3],
                                      strict_add[:, :].unsqueeze(1).to_broadcast([P, 4, C3]),
                                      ALU.add).then_inc(w_ready, 1)

                soft(0)
                for g in range(NGRP):
                    masked(g)
                    if g + 1 < NGRP:
                        soft(g + 1)
        sba.close()
        sbk.close()
        if stop == "sb":
            sbx.close(); first.close()
            return

        mx = ExitStack()
        mix = sb("mix", [P, KD, T], ctx=mx)
        mix_ready = sem("mix_ready")
        s_hg, s_sb, s_wo = FIRST_SLAB["hg_out"], FIRST_SLAB["sb_out"], FIRST_SLAB["w_o"]
        flat = lambda t, i: t[:, 2 * i:2 * i + 2, :].rearrange("p a t -> p (a t)")
        nat_cols = lambda t, i: t[:, :, 256 * i:256 * (i + 1)]
        bank_nat = lambda b: psum[:, b, :].rearrange("p (n c) -> p n c", n=NT)
        part = lambda i: proj[:, SIG_GB + i, :]
        src_b = [sb(n, [P, KD, T], F32R, ctx=mx) for n in ("inH2", "inL2")]
        split_input(ohT, src_in)
        split_input(osT, src_b)
        with nc.Block(no_gpsimd_drain=True) as block:
            @block.sync
            def _(sp):
                feed(sp, s_wo)

            @block.tensor
            def _(pe):
                project(pe, s_hg, 4, turned_slab, src_in)
                project(pe, s_sb, 4, turned_slab, src_b, before=4)

            @block.scalar
            def _(act):
                for s in range(s_hg, s_wo):
                    split_hi(act, s + RING)

            @block.vector
            def _(dve):
                for i in range(4):
                    dve.wait_ge(slab_used, s_hg + i + 1)
                    dve.tensor_tensor(flat(mix, i), psum[:, (s_hg + i) % BANKS, :], proj[:, SIG_GA + i, :],
                                      ALU.mult).then_inc(bank_read, 1)
                    split_lo(dve, s_hg + i + RING)
                for i in range(4):
                    dve.wait_ge(slab_used, s_sb + i + 1)
                    dve_chain.step(dve, dve.tensor_tensor(part(i), psum[:, (s_sb + i) % BANKS, :],
                                                          part(i), ALU.mult))
                    dve.tensor_tensor(flat(mix, i), flat(mix, i), part(i), ALU.add).then_inc(bank_read, 1)
                    split_lo(dve, s_sb + i + RING)
        end_slabs(8)
        split_input(mix, src_in)

        def onto_residual(s0):
            with nc.Block(no_gpsimd_drain=True) as block:
                @block.sync
                def _(sp):
                    feed(sp, s0 + 4)

                @block.tensor
                def _(pe):
                    project(pe, s0, 4, natural_slab, src_in)

                @block.scalar
                def _(act):
                    for i in range(4):
                        split_hi(act, s0 + i + RING)

                @block.vector
                def _(dve):
                    for i in range(4):
                        dve.wait_ge(slab_used, s0 + i + 1)
                        dve.tensor_tensor(nat_cols(x, i), nat_cols(x, i), bank_nat((s0 + i) % BANKS),
                                          ALU.add).then_inc(bank_read, 1)
                        split_lo(dve, s0 + i + RING)
            end_slabs(4)

        onto_residual(s_wo)
        mx.close()
        sbx.close()
        first.close()
        if stop == "mix":
            return

        norm_turn(x, src_in, 1)
        ff = ExitStack()
        act_H = sb("act_H", [P, FT, T], F32R, ctx=ff)
        act_L = sb("act_L", [P, FT, T], F32R, ctx=ff)
        gate = sb("gate", [P, BANKS, T], ctx=ff)
        both = sb("both", [P, BANKS, T], ctx=ff)
        silu_ready, both_ready = sem("silu_ready"), sem("ffn_both_ready")
        s_in, s_out = FIRST_SLAB["ffn_in"], FIRST_SLAB["ffn_out"]
        row = lambda t, i: t[:, bass.ds(i, 1), :].rearrange("p a t -> p (a t)")
        with nc.Block(no_gpsimd_drain=True) as block:
            @block.sync
            def _(sp):
                feed(sp, s_out + N_FFN_OUT)

            @block.tensor
            def _(pe):
                project(pe, s_in, N_FFN_IN, turned_slab, src_in)
                for i in range(N_FFN_OUT):
                    s = s_out + i
                    pe.wait_ge(split_ready, s + 1)
                    pe.wait_ge(bank_read, state["banks"] + min(2 * i + 2, FT))
                    w = weights_of(s % RING, 2)
                    for kk in range(2):
                        for n in range(NT):
                            for c in range(2):
                                mm = three(pe, psum[:, 4 + 2 * n + c, :],
                                           [v[:, 2 * i + kk, n * P:(n + 1) * P] for v in (act_H, act_L)],
                                           [v[:, kk, c * 512:(c + 1) * 512] for v in w],
                                           i == 0 and kk == 0, i == N_FFN_OUT - 1 and kk == 1)
                    mm.then_inc(slab_used, 1)

            @block.scalar
            def _(act):
                def body(s, it):
                    act.wait_ge(slab_used, at(it, s + 1))
                    act.wait_ge(bank_read, at(it, state["banks"] + s - s_in - BANKS + 1))
                    act.activation(gate[:, s % BANKS, :], psum[:, s % BANKS, 0:T], ACT.Silu).then_inc(silu_ready, 1)
                    split_hi(act, s + RING, it)
                per_slab(act, s_in, N_FFN_IN, body)
                for i in range(N_FFN_OUT):
                    split_hi(act, s_out + i + RING)

            @block.vector
            def _(dve):
                def body(s, it):
                    i, b = at(it, s - s_in), s % BANKS
                    dve.wait_ge(silu_ready, at(it, s - s_in + 1))
                    dve.tensor_tensor(both[:, b, :], gate[:, b, :], psum[:, b, T:2 * T],
                                      ALU.mult).then_inc(both_ready, 1)
                    dve.tensor_tensor(row(act_H, i), gate[:, b, :], psum[:, b, T:2 * T],
                                      ALU.mult).then_inc(both_ready, 1)
                    dve.wait_ge(both_ready, at(it, 2 * (s - s_in) + 2, 2 * GROUP))
                    dve.tensor_tensor(row(act_L, i), both[:, b, :], row(act_H, i).bitcast(F32),
                                      ALU.subtract).then_inc(bank_read, 1)
                    split_lo(dve, s + RING, it)
                per_slab(dve, s_in, N_FFN_IN, body)
                for i in range(N_FFN_OUT):
                    split_lo(dve, s_out + i + RING)
                dve.wait_ge(slab_used, s_out + N_FFN_OUT)
                for n in range(NT):
                    dve.tensor_tensor(x[:, n, :], x[:, n, :],
                                      psum[:, 4 + 2 * n:6 + 2 * n, :].rearrange("p b c -> p (b c)"), ALU.add)
        end_slabs(FT)
        ff.close()
        if stop == "ffn":
            return

        norm_turn(x, src_in, 2)
        N_WIN2 = 12
        SL_GQ, SL_GK, SL_GR, SL_NQ, SL_C, SL_SW, SL_GV, SL_V, SL_SMALL = 0, 1, 2, 4, 6, 7, 8, 10, 11
        second = ExitStack()
        catT = sb("catT", [P, KD, T], ctx=second)
        proj2 = sb("proj2", [P, N_WIN2, 512], ctx=second)
        nsx = ExitStack()
        w1 = sb("w1", [P, 2, CB // 2, P], ctx=nsx)
        w2k = sb("w2k", [P, 2, ND], ctx=nsx)
        w2v = sb("w2v", [P, ND], ctx=nsx)
        pos = sb("pos", [P, 2, CB // 2], ctx=nsx)
        relx = sb("relx", [BUCKETS + 1, NH], ctx=nsx)
        buckets = sb("buckets", [BUCKETS + 1, 2, 2 * T - 1], ctx=nsx)
        gla_w2 = sb("gla_w2", [GRANK, T], ctx=nsx)
        gla_vec = sb("gla_vec", [P, 3], ctx=nsx)
        N_SMALL2 = 8
        small2 = sem("small_weights_landed")

        def small_slab(pe, slot, bank, src):
            w = weights_of(slot, KD)
            for k in range(KD):
                three(pe, psum[:, bank, 0:T], [v[:, k, 0:P] for v in w], [v[:, k, :] for v in src],
                      k == 0, k == KD - 1)
            for n in range(NT):
                for k in range(KD):
                    mm = three(pe, psum[:, bank, T + 24 * n:T + 24 * (n + 1)],
                               [v[:, k, n * P:(n + 1) * P] for v in src],
                               [v[:, k, GRANK:GRANK + 24] for v in w], k == 0, k == KD - 1)
            return mm

        s_w2 = FIRST_SLAB["win2_turned"]
        with nc.Block(no_gpsimd_drain=True) as block:
            act_step, dve_step = copy_out(proj2, s_w2, N_WIN2 - 1)

            @block.sync
            def _(sp):
                sp.dma_start(w1[:, :, :, :], ins["cmp_w1"]).then_inc(small2, 16)
                for h in range(2):
                    sp.dma_start(w2k[:, h, :], ins["cmp_k_w2"]).then_inc(small2, 16)
                sp.dma_start(w2v[:, :], ins["cmp_v_w2"]).then_inc(small2, 16)
                sp.dma_start(pos[:, :, :], ins["cmp_pos"]).then_inc(small2, 16)
                sp.dma_start(relx[0:BUCKETS, :], ins["rel_bias"]).then_inc(small2, 16)
                sp.dma_start(buckets[:, :, :], ins["buckets"]).then_inc(small2, 16)
                sp.dma_start(gla_w2[:, :], ins["gla_w2"]).then_inc(small2, 16)
                sp.dma_start(gla_vec[:, :], ins["gla_vec"]).then_inc(small2, 16)
                feed(sp, s_w2 + N_WIN2)
                sp.wait_ge(small2, 16 * (N_SMALL2 + 1))

            @block.gpsimd
            def _(pool):
                pool_chain.step(pool, pool.memset(relx[BUCKETS:BUCKETS + 1, :], MASKED))

            @block.tensor
            def _(pe):
                project(pe, s_w2, 8, turned_slab, src_in)
                project(pe, s_w2 + 8, 3, natural_slab, src_in, before=8)
                project(pe, s_w2 + 11, 1, small_slab, src_in, before=11)

            @block.scalar
            def _(act):
                act_step(act)
                s = s_w2 + N_WIN2 - 1
                act.wait_ge(slab_used, s + 1)
                act.activation(proj2[0:GRANK, SL_SMALL, 0:T], psum[0:GRANK, s % BANKS, 0:T], ACT.Copy)
                act.activation(proj2[:, SL_SMALL, T:T + 48], psum[:, s % BANKS, T:T + 48],
                               ACT.Copy).then_inc(bank_read, 1)
                split_hi(act, s + RING)

            @block.vector
            def _(dve):
                dve_step(dve)
                split_lo(dve, s_w2 + N_WIN2 - 1 + RING)
        end_slabs(N_WIN2)

        gl = ExitStack()
        GP = GH // 2
        CH = GP * NT
        gu = sb("gu", [P, GP * T], ctx=gl)
        ga_ = sb("ga_", [P, GP * T], ctx=gl)
        gcum = sb("gcum", [P, GP * T], ctx=gl)
        gmask = sb("gmask", [P, GP * T], ctx=gl)
        gdec = sb("gdec", [P, 3, CH], ctx=gl)
        gfac = sb("gfac", [P, GP], ctx=gl)
        gscT = sb("gscT", [P, NT * GH, P], ctx=gl)
        gkeN = sb("gkeN", [P, GP * P], ctx=gl)
        gS = sb("gS", [P, GP, GV], ctx=gl)
        gO = sb("gO", [P, NT * GH, GV], ctx=gl)
        gSq = sb("gSq", [P, NT * GH, GV], ctx=gl)
        gms = sb("gms", [P, NT * GH], ctx=gl)
        gq = proj2[:, SL_GQ, :]
        gk = proj2[:, SL_GK, :]
        g_names = ("u_done", "u_ready", "l_ready", "mid_ready", "d_ready", "e_ready", "q_ready", "sc_done",
                   "turned", "keN_ready", "dS_done", "S_ready", "scT_ready", "o_done", "sq_ready", "ms_ready",
                   "o_scaled", "o_turned", "masks_ready")
        G = {n: sem("gla_" + n) for n in g_names}
        pairs_of = lambda v, s=P: v.rearrange("p (c s) -> p c s", s=s)
        gV = lambda t, h: proj2[:, SL_GV + h // 2, t * 256 + (h % 2) * GV:t * 256 + (h % 2 + 1) * GV]
        g_at = lambda c, h: (h % 2) * 4 + c * GP + h // 2
        rows = lambda h: slice((h % 2) * GD, (h % 2 + 1) * GD)
        with nc.Block(no_gpsimd_drain=True) as block:
            @block.tensor
            def _(pe):
                for f in range(GP):
                    mm = pe.matmul(psum[:, 0, f * T:(f + 1) * T], gla_w2[:, f * P:(f + 1) * P],
                                   proj2[0:GRANK, SL_SMALL, 0:T], start=True, stop=True)
                mm.then_inc(G["u_done"], 1)
                pe.wait_ge(G["q_ready"], 1)
                for f in range(GP):
                    mm = pe.transpose(psum[:, 3, f * P:(f + 1) * P], gk[:, f * T:f * T + P], ident[:, :])
                mm.then_inc(G["turned"], 1)
                for c in range(NT):
                    for h in range(GH):
                        at_ = slice((h // 2) * T + c * P, (h // 2) * T + (c + 1) * P)
                        mm = pe.matmul(by4(1, 2)[:, g_at(c, h), :], gk[rows(h), at_], gq[rows(h), at_],
                                       start=True, stop=True)
                mm.then_inc(G["sc_done"], 1)
                pe.wait_ge(G["keN_ready"], 1)
                for h in range(GH):
                    mm = pe.matmul(psum[rows(h), 0, (h // 2) * GV:(h // 2 + 1) * GV], gkeN[:, h * GD:(h + 1) * GD],
                                   gV(0, h), start=True, stop=True)
                mm.then_inc(G["dS_done"], 1)
                pe.wait_ge(G["scT_ready"], 1)
                pe.wait_ge(G["S_ready"], 1)
                for c in range(NT):
                    for h in range(GH):
                        o = by4(4, 2)[:, g_at(c, h), :]
                        mm = pe.matmul(o, gscT[:, g_at(c, h), :], gV(c, h), start=True, stop=(c == 0))
                        if c == 1:
                            mm = pe.matmul(o, gq[rows(h), (h // 2) * T + P:(h // 2 + 1) * T], gS[rows(h), h // 2, :],
                                           start=False, stop=True)
                mm.then_inc(G["o_done"], 1)
                pe.wait_ge(G["o_scaled"], 1)
                for h in range(GH):
                    for c in range(NT):
                        mm = pe.transpose(by4(6, 2)[:, h * 2 + c, :], gO[:, g_at(c, h), :], ident[:, :])
                mm.then_inc(G["o_turned"], 1)

            @block.gpsimd
            def _(pool):
                pool_chain.step(pool, pool.memset(gmask[:, :], 1.0))
                pool_chain.step(pool, pool.memset(pairs_of(gmask[:, :])[:, :, 0:1], 0.0))
                pool.memset(gscT[:, :, :], 0.0).then_inc(G["masks_ready"], 1)
                pool.wait_ge(G["ms_ready"], 1)
                inv_sqrt(pool, gms[:, :], gms[:, :])


            @block.scalar
            def _(act):
                act.wait_ge(G["u_ready"], 1)
                act_chain.step(act, act.activation(ga_[:, :], gu[:, :], ACT.Abs))
                act_chain.step(act, act.activation(ga_[:, :], ga_[:, :], ACT.Exp, scale=-1.0))
                act.activation(ga_[:, :], ga_[:, :], ACT.Ln, bias=1.0).then_inc(G["l_ready"], 1)
                act.wait_ge(G["mid_ready"], 1)
                act.activation(gdec[:, :, :], gdec[:, :, :], ACT.Exp, scale=1 / GTAU).then_inc(G["e_ready"], 1)
                act.wait_ge(G["d_ready"], 1)
                act.activation(ga_[:, :], gu[:, :], ACT.Exp, scale=1 / GTAU).then_inc(G["e_ready"], 1)
                act.activation(gcum[:, :], gu[:, :], ACT.Exp, scale=-1 / GTAU).then_inc(G["e_ready"], 1)
                act.wait_ge(G["turned"], 1)
                act.activation(gkeN[:, :], psum[:, 3, 0:GP * P], ACT.Copy).then_inc(G["keN_ready"], 1)
                silu = proj2[:, SL_GR:SL_GR + 2, :]
                act_chain.step(act, act.activation(silu, silu, ACT.Silu))
                act.wait_ge(G["o_done"], 1)
                act.activation(gSq[:, :, :], by4(4, 2), ACT.Square, scale=GV ** -0.5).then_inc(G["sq_ready"], 1)
                act.activation(gO[:, :, :], by4(4, 2), ACT.Copy).then_inc(G["sq_ready"], 1)

            @block.vector
            def _(dve):
                dve.wait_ge(G["u_done"], 1)
                for f in range(GP):
                    o = dve.tensor_scalar(gu[:, f * T:(f + 1) * T], psum[:, 0, f * T:(f + 1) * T],
                                          gla_vec[:, f:f + 1], None, ALU.add)
                o.then_inc(G["u_ready"], 1)
                dve.wait_ge(G["l_ready"], 1)
                dve_chain.step(dve, dve.scalar_tensor_tensor(out=gu[:, :], in0=gu[:, :], scalar=0.0, in1=ga_[:, :],
                                                             op0=ALU.min, op1=ALU.subtract))
                dve.wait_ge(G["masks_ready"], 1)
                dve_chain.step(dve, dve.tensor_tensor_scan(gcum[:, :], gmask[:, :], gu[:, :], 0.0,
                                                           ALU.mult, ALU.add))
                mid = pairs_of(gcum[:, :])[:, :, P // 2 - 1:P // 2]
                last = pairs_of(gcum[:, :])[:, :, P - 1:P]
                dve.tensor_copy(gdec[:, 0, :].unsqueeze(2), mid)
                dve.tensor_copy(gdec[:, 1, :].unsqueeze(2), last)
                dve.tensor_tensor(gdec[:, 2, :].unsqueeze(2), last, mid, ALU.subtract).then_inc(G["mid_ready"], 1)
                dve_chain.step(dve, dve.tensor_tensor(pairs_of(gu[:, :]), pairs_of(gcum[:, :]),
                                                      mid.to_broadcast([P, CH, P]), ALU.subtract))
                dve.tensor_scalar(gu[:, :], gu[:, :], EXPO_CAP * GTAU, -EXPO_CAP * GTAU, ALU.min,
                                  ALU.max).then_inc(G["d_ready"], 1)
                dve.wait_ge(G["e_ready"], 3)
                dve.scalar_tensor_tensor(out=gq, in0=gq, scalar=GD ** -0.5, in1=ga_[:, :], op0=ALU.mult,
                                         op1=ALU.mult)
                dve.tensor_tensor(gk, gk, gcum[:, :], ALU.mult).then_inc(G["q_ready"], 1)
                dve_chain.step(dve, dve.tensor_tensor(gfac[:, :].unsqueeze(2),
                                                      gdec[:, 2, :].rearrange("p (f c) -> p f c", c=NT)[:, :, 0:1],
                                                      gdec[:, 0, :].rearrange("p (f c) -> p f c", c=NT)[:, :, 1:2],
                                                      ALU.mult))
                dve.wait_ge(G["sc_done"], 1)
                dve.copy_predicated(gscT[:, :, :], causal[:, :].bitcast(U32).unsqueeze(1).to_broadcast([P, NT * GH, P]),
                                    by4(1, 2)).then_inc(G["scT_ready"], 1)
                dve.wait_ge(G["dS_done"], 1)
                dve.tensor_tensor(gS[:, :, :], psum[:, 0, 0:GP * GV].rearrange("p (f v) -> p f v", f=GP),
                                  gfac[:, :].unsqueeze(2).to_broadcast([P, GP, GV]), ALU.mult).then_inc(G["S_ready"], 1)
                dve.wait_ge(G["sq_ready"], 1)
                dve.tensor_reduce(gms[:, :], gSq[:, :, :], AX.X, ALU.add).then_inc(G["ms_ready"], 1)
                dve.wait_ge(rstd_ready, rstds["n"])
                dve.wait_ge(G["sq_ready"], 2)
                dve.tensor_tensor(gO[:, :, :], gO[:, :, :], gms[:, :].unsqueeze(2).to_broadcast([P, NT * GH, GV]),
                                  ALU.mult).then_inc(G["o_scaled"], 1)
                dve.wait_ge(G["o_turned"], 1)
                for h in range(GH):
                    dve.scalar_tensor_tensor(
                        out=catT[:, h, :], in0=psum[:, 6 + h // 2, (h % 2) * T:(h % 2 + 1) * T],
                        scalar=gla_vec[:, 2:3], in1=proj2[:, SL_GR + h // 2, (h % 2) * T:(h % 2 + 1) * T],
                        op0=ALU.mult, op1=ALU.mult)
        gl.close()
        if stop == "gla":
            nsx.close(); second.close()
            return

        nb = ExitStack()
        bias = sb("bias", [P, NH, T], ctx=nsx)
        bias_c = sb("bias_c", [P, NT, NCMP, NH], ctx=nsx)
        kdup = sb("kdup", [P, 2, NG, T], ctx=nsx)
        kcmp = sb("kcmp", [P, NG, NCMP], ctx=nsx)
        vcmp = sb("vcmp", [NCMP, NG, ND], ctx=nsx)
        ngate = sb("ngate", [P, NT, 3 * NH], ctx=nsx)
        gsel = sb("gsel", [P, NH, 6], ctx=nsx)
        seen = sb("seen", [P, 1], ctx=nsx)
        kc2 = sb("kc2", [P, 2, NG, T], ctx=nb)
        hid = sb("hid", [P, 2, NG * NCMP], ctx=nb)
        posb = sb("posb", [P, 2], ctx=nb)
        bias_up = sb("bias_up", [P, NH, T], ctx=nb)
        turn_over = sb("turn_over", [P, P], ctx=nb)
        line = sb("line", [NH, 2 * T], ctx=nb)
        bias_line = nc.dram_tensor("bias_line", [NH, 2 * T], F32, kind="Internal").ap()
        N_ = {n: sem("nsa_" + n) for n in (
            "line_done", "line_ready", "line_stored", "bias_landed", "cmp_bias_done", "cmp_bias_ready", "kc_ready",
            "hid_done", "pos_ready", "hid_ready", "cmp_done", "gate_ready", "seen_ready", "over_ready",
            "bias_done")}
        with nc.Block(no_gpsimd_drain=True) as block:
            @block.sync
            def _(sp):
                sp.wait_ge(N_["line_ready"], 1)
                sp.dma_start(bias_line[:, 0:2 * T - 1], line[:, 0:2 * T - 1]).then_inc(N_["line_stored"], 16)
                sp.wait_ge(N_["line_stored"], 16)
                toeplitz = bass.AP(bias_line.tensor, 0, [[1, P], [2 * T, NH], [1, T]])
                sp.dma_start(bias_up[:, :, :], toeplitz).then_inc(N_["bias_landed"], 16)
                sp.wait_ge(N_["bias_landed"], 16)

            @block.tensor
            def _(pe):
                pe.matmul(psum[0:NH, 0, 0:2 * T - 1], relx[:, :], buckets[:, 1, :], start=True,
                          stop=True).then_inc(N_["line_done"], 1)
                for t in range(NT):
                    for n in range(NCMP):
                        at_ = T - 1 + t * P - CS * n - (CB - 1)
                        i = (t * NCMP + n) * NH
                        mm = pe.matmul(psum[:, 1, i:i + NH], buckets[:, 0, at_:at_ + P], relx[:, :],
                                       start=True, stop=True)
                mm.then_inc(N_["cmp_bias_done"], 1)
                pe.wait_ge(N_["kc_ready"], 1)
                for kv in range(2):
                    for j in range(CB // 2):
                        src = kc2[:, kv, :, :].rearrange("p g (b s) -> p g b s", s=CS)
                        pe.matmul(psum[:, 2 + kv, 0:NG * NCMP], w1[:, kv, j, :],
                                  src[:, :, 2 * j // CS:2 * j // CS + NCMP, 2 * j % CS],
                                  start=(j == 0), stop=(j == CB // 2 - 1))
                        mm = pe.matmul(psum[:, 4 + kv, 0:1], w1[:, kv, j, :], pos[:, kv, j:j + 1],
                                       start=(j == 0), stop=(j == CB // 2 - 1))
                    mm.then_inc(N_["hid_done"], 1)
                pe.wait_ge(N_["hid_ready"], 2)
                pe.matmul(psum[:, 6, 0:NG * NCMP], w2k[:, :, :].rearrange("p a d -> p (a d)"), hid[:, 0, :],
                          start=True, stop=True).then_inc(N_["cmp_done"], 1)
                for g in range(NG):
                    mm = pe.matmul(psum[0:NCMP, 7, g * ND:(g + 1) * ND], hid[:, 1, g * NCMP:(g + 1) * NCMP],
                                   w2v[:, :], start=True, stop=True)
                mm.then_inc(N_["cmp_done"], 1)
                pe.wait_ge(N_["over_ready"], 1)
                pe.wait_ge(N_["bias_landed"], 16)
                pe.wait_ge(N_["cmp_bias_ready"], 1)
                pe.wait_ge(N_["line_ready"], 1)
                for b in range(4):
                    mm = pe.matmul(psum[:, b, :], turn_over[:, :],
                                   bias_up[:, 2 * b:2 * b + 2, :].rearrange("p h c -> p (h c)"),
                                   start=True, stop=True)
                mm.then_inc(N_["bias_done"], 1)

            @block.scalar
            def _(act):
                act.wait_ge(N_["line_done"], 1)
                act.activation(line[:, 0:2 * T - 1], psum[0:NH, 0, 0:2 * T - 1], ACT.Copy).then_inc(N_["line_ready"], 1)
                act.activation(ngate[:, :, :].rearrange("p n c -> p (n c)"), proj2[:, SL_SMALL, T:T + 3 * NT * NH],
                               ACT.Sigmoid).then_inc(N_["gate_ready"], 1)
                for kv in range(2):
                    act.wait_ge(N_["hid_done"], kv + 1)
                    act_chain.step(act, act.activation(posb[:, kv:kv + 1], psum[:, 4 + kv, 0:1], ACT.Copy))
                    act.activation(hid[:, kv, :], psum[:, 2 + kv, 0:NG * NCMP], ACT.Gelu_apprx_tanh,
                                   bias=posb[:, kv:kv + 1]).then_inc(N_["hid_ready"], 1)
                act.wait_ge(N_["cmp_done"], 2)
                act.activation(kcmp[:, :, :].rearrange("p g n -> p (g n)"), psum[:, 6, 0:NG * NCMP], ACT.Copy)
                act.activation(vcmp[:, :, :].rearrange("p g d -> p (g d)"), psum[0:NCMP, 7, 0:NG * ND], ACT.Copy)

            @block.gpsimd
            def _(pool):
                pool_chain.step(pool, pool.memset(seen[:, :], 1.0))
                pool_chain.step(pool, pool.memset(turn_over[:, :], 0.0))
                pool.affine_select(out=turn_over[:, :], in_=turn_over[:, :], compare_op=ALU.not_equal, fill=1.0,
                                   base=-(P - 1), pattern=[[1, P]], channel_multiplier=1).then_inc(N_["over_ready"], 1)
                pool.affine_select(out=seen[:, :], in_=seen[:, :], compare_op=ALU.is_ge, fill=0.0,
                                   base=-(CB - 1), pattern=[[1, 1]],
                                   channel_multiplier=1).then_inc(N_["seen_ready"], 1)

            @block.vector
            def _(dve):
                two = lambda r, sl: proj2[r, sl, :].rearrange("p (a t) -> p a t", a=2)
                for g in range(NG):
                    r = slice(g * ND, (g + 1) * ND)
                    dve.tensor_copy(kc2[0:ND, :, g, :], two(r, SL_C))
                    o = dve.tensor_copy(kc2[ND:P, :, g, 0:T - 1], two(r, SL_C)[:, :, 1:T])
                o.then_inc(N_["kc_ready"], 1)
                for g in range(NG):
                    r = slice(g * ND, (g + 1) * ND)
                    for half in range(2):
                        dve.tensor_copy(kdup[half * ND:(half + 1) * ND, :, g, :], two(r, SL_SW))
                dve.wait_ge(N_["cmp_bias_done"], 1)
                dve.tensor_copy(bias_c[:, :, :, :].rearrange("p t n h -> p (t n h)"), psum[:, 1, 0:NT * NCMP * NH])\
                   .then_inc(N_["cmp_bias_ready"], 1)
                dve.wait_ge(N_["gate_ready"], 1)
                ng3 = lambda t: ngate[:, t, :].rearrange("p (h i) -> p h i", i=3)
                dve.tensor_copy(gsel[:, :, 0:2], ng3(1)[:, :, 1:3])
                dve.tensor_copy(gsel[:, :, 2:4], ng3(0)[:, :, 1:3])
                dve.wait_ge(N_["seen_ready"], 1)
                dve.tensor_scalar(gsel[:, :, 4:5], ng3(0)[:, :, 0:1], seen[:, 0:1], None, ALU.mult)
                dve.tensor_copy(gsel[:, :, 5:6], ng3(1)[:, :, 0:1])
                dve.wait_ge(N_["bias_done"], 1)
                dve.tensor_copy(bias[:, :, :].rearrange("p (b h) c -> p b (h c)", b=4), psum[:, 0:4, :])
        nb.close()

        na = ExitStack()
        SC = 512 + 256 + NT * NCMP
        sc = sb("sc", [P, 2, SC + 2], ctx=na)
        negm = sb("negm", [P, 2, 6], ctx=na)
        den = sb("den", [P, 2, 6], ctx=na)
        coef = sb("coef", [P, 2, 6], ctx=na)
        pT = sb("pT", [P, 2, 2, 3 * P], ctx=na)
        pTc = sb("pTc", [NCMP, 2, T], ctx=na)
        A_ = {n: sem("na_" + n) for n in ("s_done", "scored", "max_ready", "exp_ready", "scaled", "t_done",
                                          "pT_ready", "o_done", "o_out")}
        SPANS = [(0, 256), (256, 512), (512, 640), (640, 768), (768, 768 + NCMP), (768 + NCMP, 768 + 2 * NCMP)]
        nqT = lambda h: proj2[(h % 2) * ND:(h % 2 + 1) * ND, SL_NQ + h // 4, ((h // 2) % 2) * T:((h // 2) % 2 + 1) * T]
        half = lambda h: slice((h % 2) * ND, (h % 2 + 1) * ND)
        with nc.Block(no_gpsimd_drain=True) as block:
            @block.tensor
            def _(pe):
                def scores(h):
                    g, bA, bB = h // (NH // NG), 2 * (h % 2), 2 * (h % 2) + 1
                    if h >= 2:
                        pe.wait_ge(A_["scored"], h - 1)
                    q = nqT(h)
                    for i in range(2):
                        pe.matmul(psum[:, bA, i * T:(i + 1) * T], q[:, P:T], kdup[half(h), i, g, :],
                                  start=True, stop=True)
                    for i in range(2):
                        pe.matmul(psum[:, bB, i * P:(i + 1) * P], q[:, 0:P], kdup[half(h), i, g, 0:P],
                                  start=True, stop=True)
                    for t in range(NT):
                        mm = pe.matmul(psum[:, bB, T + t * NCMP:T + (t + 1) * NCMP], q[:, t * P:(t + 1) * P],
                                       kcmp[half(h), g, :], start=True, stop=True)
                    mm.then_inc(A_["s_done"], 1)

                def turn(h):
                    pe.wait_ge(A_["scaled"], h + 1)
                    if h >= 1:
                        pe.wait_ge(A_["pT_ready"], h)
                    s = sc[:, h % 2, :]
                    for i in range(2):
                        b = 4 + i
                        pe.transpose(psum[:, b, 0:P], s[:, 512 + i * P:512 + (i + 1) * P], ident[:, :])
                        pe.transpose(psum[:, b, P:T], s[:, i * T:i * T + P], ident[:, :])
                        pe.transpose(psum[:, b, T:3 * P], s[:, i * T + P:(i + 1) * T], ident[:, :])
                        mm = pe.transpose(psum[0:NCMP, b, 3 * P:4 * P], s[:, 768 + i * NCMP:768 + (i + 1) * NCMP],
                                          ident[:, :])
                    mm.then_inc(A_["t_done"], 1)

                def outputs(h):
                    g = h // (NH // NG)
                    pe.wait_ge(A_["pT_ready"], h + 1)
                    if h % 2 == 0 and h >= 4:
                        pe.wait_ge(A_["o_out"], h // 2 - 1)
                    o = psum[half(h), 6 + (h // 2) % 2, 0:T]
                    for i in range(2):
                        v = lambda kt: proj2[:, SL_V, kt * 256 + i * P + g * ND:kt * 256 + i * P + (g + 1) * ND]
                        pe.matmul(o, v(0), pT[:, h % 2, i, 0:T], start=(i == 0), stop=True, skip_group_check=True)
                        pe.matmul(o[:, P:T], v(1), pT[:, h % 2, i, T:3 * P], start=False, stop=True,
                                  skip_group_check=True)
                    mm = pe.matmul(o, vcmp[:, g, :], pTc[:, h % 2, :], start=False, stop=True,
                                   skip_group_check=True)
                    mm.then_inc(A_["o_done"], 1)

                scores(0)
                for h in range(NH):
                    if h + 1 < NH:
                        scores(h + 1)
                    turn(h)
                    outputs(h)

            @block.scalar
            def _(act):
                def exps(h):
                    act.wait_ge(A_["max_ready"], h + 1)
                    for i, (a, b) in enumerate(SPANS):
                        e = act.activation(sc[:, h % 2, a:b], sc[:, h % 2, a:b], ACT.Exp,
                                           bias=negm[:, h % 2, i:i + 1], accum_out=den[:, h % 2, i:i + 1])
                    e.then_inc(A_["exp_ready"], 1)

                exps(0)
                for h in range(NH):
                    act.wait_ge(A_["t_done"], h + 1)
                    if h >= 2:
                        act.wait_ge(A_["o_done"], h - 1)
                    act.activation(pT[:, h % 2, :, :], psum[:, 4:6, 0:3 * P], ACT.Copy)
                    act.activation(pTc[:, h % 2, :].rearrange("p (t q) -> p t q", t=NT), psum[0:NCMP, 4:6, 3 * P:4 * P],
                                   ACT.Copy).then_inc(A_["pT_ready"], 1)
                    if h + 1 < NH:
                        exps(h + 1)
                    if h % 2 == 1:
                        act.wait_ge(A_["o_done"], h + 1)
                        act.activation(catT[:, 4 + h // 2, :], psum[:, 6 + (h // 2) % 2, 0:T],
                                       ACT.Copy).then_inc(A_["o_out"], 1)

            @block.vector
            def _(dve):
                SCALE = ND ** -0.5

                def score(h):
                    dve.wait_ge(A_["s_done"], h + 1)
                    if h >= 2:
                        dve.wait_ge(A_["t_done"], h - 1)
                    s, bA, bB = sc[:, h % 2, :], 2 * (h % 2), 2 * (h % 2) + 1
                    wide = lambda v, n: v.rearrange("p (a c) -> p a c", a=n)
                    dve.scalar_tensor_tensor(out=wide(s[:, 0:512], 2), in0=wide(psum[:, bA, :], 2), scalar=SCALE,
                                             in1=bias[:, h:h + 1, :].to_broadcast([P, 2, T]),
                                             op0=ALU.mult, op1=ALU.add)
                    dve.scalar_tensor_tensor(out=wide(s[:, 512:768], 2), in0=wide(psum[:, bB, 0:256], 2), scalar=SCALE,
                                             in1=bias[:, h:h + 1, P:T].to_broadcast([P, 2, P]),
                                             op0=ALU.mult, op1=ALU.add)
                    o = dve.scalar_tensor_tensor(
                        out=s[:, 768:768 + 2 * NCMP], in0=psum[:, bB, T:T + 2 * NCMP], scalar=SCALE,
                        in1=bias_c[:, :, :, h].rearrange("p t n -> p (t n)"), op0=ALU.mult, op1=ALU.add)
                    o.then_inc(A_["scored"], 1)
                    dve.wait_ge(A_["scored"], h + 1)
                    nm = negm[:, h % 2, :]
                    dve.tensor_reduce(nm[:, 0:2], wide(s[:, 0:512], 2), AX.X, ALU.max, negate=True)
                    dve.tensor_reduce(nm[:, 2:4], wide(s[:, 512:768], 2), AX.X, ALU.max, negate=True)
                    dve.tensor_reduce(nm[:, 4:6], wide(s[:, 768:768 + 2 * NCMP], 2), AX.X, ALU.max,
                                      negate=True).then_inc(A_["max_ready"], 1)

                def scale(h):
                    dve.wait_ge(A_["exp_ready"], h + 1)
                    c = coef[:, h % 2, :]
                    dve_chain.step(dve, dve.reciprocal(c, den[:, h % 2, :]))
                    dve_chain.step(dve, dve.tensor_tensor(c, c, gsel[:, h, :], ALU.mult))
                    for i, (a, b) in enumerate(SPANS):
                        o = dve.tensor_scalar(sc[:, h % 2, a:b], sc[:, h % 2, a:b], c[:, i:i + 1], None, ALU.mult)
                    o.then_inc(A_["scaled"], 1)

                score(0)
                for h in range(NH):
                    if h + 1 < NH:
                        score(h + 1)
                    scale(h)
        na.close()
        nsx.close()
        if stop == "nsa":
            second.close()
            return

        split_input(catT, src_in)
        onto_residual(FIRST_SLAB["w_out"])
        second.close()
        if stop == "wout":
            return

        xa = ExitStack()
        src_mem = [sb(n, [P, KD, T], F32R, ctx=xa) for n in ("memH", "memL")]
        xp = sb("xp", [P, 12, 512], ctx=xa)
        xoT = sb("xoT", [P, KD, T], ctx=xa)
        xs = sb("xs", [P, NT * XH, T], ctx=xa)
        xpT = sb("xpT", [P, XH, NT, T], ctx=xa)
        xneg = sb("xneg", [P, NT * XH], ctx=xa)
        xden = sb("xden", [P, NT * XH], ctx=xa)
        mem = xs[:, :, :].rearrange("p (n a) t -> p n (a t)", n=NT)
        X_ = {n: sem("xa_" + n) for n in ("mem_landed", "s_done", "max_ready", "exp_ready", "scaled", "t_done",
                                          "pT_ready", "o_done")}
        with nc.Block(no_gpsimd_drain=True) as block:
            @block.sync
            def _(sp):
                sp.dma_start(mem, ins["mem"].rearrange("b (t p) d -> p (b t) d", p=P)).then_inc(X_["mem_landed"], 16)
                sp.wait_ge(X_["mem_landed"], 16)
        norm_turn(mem, src_mem, 4)
        norm_turn(x, src_in, 3)
        s_xa = FIRST_SLAB["xa_wk"]
        with nc.Block(no_gpsimd_drain=True) as block:
            act_step, dve_step = copy_out(xp, s_xa, 12)

            @block.sync
            def _(sp):
                feed(sp, s_xa + 12)

            @block.tensor
            def _(pe):
                project(pe, s_xa, 4, turned_slab, src_mem)
                project(pe, s_xa + 4, 4, natural_slab, src_mem, before=4)
                project(pe, s_xa + 8, 4, turned_slab, src_in, before=8)

            @block.scalar
            def _(act):
                act_step(act)

            @block.vector
            def _(dve):
                dve_step(dve)
        end_slabs(12)
        tile_of = lambda s0, f: xp[:, s0 + f // 2, (f % 2) * T:(f % 2 + 1) * T]
        by2 = lambda b, n: psum[:, b:b + n, :].rearrange("p b (j c) -> p (b j) c", c=T)
        XT = XD // P
        with nc.Block(no_gpsimd_drain=True) as block:
            @block.tensor
            def _(pe):
                for h in range(XH):
                    for t in range(NT):
                        for j in range(XT):
                            mm = pe.matmul(by2(0, 4)[:, h * NT + t, :], tile_of(8, XT * h + j)[:, t * P:(t + 1) * P],
                                           tile_of(0, XT * h + j), start=(j == 0), stop=(j == XT - 1))
                mm.then_inc(X_["s_done"], 1)
                for h in range(XH):
                    pe.wait_ge(X_["scaled"], h + 1)
                    for m in range(NT):
                        for t in range(NT):
                            mm = pe.transpose(by2(4, 4)[:, h * NT + m, t * P:(t + 1) * P],
                                              xs[:, h * NT + t, m * P:(m + 1) * P], ident[:, :])
                    mm.then_inc(X_["t_done"], 1)
                for h in range(XH):
                    pe.wait_ge(X_["pT_ready"], h + 1)
                    for j in range(XT):
                        for m in range(NT):
                            v = xp[:, 4 + h, m * 256 + j * P:m * 256 + (j + 1) * P]
                            mm = pe.matmul(by2(0, 4)[:, XT * h + j, :], v, xpT[:, h, m, :],
                                           start=(m == 0), stop=(m == NT - 1))
                mm.then_inc(X_["o_done"], 1)

            @block.scalar
            def _(act):
                act.wait_ge(X_["max_ready"], 1)
                for i in range(NT * XH):
                    act.activation(xs[:, i, :], by2(0, 4)[:, i, :], ACT.Exp, bias=xneg[:, i:i + 1], scale=XD ** -0.5,
                                   accum_out=xden[:, i:i + 1]).then_inc(X_["exp_ready"], 1)
                for h in range(XH):
                    act.wait_ge(X_["t_done"], h + 1)
                    act.activation(xpT[:, h, :, :], by2(4, 4)[:, h * NT:(h + 1) * NT, :],
                                   ACT.Copy).then_inc(X_["pT_ready"], 1)
                act.wait_ge(X_["o_done"], 1)
                act.activation(xoT[:, :, :], by2(0, 4), ACT.Copy)

            @block.vector
            def _(dve):
                dve.wait_ge(X_["s_done"], 1)
                dve_chain.step(dve, dve.tensor_reduce(xneg[:, :], by2(0, 4), AX.X, ALU.max, negate=True))
                dve.tensor_scalar(xneg[:, :], xneg[:, :], XD ** -0.5, None, ALU.mult).then_inc(X_["max_ready"], 1)
                dve.wait_ge(X_["exp_ready"], NT * XH)
                dve_chain.step(dve, dve.reciprocal(xden[:, :], xden[:, :]))
                for h in range(XH):
                    for t in range(NT):
                        i = h * NT + t
                        o = dve.tensor_scalar(xs[:, i, :], xs[:, i, :], xden[:, i:i + 1], None, ALU.mult)
                    o.then_inc(X_["scaled"], 1)
        split_input(xoT, src_in)
        onto_residual(FIRST_SLAB["xa_wo"])
        xa.close()
        if stop == "xa":
            return

        norm_turn(x, src_in, 5)
        s_pq, s_down, s_up = FIRST_SLAB["peer_wq"], FIRST_SLAB["peer_down"], FIRST_SLAB["peer_up"]
        N_DOWN, N_UP = PK // 2, PK // 2
        KH = PH * PTOP
        assert KH == P and PK == P
        pr = ExitStack()
        HID = sb("hidden", [P, PK, T], ctx=pr)
        iota_e = sb("iota_e", [P, P], ctx=pr)
        gbx = ExitStack()
        IT, JT, GT = (sb(n, [P, T], ctx=gbx) for n in ("IT", "JT", "GT"))
        TAIL = 80
        room = HID[:, TAIL:PK, :].rearrange("p i t -> p (i t)")
        taken = {"words": 0}

        def in_room(*shape, dt=F32):
            n = int(np.prod(shape))
            lo = taken["words"]
            taken["words"] += n
            assert taken["words"] <= (PK - TAIL) * T
            v = room[:, lo:lo + n]
            v = v if dt is F32 else v.bitcast(dt)
            letters = "abcd"[:len(shape)]
            return v.rearrange(f"p ({' '.join(letters)}) -> p {' '.join(letters)}",
                               **dict(zip(letters[1:], shape[1:])))

        NHALF = 2 * PH
        pqT = in_room(PH, T)
        subk = in_room(PH, PK)
        work = in_room(NHALF, PK)
        cand = in_room(PH, PTOP * PTOP)
        cwork = in_room(PH, PTOP * PTOP)
        vals = in_room(NHALF, PTOP)
        idx_u = in_room(NHALF, PTOP, dt=U32)
        idx_f = in_room(NHALF, PTOP)
        ts_ = in_room(PH, PTOP)
        tpos = in_room(PH, PTOP, dt=U32)
        ab_u = in_room(2, PH, PTOP, dt=U32)
        ab_f = in_room(2, PH, PTOP)
        zsum = in_room(PH, 1)
        tables = in_room(3, NT, KH)
        R_ = {n: sem("peer_" + n) for n in (
            "loads", "iota_ready", "scored", "scores_read", "exp_in", "exp_out", "table_ready", "turned",
            "room_left", "j_near", "j_ready", "i_ready", "gi_ready", "g_done", "g_used", "tile_hi", "tile_ready", "half_used",
            "up_hi", "up_ready")}
        with nc.Block(no_gpsimd_drain=True) as block:
            act_step, dve_step = copy_out(pqT.rearrange("p (a c) t -> p a (c t)", c=2), s_pq, 4)

            @block.sync
            def _(sp):
                sp.dma_start(subk, ins["subkeys"]).then_inc(R_["loads"], 16)
                feed(sp, s_pq + 4)
                sp.wait_ge(R_["loads"], 16)

            @block.gpsimd
            def _(pool):
                pool.iota(iota_e[:, :], pattern=[[1, P]], base=0, channel_multiplier=0,
                          allow_small_or_imprecise_dtypes=True).then_inc(R_["iota_ready"], 1)

            @block.tensor
            def _(pe):
                project(pe, s_pq, 4, turned_slab, src_in)

            @block.scalar
            def _(act):
                act_step(act)

            @block.vector
            def _(dve):
                dve_step(dve)
        end_slabs(4)

        LOWEST = -3.0e38
        N_STEPS = 17
        EXP_STEP = 11
        SCORE_SLAB = 12
        TABLE_SLAB = NT * N_STEPS + 2
        assert 2 * (TABLE_SLAB + 4) <= TAIL and TABLE_SLAB % GROUP == 0
        s = by4(4, 4)

        def select(dve, t, step):
            def each_row(n, op):
                for i in range(n):
                    o = op(i)
                dve_chain.step(dve, o)

            wide = lambda v: v.rearrange("p h (k a) -> p h k a", k=PTOP)
            if step == 0:
                dve.wait_ge(R_["scored"], t + 1)
                each_row(NHALF, lambda i: dve.max(vals[:, i, 0:8], s[:, i, :]))
            elif step == 1:
                each_row(NHALF, lambda i: dve.max_index(idx_u[:, i, 0:8], vals[:, i, 0:8], s[:, i, :]))
            elif step == 2:
                each_row(NHALF, lambda i: dve.match_replace(work[:, i, :], vals[:, i, 0:8], s[:, i, :], LOWEST))
                dve.sem_inc(R_["scores_read"], 1)
            elif step == 3:
                each_row(NHALF, lambda i: dve.max(vals[:, i, 8:16], work[:, i, :]))
            elif step == 4:
                each_row(NHALF, lambda i: dve.max_index(idx_u[:, i, 8:16], vals[:, i, 8:16], work[:, i, :]))
            elif step == 5:
                dve.tensor_copy(idx_f, idx_u)
                dve_chain.step(dve, dve.tensor_tensor(
                    cand.rearrange("p h (a b) -> p h a b", a=PTOP),
                    vals[:, 0:PH, :].unsqueeze(3).to_broadcast([P, PH, PTOP, PTOP]),
                    vals[:, PH:NHALF, :].unsqueeze(2).to_broadcast([P, PH, PTOP, PTOP]), ALU.add))
            elif step == 6:
                each_row(PH, lambda h: dve.max(ts_[:, h, 0:8], cand[:, h, :]))
            elif step == 7:
                each_row(PH, lambda h: dve.max_index(tpos[:, h, 0:8], ts_[:, h, 0:8], cand[:, h, :]))
            elif step == 8:
                each_row(PH, lambda h: dve.match_replace(cwork[:, h, :], ts_[:, h, 0:8], cand[:, h, :], LOWEST))
            elif step == 9:
                each_row(PH, lambda h: dve.max(ts_[:, h, 8:16], cwork[:, h, :]))
            elif step == 10:
                each_row(PH, lambda h: dve.max_index(tpos[:, h, 8:16], ts_[:, h, 8:16], cwork[:, h, :]))
            elif step == EXP_STEP:
                dve_chain.step(dve, dve.tensor_copy(zsum, ts_[:, :, 0:1]))
                dve.tensor_tensor(ts_, ts_, zsum.to_broadcast([P, PH, PTOP]),
                                  ALU.subtract).then_inc(R_["exp_in"], 1)
                dve.tensor_single_scalar(ab_u[:, 0, :, :], tpos, 4, ALU.logical_shift_right)
                dve_chain.step(dve, dve.tensor_single_scalar(ab_u[:, 1, :, :], tpos, 15, ALU.bitwise_and))
                dve_chain.step(dve, dve.tensor_copy(ab_f, ab_u))
            elif step in (12, 14):
                c, eq = (0, cand) if step == 12 else (1, cwork)
                dve_chain.step(dve, dve.tensor_tensor(
                    wide(eq), ab_f[:, c, :, :].unsqueeze(3).to_broadcast([P, PH, PTOP, PTOP]),
                    iota_e[:, 0:PTOP].unsqueeze(1).unsqueeze(1).to_broadcast([P, PH, PTOP, PTOP]),
                    ALU.is_equal))
            elif step in (13, 15):
                c, eq = (0, cand) if step == 13 else (1, cwork)
                dve_chain.step(dve, dve.tensor_tensor(
                    wide(eq), wide(eq),
                    idx_f[:, c * PH:(c + 1) * PH, :].unsqueeze(2).to_broadcast([P, PH, PTOP, PTOP]), ALU.mult))
                dve_chain.step(dve, dve.tensor_reduce(
                    tables[:, c, t, :], eq.rearrange("p h (k a) -> p (h k) a", k=PTOP), AX.X, ALU.add))
            else:
                dve.wait_ge(R_["exp_out"], t + 1)
                dve_chain.step(dve, dve.tensor_reduce(zsum, ts_, AX.X, ALU.add))
                dve_chain.step(dve, dve.reciprocal(zsum, zsum))
                dve.tensor_tensor(tables[:, 2, t, :].rearrange("p (h k) -> p h k", k=PTOP), ts_,
                                  zsum.to_broadcast([P, PH, PTOP]), ALU.mult).then_inc(R_["table_ready"], 1)

        with nc.Block(no_gpsimd_drain=True) as block:
            @block.sync
            def _(sp):
                feed(sp, s_down + N_DOWN)

            @block.tensor
            def _(pe):
                def scores(t):
                    for half_ in range(2):
                        r = slice(half_ * 64, (half_ + 1) * 64)
                        for h in range(PH):
                            mm = pe.matmul(s[:, half_ * PH + h, :], pqT[r, h, t * P:(t + 1) * P],
                                           subk[r, h, :], start=True, stop=True)
                    mm.then_inc(R_["scored"], 1)

                scores(0)
                project(pe, s_down, SCORE_SLAB, turned_slab, src_in)
                pe.wait_ge(R_["scores_read"], 1)
                scores(1)
                project(pe, s_down + SCORE_SLAB, TABLE_SLAB - SCORE_SLAB, turned_slab, src_in, before=SCORE_SLAB)
                pe.wait_ge(R_["table_ready"], NT)
                for c in range(3):
                    for t in range(NT):
                        mm = pe.transpose(psum[:, 4 + c, t * P:(t + 1) * P], tables[:, c, t, :], ident[:, :])
                mm.then_inc(R_["turned"], 1)
                project(pe, s_down + TABLE_SLAB, N_DOWN - TABLE_SLAB, turned_slab, src_in, before=TABLE_SLAB)
                pe.wait_ge(R_["room_left"], 1)
                for n in range(NT):
                    for c in range(2):
                        pe.matmul(psum[:, 4 + 2 * n + c, :], ident[:, :], x[:, n, c * 512:(c + 1) * 512],
                                  start=True, stop=False)

            @block.scalar
            def _(act):
                def body(s, it):
                    act.wait_ge(slab_used, at(it, s + 1))
                    act.activation(HID[:, bass.ds(at(it, 2 * (s - s_down), 2 * GROUP), 2), :]
                                   .rearrange("p i t -> p (i t)"),
                                   psum[:, s % BANKS, :], ACT.Gelu_apprx_tanh).then_inc(bank_read, 1)
                    split_hi(act, s + RING, it)

                for i in range(TAIL // 2):
                    body(s_down + i, None)
                    if i < NT * N_STEPS and i % N_STEPS == EXP_STEP:
                        act.wait_ge(R_["exp_in"], i // N_STEPS + 1)
                        act.activation(ts_, ts_, ACT.Exp).then_inc(R_["exp_out"], 1)
                act.wait_ge(R_["room_left"], 1)
                with act.Fori(TAIL // 2 // GROUP, N_DOWN // GROUP) as it:
                    for j in range(GROUP):
                        body(s_down + j, it)

            @block.vector
            def _(dve):
                dve.wait_ge(R_["iota_ready"], 1)
                for i in range(TABLE_SLAB + 2):
                    split_lo(dve, s_down + i + RING)
                    if i < NT * N_STEPS:
                        select(dve, i // N_STEPS, i % N_STEPS)
                dve.wait_ge(R_["turned"], 1)
                for c, dst in enumerate((IT, JT, GT)):
                    o = dve.tensor_copy(dst[:, :], psum[:, 4 + c, 0:T])
                o.then_inc(R_["room_left"], 1)
                per_slab(dve, s_down + TABLE_SLAB + 2, N_DOWN - TABLE_SLAB - 2,
                         lambda s, it: split_lo(dve, s + RING, it))
        end_slabs(N_DOWN)

        QT = 2
        NBUF = 4
        NSTEP = T // QT
        hot = x[:, :, :].rearrange("p n d -> p (n d)").rearrange("p (q s k c) -> p q s k c", q=NBUF, s=2, k=QT)
        with nc.Block(no_gpsimd_drain=True) as block:
            step_of = lambda it, c: c if it is None else it * NBUF + c

            def steps(eng, body):
                for q in range(NBUF):
                    body(q, None)
                with eng.Fori(1, NSTEP // NBUF) as it:
                    for q in range(NBUF):
                        body(q, it)

            pair = lambda v, q, it: v[:, bass.ds(step_of(it, q) * QT, QT)].unsqueeze(2).to_broadcast([P, QT, P])

            by_scalar = lambda it, c: c if it is None else it * (NBUF - 1) + c

            @block.scalar
            def _(act):
                def body(q, it):
                    if q == NBUF - 1:
                        return
                    if it is not None:
                        act.wait_ge(R_["g_done"], step_of(it, q - NBUF + 1))
                    v = hot[:, q, 0, :, :]
                    for k in range(QT):
                        o = act.activation(v[:, k, :], iota_e[:, :], ACT.Abs, scale=-1.0,
                                           bias=JT[:, bass.ds(step_of(it, q) * QT + k, 1)])
                    o.then_inc(R_["j_near"], 1)
                    act.wait_ge(R_["j_near"], by_scalar(it, q + 1))
                    act.activation(v, v, ACT.Relu, scale=-1.0, bias=1.0).then_inc(R_["j_ready"], 1)
                steps(act, body)

            @block.gpsimd
            def _(pool):
                def body(q, it):
                    pool.wait_ge(R_["i_ready"], step_of(it, q + 1))
                    v = hot[:, q, 1, :, :]
                    pool.tensor_tensor(v, v, pair(GT, q, it), ALU.mult).then_inc(R_["gi_ready"], 1)
                steps(pool, body)
                pool.wait_ge(R_["gi_ready"], NSTEP)

            @block.tensor
            def _(pe):
                def body(q, it):
                    if q < NBUF - 1:
                        pe.wait_ge(R_["j_ready"], by_scalar(it, q + 1))
                    pe.wait_ge(R_["gi_ready"], step_of(it, q + 1))
                    if it is not None:
                        pe.wait_ge(R_["g_used"], step_of(it, q - NBUF + 1))
                    for k in range(QT):
                        mm = pe.matmul(psum[:, q, k * P:(k + 1) * P], hot[:, q, 0, k, :], hot[:, q, 1, k, :],
                                       start=True, stop=True)
                    mm.then_inc(R_["g_done"], 1)
                steps(pe, body)

            @block.vector
            def _(dve):
                def gated(q, step):
                    dve.wait_ge(R_["g_done"], step + 1)
                    v = HID[:, :, bass.ds(step * QT, QT)].rearrange("p i k -> p k i")
                    dve.tensor_tensor(v, v, psum[:, q, 0:QT * P].rearrange("p (k i) -> p k i", k=QT),
                                      ALU.mult).then_inc(R_["g_used"], 1)

                def one_hot(q, it):
                    if q == NBUF - 1:
                        dve.tensor_tensor(hot[:, q, 0, :, :], iota_e[:, :].unsqueeze(1).to_broadcast([P, QT, P]),
                                          pair(JT, q, it), ALU.is_equal)
                    dve.tensor_tensor(hot[:, q, 1, :, :], iota_e[:, :].unsqueeze(1).to_broadcast([P, QT, P]),
                                      pair(IT, q, it), ALU.is_equal).then_inc(R_["i_ready"], 1)

                for q in range(NBUF):
                    one_hot(q, None)
                with dve.Fori(1, NSTEP // NBUF) as it:
                    for q in range(NBUF):
                        gated(q, it * NBUF + (q - NBUF))
                        one_hot(q, it)
                for q in range(NBUF):
                    gated(q, NSTEP - NBUF + q)
        gbx.close()

        wgtH = sb("wgtH", [P, 2, T], F32R, ctx=pr)
        wgtL = sb("wgtL", [P, 2, T], F32R, ctx=pr)
        fin_gain = x[:, 0, :]
        with nc.Block(no_gpsimd_drain=True) as block:
            def up_slabs(eng, body):
                for j in range(GROUP):
                    body(s_up + j, None)
                with eng.Fori(1, N_UP // GROUP - 1) as it:
                    for j in range(GROUP):
                        body(s_up + j, it)
                for j in range(N_UP - GROUP, N_UP):
                    body(s_up + j, None)

            @block.sync
            def _(sp):
                sp.dma_start(fin_gain, ins["norm_final"].partition_broadcast(P)).then_inc(R_["loads"], 16)
                feed(sp, N_SLABS)
                sp.wait_ge(R_["loads"], 32)

            @block.tensor
            def _(pe):
                def body(s, it):
                    w = weights_of(s % RING, 2)
                    for a in range(2):
                        if a == 0:
                            if it is not None or s >= s_up + RING:
                                pe.wait_ge(R_["up_ready"], at(it, s - s_up - RING + 1))
                        else:
                            pe.wait_ge(split_ready, at(it, s + 1))
                        pe.wait_ge(R_["tile_ready"], at(it, 2 * (s - s_up) + a + 1, 2 * GROUP))
                        last = s == N_SLABS - 1 and a == 1
                        for n in range(NT):
                            for c in range(2):
                                mm = three(pe, psum[:, 4 + 2 * n + c, :],
                                           [v[:, a, n * P:(n + 1) * P] for v in (wgtH, wgtL)],
                                           [v[:, a, c * 512:(c + 1) * 512] for v in w], False, last)
                        mm.then_inc((R_["half_used"], slab_used)[a], 1)
                up_slabs(pe, body)

            half = lambda t, slot, a: t[:, slot, a * D:(a + 1) * D]

            @block.scalar
            def _(act):
                def tile_hi(i, a):
                    act.activation(wgtH[:, a, :], HID[:, bass.ds(i, 1), :].rearrange("p i t -> p (i t)"),
                                   ACT.Copy).then_inc(R_["tile_hi"], 1)

                def body(s, it):
                    slot = s % RING
                    for a in range(2):
                        act.wait_ge(*((R_["half_used"], at(it, s - s_up + 1)), (slab_used, at(it, s + 1)))[a])
                        if s + 1 < N_SLABS:
                            tile_hi(at(it, 2 * (s + 1 - s_up) + a, 2 * GROUP), a)
                        if s + RING < N_SLABS:
                            if a == 0:
                                act.wait_ge(slab_landed[slot], at(it, 16 * ((s + RING) // RING + 1), 16 * GROUP // RING))
                            act.activation(half(wH, slot, a), half(ring, slot, a),
                                           ACT.Copy).then_inc((R_["up_hi"], hi_ready)[a], 1)

                for a in range(2):
                    tile_hi(a, a)
                up_slabs(act, body)

            @block.vector
            def _(dve):
                def tile_lo(i, a):
                    dve.wait_ge(R_["tile_hi"], i + 1)
                    dve.tensor_tensor(wgtL[:, a, :], HID[:, bass.ds(i, 1), :].rearrange("p i t -> p (i t)"),
                                      wgtH[:, a, :].bitcast(F32), ALU.subtract).then_inc(R_["tile_ready"], 1)

                def body(s, it):
                    slot = s % RING
                    for a in range(2):
                        if s + 1 < N_SLABS:
                            tile_lo(at(it, 2 * (s + 1 - s_up) + a, 2 * GROUP), a)
                        if s + RING < N_SLABS:
                            dve.wait_ge(*((R_["up_hi"], at(it, s - s_up + 1)), (hi_ready, at(it, s + RING + 1)))[a])
                            dve.tensor_tensor(half(wL, slot, a), half(ring, slot, a), half(wH, slot, a).bitcast(F32),
                                              ALU.subtract).then_inc((R_["up_ready"], split_ready)[a], 1)

                for a in range(2):
                    tile_lo(a, a)
                up_slabs(dve, body)

        fin_sq, fin_ready, out_stored = sem("final_squares"), sem("final_ready"), sem("out_stored")
        total = psum[:, 4:8, :].rearrange("p (n b) c -> p n (b c)", n=NT)
        result = HID[:, 0:NT * D // T, :].rearrange("p (n i) t -> p n (i t)", n=NT)
        squares = HID[:, NT * D // T:2 * NT * D // T, :].rearrange("p (n i) t -> p n (i t)", n=NT)
        with nc.Block(no_gpsimd_drain=True) as block:
            @block.scalar
            def _(act):
                for t in range(NT):
                    act.activation(squares[:, t, :], total[:, t, :], ACT.Square, scale=D ** -0.5,
                                   accum_out=mean_sq[:, t:t + 1]).then_inc(fin_sq, 1)

            @block.gpsimd
            def _(pool):
                pool.wait_ge(fin_sq, NT)
                inv_sqrt(pool, rstd[:, 0:NT], mean_sq[:, 0:NT])

            @block.vector
            def _(dve):
                dve.wait_ge(rstd_ready, rstds["n"])
                for t in range(NT):
                    dve.scalar_tensor_tensor(out=result[:, t, :], in0=total[:, t, :], scalar=rstd[:, t:t + 1],
                                             in1=fin_gain, op0=ALU.mult, op1=ALU.mult).then_inc(fin_ready, 1)

            @block.sync
            def _(sp):
                for t in range(NT):
                    sp.wait_ge(fin_ready, t + 1)
                    sp.dma_start(out[0, t * P:(t + 1) * P, :], result[:, t, :]).then_inc(out_stored, 16)
                sp.wait_ge(out_stored, 16 * NT)
        pr.close()



def lay_out(inputs):
    a = {k: np.asarray(v) for k, v in inputs.items()}

    def cols(w, order=None):
        w = w.reshape(KD, P, -1, 256)
        return w.transpose(2, 1, 0, 3).reshape(-1, P, SLAB)

    def vec(v):
        return v.reshape(KD, P).T

    w_in = a["w_in"][0]
    sec = lambda *n: np.concatenate([w_in[:, D * i:D * (i + 1)] for i in n], axis=1)
    parts = [cols(sec(0, 1, 3, 7, 8)), cols(sec(4, 5, 2, 6)),
             cols(a["w_hg_out"][0]), cols(a["w_sb_out"][0]), cols(a["w_o"][0])]
    fi = a["w_ffn_in"][0].reshape(KD, P, 2, FT, P)
    parts.append(fi.transpose(3, 1, 0, 2, 4).reshape(FT, P, SLAB))
    fo = a["w_ffn_out"][0].reshape(FT // 2, 2, P, D)
    parts.append(fo.transpose(0, 2, 1, 3).reshape(FT // 2, P, SLAB))
    w2 = a["w_in_2"][0]
    o = np.cumsum([0, 256, 256, 512, 512, 16, 512, 128, 128, 128, 128, 128, 128, 24])
    gq, gk, gv, gr, glr, nq, kc, vc, ks, vs, kw, vw, ng = (w2[:, o[i]:o[i + 1]] for i in range(13))
    pad = np.zeros((D, 256 - 40), np.float32)
    parts.append(cols(np.concatenate([gq, gk, gr, nq, kc, vc, ks, kw, gv, vs, vw, glr, ng, pad], axis=1)))
    for n in ("w_out_2", "xa_wk_2", "xa_wv_2", "xa_wq_2", "xa_wo_2", "peer_wq_2"):
        parts.append(cols(a[n][0]))
    parts.append(cols(a["peer_down_2"][0].T))
    up = a["peer_up_2"][0].reshape(PK // 2, 2, P, D)
    parts.append(up.transpose(0, 2, 1, 3).reshape(PK // 2, P, SLAB))
    w_stream = np.concatenate(parts, axis=0)
    assert w_stream.shape == (N_SLABS, P, SLAB)

    gains = np.stack([vec(a["norm1_gain"][0]), vec(a["norm2_gain"][0]), vec(a["norm_mix_2"][0]),
                      vec(a["norm_xattn_2"][0]), vec(a["norm_mem_2"][0]), vec(a["norm_ffn_2"][0]),
                      vec(a["sb_q_norm"][0]), vec(a["sb_k_norm"][0]), vec(a["hg_out_norm"][0])], axis=1)
    lb_logits = a["lb_logits"].reshape(2, KD, P).transpose(2, 0, 1)

    paired = lambda v: v.reshape(CB // 2, 2 * ND, -1).transpose(1, 0, 2)
    cmp_w1 = np.stack([paired(a["cmp_k_w1_2"][0]), paired(a["cmp_v_w1_2"][0])], axis=1)
    cmp_pos = np.stack([paired(a["cmp_pos_k_2"][0])[:, :, 0], paired(a["cmp_pos_v_2"][0])[:, :, 0]], axis=1)
    gla_vec = np.concatenate([a["gla_gate_b_2"][0].reshape(2, P).T, a["gla_out_norm_2"][0].reshape(P, 1)], axis=1)
    return {
        "x": a["x"], "w_stream": w_stream, "gains": gains, "lb_logits": lb_logits,
        "cmp_w1": cmp_w1, "cmp_pos": cmp_pos, "cmp_k_w2": a["cmp_k_w2_2"][0], "cmp_v_w2": a["cmp_v_w2_2"][0],
        "rel_bias": a["rel_bias_2"], "buckets": bucket_rows(), "gla_w2": a["gla_gate_w2_2"][0], "gla_vec": gla_vec,
        "mem": a["mem_2"], "norm_final": a["norm_final_2"],
        "subkeys": a["peer_subkeys_2"][0].transpose(1, 3, 0, 2).reshape(P, PH, PK),
    }


def bucket_rows():
    n = np.arange(T)
    exact = BUCKETS // 2
    log_ratio = np.log(np.maximum(n, 1).astype(np.float32) / np.float32(exact)) / np.float32(
        np.log(MAX_DIST / exact))
    large = np.minimum(exact + (log_ratio * (BUCKETS - exact)).astype(np.int32), BUCKETS - 1)
    bucket = np.where(n < exact, n, large)
    up = np.zeros((BUCKETS + 1, 2 * T - 1), np.float32)
    up[BUCKETS, :T - 1] = 1
    up[bucket, T - 1 + n] = 1
    return np.stack([up, up[:, ::-1]], axis=1)


_OUT = (1, T, D)


def kernel(**inputs):
    import concourse.bacc as _bacc
    from concourse.bass_utils import run_bass_kernel_spmd as _run

    nc = _bacc.Bacc("TRN2", target_bir_lowering=False, num_devices=1)
    arrays, args = {}, {}
    for name, v in lay_out(inputs).items():
        v = np.ascontiguousarray(v)
        arrays[f"in_{name}"] = v
        args[name] = nc.dram_tensor(f"in_{name}", v.shape, mybir.dt.from_np(v.dtype), kind="ExternalInput").ap()
    out = nc.dram_tensor("out_0", _OUT, F32, kind="ExternalOutput").ap()
    build(nc, args, out)
    r = _run(nc, [arrays], core_ids=[0])
    return r.results[0]["out_0"]
```

```python
from contextlib import ExitStack

import concourse.bass as bass
import numpy as np
from concourse import mybir

F32 = mybir.dt.float32
F32R = mybir.dt.float32r
U32 = mybir.dt.uint32
ALU = mybir.AluOpType
ACT = mybir.ActivationFunctionType
AX = mybir.AxisListType

P = 128
T = 256
NT = T // P
D = 1024
KD = D // P
EPS = 1e-6
RING = 2
BANKS = 4
GROUP = 4
SLAB = 2048
FF = 2816
FT = FF // P
MASKED = -1e30
EXPO_CAP = 80.0

HH, HD, HCHUNK = 8, 128, 64
SH, SD = 16, 64
GH, GD, GV, GRANK, GTAU = 4, 64, 128, 16, 16.0
NH, NG, ND = 8, 2, 64
CB, CS = 32, 16
NCMP = (T - CB) // CS + 1
BUCKETS, MAX_DIST = 32, 2048
XH, XD = 4, 256
PH, PK, PTOP = 8, 128, 16

N_WIN_TURNED, N_WIN_NATURAL = 20, 16
N_FFN_IN, N_FFN_OUT = FT, FT // 2
STREAM = [("win_turned", 20), ("win_natural", 16), ("hg_out", 4), ("sb_out", 4), ("w_o", 4),
          ("ffn_in", FT), ("ffn_out", FT // 2),
          ("win2_turned", 8), ("win2_natural", 3), ("win2_small", 1), ("xa_wk", 4), ("xa_wv", 4),
          ("w_out", 4), ("xa_wq", 4), ("xa_wo", 4), ("peer_wq", 4),
          ("peer_down", PK // 2), ("peer_up", PK // 2)]
FIRST_SLAB = {}
_at = 0
for _name, _n in STREAM:
    FIRST_SLAB[_name] = _at
    _at += _n
N_SLABS = _at


def build(nc, ins, out):
    top = ExitStack()
    with top:
        def sb(name, shape, dt=F32, ctx=top):
            return ctx.enter_context(nc.sbuf_tensor(name, shape, dt))

        def sem(name):
            return top.enter_context(nc.semaphore(name))

        psum = top.enter_context(nc.psum_tensor("psum", [P, 8, 512], F32))

        ring = sb("ring", [P, RING, SLAB])
        wH = sb("wH", [P, RING, SLAB], F32R)
        wL = sb("wL", [P, RING, SLAB], F32R)
        x = sb("x", [P, NT, D])
        inH = sb("inH", [P, KD, T], F32R)
        inL = sb("inL", [P, KD, T], F32R)
        src_in = (inH, inL)
        ident = sb("ident", [P, P])
        causal = sb("causal", [P, P])
        mean_sq = sb("mean_sq", [P, 4])
        rstd = sb("rstd", [P, 4])
        gains = sb("gains", [P, 9, KD])
        minus_half = sb("minus_half", [P, 32])

        slab_landed = [sem(f"slab_landed{i}") for i in range(RING)]
        hi_ready = sem("hi_ready")
        split_ready = sem("split_ready")
        slab_used = sem("slab_used")
        bank_read = sem("bank_read")
        w_stream = ins["w_stream"]
        state = {"fed": 0, "banks": 0}

        def at(it, c, k=GROUP):
            return c if it is None else it * k + c

        def feed(sp, end):
            upto = min(N_SLABS, (end + 1 + RING) // RING * RING)
            first_, state["fed"] = state["fed"], max(upto, state["fed"])

            def one(s, it=None):
                if it is not None or s >= RING:
                    sp.wait_ge(split_ready, at(it, s - RING + 1, RING))
                src = w_stream[s, :, :] if it is None else w_stream[bass.ds(at(it, s, RING), 1), :, :] \
                    .rearrange("a p n -> p (a n)")
                sp.dma_start(ring[:, s % RING, :], src).then_inc(slab_landed[s % RING], 16)

            g0, g1 = -(-first_ // RING), upto // RING
            if first_ == 0:
                for s in range(RING):
                    one(s)
                g0 = 1
            if g1 > g0:
                with sp.Fori(g0, g1) as it:
                    for j in range(RING):
                        one(j, it)
            for s in range(max(g1 * RING, first_), upto):
                one(s)

        def split_hi(act, s, it=None):
            if it is None and s >= N_SLABS:
                return
            slot = s % RING
            act.wait_ge(slab_landed[slot], at(it, 16 * (s // RING + 1), 16 * GROUP // RING))
            if it is not None or s >= RING:
                act.wait_ge(slab_used, at(it, s - RING + 1))
            act.activation(wH[:, slot, :], ring[:, slot, :], ACT.Copy).then_inc(hi_ready, 1)

        def split_lo(dve, s, it=None):
            if it is None and s >= N_SLABS:
                return
            slot = s % RING
            dve.wait_ge(hi_ready, at(it, s + 1))
            dve.tensor_tensor(wL[:, slot, :], ring[:, slot, :], wH[:, slot, :].bitcast(F32),
                              ALU.subtract).then_inc(split_ready, 1)

        def per_slab(eng, s0, n, body, peel=0):
            rounds = n // GROUP
            if rounds - peel < 2:
                peel = rounds
            for j in range(peel * GROUP):
                body(s0 + j, None)
            if rounds > peel:
                with eng.Fori(peel, rounds) as it:
                    for j in range(GROUP):
                        body(s0 + j, it)
            for j in range(rounds * GROUP, n):
                body(s0 + j, None)

        def three(pe, out_, lhs, rhs, start, stop):
            pe.matmul(out_, lhs[0], rhs[0], start=start, stop=False)
            pe.matmul(out_, lhs[0], rhs[1], start=False, stop=False)
            return pe.matmul(out_, lhs[1], rhs[0], start=False, stop=stop)

        def weights_of(slot, k):
            return [w[:, slot, :].rearrange("p (k c) -> p k c", k=k) for w in (wH, wL)]

        def turned_slab(pe, slot, bank, src):
            w = weights_of(slot, KD)
            for c in range(2):
                for k in range(KD):
                    mm = three(pe, psum[:, bank, c * T:(c + 1) * T], [v[:, k, c * P:(c + 1) * P] for v in w],
                               [v[:, k, :] for v in src], k == 0, k == KD - 1)
            return mm

        def natural_slab(pe, slot, bank, src):
            w = weights_of(slot, KD)
            for n in range(NT):
                for k in range(KD):
                    mm = three(pe, psum[:, bank, n * 256:(n + 1) * 256], [v[:, k, n * P:(n + 1) * P] for v in src],
                               [v[:, k, :] for v in w], k == 0, k == KD - 1)
            return mm

        def project(pe, s0, n, one_slab, src, before=0, banks=BANKS):
            base = state["banks"] + before - banks + 1

            def body(s, it):
                pe.wait_ge(split_ready, at(it, s + 1))
                if it is not None or before + s - s0 >= banks:
                    pe.wait_ge(bank_read, at(it, base + s - s0))
                one_slab(pe, s % RING, s % banks, src).then_inc(slab_used, 1)

            per_slab(pe, s0, n, body, peel=0 if before >= banks else 1)

        def end_slabs(n):
            state["banks"] += n

        class Chain:

            def __init__(self, name):
                self.sem, self.n = sem(name), 0

            def step(self, eng, ins_):
                self.n += 1
                ins_.then_inc(self.sem, 1)
                eng.wait_ge(self.sem, self.n)

        dve_chain, act_chain, pool_chain = Chain("dve_step"), Chain("act_step"), Chain("pool_step")

        dma_in = sem("dma_in")

        norm_ready, norm_scaled, norm_turned, norm_hi = (
            sem(n) for n in ("norm_ready", "norm_scaled", "norm_turned", "norm_hi"))
        norms = {"n": 0}
        rstd_ready = sem("rstd_ready")
        rstds = {"n": 0}

        def inv_sqrt(pool, dst, src):
            pool_chain.step(pool, pool.tensor_scalar(dst, src, EPS, None, ALU.add))
            rstds["n"] += 1
            pool.tensor_tensor(dst, dst, minus_half[:, 0:dst.shape[1]], ALU.pow).then_inc(rstd_ready, 1)

        input_rounded = sem("input_rounded")
        splits = {"n": 0}

        class Split:

            def __init__(self, src, dst, tiles=(0, KD)):
                self.src, self.dst, self.at, self.tiles = src, dst, splits["n"], range(*tiles, 2)
                splits["n"] += len(self.tiles)

            def hi(self, act):
                for k in self.tiles:
                    act.activation(self.dst[0][:, k:k + 2, :], self.src[:, k:k + 2, :],
                                   ACT.Copy).then_inc(input_rounded, 1)

            def lo(self, dve):
                for i, k in enumerate(self.tiles):
                    dve.wait_ge(input_rounded, self.at + i + 1)
                    o = dve.tensor_tensor(self.dst[1][:, k:k + 2, :], self.src[:, k:k + 2, :],
                                          self.dst[0][:, k:k + 2, :].bitcast(F32), ALU.subtract)
                return o

        class Norm:

            def __init__(self, src, dst, gain_at, ctx):
                self.n = norms["n"]
                norms["n"] += 1
                self.src, self.dst, self.gain_at = src, dst, gain_at
                self.junk = sb(f"squares{self.n}", [P, D], ctx=ctx)
                self.diag = sb(f"diag{self.n}", [P, NT, P], ctx=ctx)
                self.tile = lambda k: psum[:, k // 2, (k % 2) * T:(k % 2 + 1) * T]

            def square(self, act, t):
                act.activation(self.junk[:, :], self.src[:, t, :], ACT.Square, scale=D ** -0.5,
                               accum_out=mean_sq[:, t:t + 1]).then_inc(norm_ready, 1)
                act.wait_ge(norm_ready, NT * self.n + t + 1)

            def squares(self, act):
                for t in range(NT):
                    self.square(act, t)

            def roots(self, pool):
                pool.wait_ge(norm_ready, NT * (self.n + 1))
                inv_sqrt(pool, rstd[:, 0:NT], mean_sq[:, 0:NT])
                self.root = rstds["n"]

            def diags(self, dve):
                dve.wait_ge(rstd_ready, self.root)
                for t in range(NT):
                    o = dve.tensor_scalar(self.diag[:, t, :], ident[:, :], rstd[:, t:t + 1], None, ALU.mult)
                o.then_inc(norm_scaled, 1)

            def turn(self, pe):
                pe.wait_ge(norm_scaled, self.n + 1)
                for k in range(KD):
                    for t in range(NT):
                        mm = pe.matmul(self.tile(k)[:, t * P:(t + 1) * P], self.src[:, t, k * P:(k + 1) * P],
                                       self.diag[:, t, :], start=True, stop=True)
                    if k % 2 == 1:
                        mm.then_inc(norm_turned, 1)

            def hi(self, act):
                for k in range(KD):
                    act.wait_ge(norm_turned, KD // 2 * self.n + k // 2 + 1)
                    act.activation(self.dst[0][:, k, :], self.tile(k), ACT.Copy,
                                   scale=gains[:, self.gain_at, k:k + 1]).then_inc(norm_hi, 1)

            def lo(self, dve):
                for k in range(KD):
                    dve.wait_ge(norm_hi, KD * self.n + 2 * (k // 2) + 2)
                    dve.scalar_tensor_tensor(out=self.dst[1][:, k, :], in0=self.tile(k),
                                             scalar=gains[:, self.gain_at, k:k + 1],
                                             in1=self.dst[0][:, k, :].bitcast(F32), op0=ALU.mult, op1=ALU.subtract)

        own = ExitStack()
        norm1 = Norm(x, src_in, 0, own)
        with nc.Block(no_gpsimd_drain=True) as block:
            @block.sync
            def _(sp):
                for t in range(NT):
                    sp.dma_start(x[:, t, :], ins["x"][0, t * P:(t + 1) * P, :]).then_inc(dma_in, 16)
                sp.dma_start(gains[:, :, :], ins["gains"]).then_inc(dma_in, 16)
                feed(sp, 0)

            @block.scalar
            def _(act):
                act.wait_ge(dma_in, 16 * 3)
                for t in range(NT):
                    norm1.square(act, t)
                split_hi(act, 0)
                norm1.hi(act)

            @block.gpsimd
            def _(pool):
                pool_chain.step(pool, pool.memset(minus_half[:, :], -0.5))
                pool_chain.step(pool, pool.memset(ident[:, :], 0.0))
                pool_chain.step(pool, pool.affine_select(
                    out=ident[:, :], in_=ident[:, :], compare_op=ALU.not_equal, fill=1.0,
                    base=0, pattern=[[-1, P]], channel_multiplier=1))
                pool_chain.step(pool, pool.memset(causal[:, :], 1.0))
                pool_chain.step(pool, pool.affine_select(
                    out=causal[:, :], in_=causal[:, :], compare_op=ALU.is_ge, fill=0.0,
                    base=0, pattern=[[1, P]], channel_multiplier=-1))
                norm1.roots(pool)

            @block.vector
            def _(dve):
                norm1.diags(dve)
                split_lo(dve, 0)
                norm1.lo(dve)

            @block.tensor
            def _(pe):
                norm1.turn(pe)
        own.close()

        first = ExitStack()
        n_win = N_WIN_TURNED + N_WIN_NATURAL
        proj = sb("proj", [P, n_win, 512], ctx=first)
        SIG_HG, SIG_GA, SIG_GB, QK_AT, V_AT, SV_AT = 8, 12, 16, 20, 28, 32
        QK_ROOT = rstds["n"] + 1

        def copy_out(dst, s0, n):
            def act_step(act):
                per_slab(act, s0, n, lambda s, it: copy_step(act, dst, s0, s, it))
            return act_step, lambda dve: per_slab(dve, s0, n, lambda s, it: split_lo(dve, s + 1, it))

        def copy_step(act, dst, s0, s, it=None, banks=BANKS):
            split_hi(act, s + 1, it)
            only_copy(act, dst, s0, s, it, banks)

        def only_copy(act, dst, s0, s, it=None, banks=BANKS):
            act.wait_ge(slab_used, at(it, s + 1))
            act.activation(dst[:, bass.ds(at(it, s - s0), 1), :].rearrange("p a n -> p (a n)"),
                           psum[:, s % banks, :], ACT.Copy).then_inc(bank_read, 1)

        NCH = HH * T // HCHUNK
        NQK = NT * SH
        ohT = sb("ohT", [P, HH, T], ctx=first)
        qkms = sb("qkms", [P, 2 * NQK], ctx=first)
        half64 = sb("half64", [P, 2 * NQK], ctx=first)
        strict = sb("strict", [P, 3 * P], ctx=first)
        strict_add = sb("strict_add", [P, 3 * P], ctx=first)
        neg_upper = sb("neg_upper", [P, P], ctx=first)
        neg_ones = sb("neg_ones", [P, P], ctx=first)
        hg = ExitStack()
        lbl = sb("lbl", [P, 2, KD], ctx=hg)
        lbw = sb("lbw", [P, 4, KD], ctx=hg)
        oml = sb("oml", [P, KD], ctx=hg)
        LG = sb("LG", [P, HH * T], ctx=hg)
        CUM = sb("CUM", [P, HH * T], ctx=hg)
        E1 = sb("E1", [P, HH * T], ctx=hg)
        dec = sb("dec", [P, 3, NCH], ctx=hg)
        hmask = sb("hmask", [P, P], ctx=hg)
        scT = sb("scT", [P, NT * HH, P], ctx=hg)
        qe = proj[:, 0:4, :].rearrange("p a n -> p (a n)")
        fk = proj[:, 4:8, :].rearrange("p a n -> p (a n)")
        gates = lambda j: proj[:, SIG_HG + 4 * j:SIG_HG + 4 * j + 4, :]
        qk = proj[:, QK_AT:QK_AT + 8, :].rearrange("p a n -> p (a n)").rearrange("p (i d) -> p i d", d=SD)
        qk_part = [slice(i * NQK, (i + 1) * NQK) for i in range(2)]
        qk_sq = scT[:, :, :].rearrange("p i (a d) -> p (i a) d", d=SD)
        chunks = lambda v: v.rearrange("p (c s) -> p c s", s=HCHUNK)
        mid = chunks(CUM[:, :])[:, :, HCHUNK // 2 - 1:HCHUNK // 2]
        last = chunks(CUM[:, :])[:, :, HCHUNK - 1:HCHUNK]
        resets = sb("resets", [P, HH * T], ctx=hg)
        (lb_ready, sig_ready, f_ready, log_ready, mid_ready, d_ready, e_ready, resets_ready, qk_sq_ready,
         qk_ms_ready) = (sem(n) for n in (
             "lb_ready", "sig_ready", "f_ready", "log_ready", "mid_ready", "d_ready", "e_ready", "hg_resets_ready",
             "qk_sq_ready", "qk_ms_ready"))
        with nc.Block(no_gpsimd_drain=True) as block:
            @block.sync
            def _(sp):
                sp.dma_start(lbl[:, :, :], ins["lb_logits"]).then_inc(dma_in, 16)
                feed(sp, n_win)
                sp.wait_ge(dma_in, 48)

            @block.tensor
            def _(pe):
                project(pe, 0, N_WIN_TURNED, turned_slab, src_in)
                project(pe, N_WIN_TURNED, N_WIN_NATURAL, natural_slab, src_in, before=N_WIN_TURNED)

            @block.gpsimd
            def _(pool):
                pool_chain.step(pool, pool.memset(resets[:, :], 1.0))
                pool.memset(chunks(resets[:, :])[:, :, 0:1], 0.0).then_inc(resets_ready, 1)
                pool_chain.step(pool, pool.memset(half64[:, :], -0.5))
                pool_chain.step(pool, pool.tensor_copy(hmask[:, :], causal[:, :]))
                pool_chain.step(pool, pool.memset(hmask[0:HCHUNK, HCHUNK:P], 0.0))
                pool_chain.step(pool, pool.memset(strict[:, :], 1.0))
                pool_chain.step(pool, pool.memset(neg_upper[:, :], -1.0))
                pool_chain.step(pool, pool.memset(neg_ones[:, :], -1.0))
                for m in (strict[:, 0:P], strict[:, 2 * P:3 * P]):
                    pool_chain.step(pool, pool.affine_select(
                        out=m, in_=m, compare_op=ALU.is_gt, fill=0.0, base=0, pattern=[[1, P]],
                        channel_multiplier=-1))
                pool_chain.step(pool, pool.affine_select(
                    out=neg_upper[:, :], in_=neg_upper[:, :], compare_op=ALU.is_ge, fill=0.0, base=0,
                    pattern=[[-1, P]], channel_multiplier=1))
                pool_chain.step(pool, pool.tensor_scalar(strict_add[:, :], strict[:, :], 1.0, -MASKED,
                                                         ALU.subtract, ALU.mult))
                pool.wait_ge(qk_ms_ready, 2)
                pool_chain.step(pool, pool.tensor_scalar(qkms[:, :], qkms[:, :], EPS, None, ALU.add))
                rstds["n"] += 1
                pool.tensor_tensor(qkms[:, :], qkms[:, :], half64[:, :], ALU.pow).then_inc(rstd_ready, 1)
                pool_chain.step(pool, pool.memset(scT[:, :, :], 0.0))

            @block.scalar
            def _(act):
                act_step, _ = copy_out(proj, 0, N_WIN_TURNED)
                act_step(act)
                for s in range(N_WIN_TURNED, n_win):
                    split_hi(act, s + 1)
                    step = s - N_WIN_TURNED
                    if step == 0:
                        act.activation(fk, fk, ACT.Sigmoid).then_inc(sig_ready, 1)
                    elif step == 1:
                        act.wait_ge(lb_ready, 1)
                        act.activation(lbw[:, 1:3, :], lbw[:, 1:3, :], ACT.Exp).then_inc(lb_ready, 1)
                    elif step == 3:
                        act.wait_ge(f_ready, 1)
                        act.activation(LG[:, :], fk, ACT.Ln).then_inc(log_ready, 1)
                    elif step in (2, 5, 8):
                        g = gates((2, 5, 8).index(step))
                        act.activation(g, g, ACT.Sigmoid)
                    elif step == 6:
                        act.wait_ge(mid_ready, 1)
                        act.activation(dec[:, :, :], dec[:, :, :], ACT.Exp)
                    elif step in (7, 9):
                        i = (7, 9).index(step)
                        if i == 1:
                            act.wait_ge(qk_ms_ready, 1)
                        act.activation(qk_sq, qk[:, qk_part[i], :], ACT.Square, scale=SD ** -0.5)\
                           .then_inc(qk_sq_ready, 1)
                    elif step == 10:
                        act.wait_ge(d_ready, 1)
                        act.activation(E1[:, :], LG[:, :], ACT.Exp).then_inc(e_ready, 1)
                    elif step == 11:
                        act.activation(CUM[:, :], LG[:, :], ACT.Exp, scale=-1.0).then_inc(e_ready, 1)
                    only_copy(act, proj, 0, s)

            @block.vector
            def _(dve):
                per_slab(dve, 0, N_WIN_TURNED, lambda s, it: split_lo(dve, s + 1, it))
                for s in range(N_WIN_TURNED, n_win):
                    split_lo(dve, s + 1)
                    step = s - N_WIN_TURNED
                    if step == 0:
                        dve.wait_ge(dma_in, 48)
                        dve_chain.step(dve, dve.tensor_tensor(lbw[:, 0, :], lbl[:, 0, :], lbl[:, 1, :], ALU.max))
                        dve.tensor_tensor(lbw[:, 1:3, :], lbl[:, :, :],
                                          lbw[:, 0:1, :].to_broadcast([P, 2, KD]), ALU.subtract).then_inc(lb_ready, 1)
                    elif step == 1:
                        dve.wait_ge(lb_ready, 2)
                        dve_chain.step(dve, dve.tensor_tensor(lbw[:, 0, :], lbw[:, 1, :], lbw[:, 2, :], ALU.add))
                        dve_chain.step(dve, dve.reciprocal(lbw[:, 3, :], lbw[:, 0, :]))
                        dve_chain.step(dve, dve.tensor_tensor(oml[:, :], lbw[:, 2, :], lbw[:, 3, :], ALU.mult))
                        dve_chain.step(dve, dve.tensor_tensor(lbw[:, 3, :], lbw[:, 1, :], lbw[:, 3, :], ALU.mult))
                    elif step == 2:
                        dve.wait_ge(sig_ready, 1)
                        for h in range(HH):
                            fh = fk[:, h * T:(h + 1) * T]
                            o = dve.tensor_scalar(fh, fh, oml[:, h:h + 1], lbw[:, 3, h:h + 1], ALU.mult, ALU.add)
                        o.then_inc(f_ready, 1)
                    elif step == 4:
                        dve.wait_ge(log_ready, 1)
                        dve_chain.step(dve, dve.tensor_scalar(fk, fk, -1.0, 1.0, ALU.mult, ALU.add))
                    elif step == 5:
                        dve.wait_ge(resets_ready, 1)
                        dve_chain.step(dve, dve.tensor_tensor_scan(CUM[:, :], resets[:, :], LG[:, :], 0.0,
                                                                   ALU.mult, ALU.add))
                    elif step == 6:
                        dve.tensor_copy(dec[:, 0, :].unsqueeze(2), mid)
                        dve.tensor_copy(dec[:, 1, :].unsqueeze(2), last)
                        dve.tensor_tensor(dec[:, 2, :].unsqueeze(2), last, mid, ALU.subtract).then_inc(mid_ready, 1)
                        dve_chain.step(dve, dve.tensor_tensor(chunks(LG[:, :]), chunks(CUM[:, :]),
                                                              mid.to_broadcast([P, NCH, HCHUNK]), ALU.subtract))
                    elif step == 7:
                        dve.tensor_scalar(LG[:, :], LG[:, :], EXPO_CAP, -EXPO_CAP, ALU.min, ALU.max)\
                           .then_inc(d_ready, 1)
                    elif step in (8, 9):
                        i = step - 8
                        dve.wait_ge(qk_sq_ready, i + 1)
                        dve.tensor_reduce(qkms[:, qk_part[i]], qk_sq, AX.X, ALU.add).then_inc(qk_ms_ready, 1)
                    elif step == 10:
                        dve.wait_ge(e_ready, 1)
                        dve.tensor_tensor(qe, qe, E1[:, :], ALU.mult)
                    elif step == 11:
                        dve.wait_ge(e_ready, 2)
                        dve.tensor_tensor(fk, fk, CUM[:, :], ALU.mult)
                    elif step in (12, 13):
                        i = step - 12
                        dve.wait_ge(rstd_ready, QK_ROOT)
                        dve.tensor_tensor(qk[:, qk_part[i], :], qk[:, qk_part[i], :],
                                          qkms[:, qk_part[i]].unsqueeze(2).to_broadcast([P, NQK, SD]), ALU.mult)
        end_slabs(n_win)

        keN = E1[:, :].rearrange("p (i d) -> p i d", d=HD)
        hS = CUM[:, 0:HH * P].rearrange("p (h v) -> p h v", h=HH)
        hSp2 = sb("hSp2", [P, D], ctx=hg)
        hSp = [v.rearrange("p (h v) -> p h v", v=P) for v in
               (resets[:, 0:D], resets[:, D:2 * D], hSp2[:, :])]
        hO = LG[:, :].rearrange("p (i v) -> p i v", v=P)
        hSq = E1[:, :].rearrange("p (i v) -> p i v", v=P)
        hms = sb("hms", [P, NT * HH], ctx=hg)
        V = lambda t, h: proj[:, V_AT + h // 2, t * 256 + (h % 2) * P:t * 256 + (h % 2) * P + P]
        by4 = lambda b, n: psum[:, b:b + n, :].rearrange("p b (j c) -> p (b j) c", c=P)
        ke_turned, sc_done, keN_ready, scT_ready, dS_done, Sp_ready, o_done, o_copied, o_scaled, o_turned = (
            sem(n) for n in ("hg_ke_turned", "hg_scores_done", "hg_keN_ready", "hg_scT_ready", "hg_dS_done",
                             "hg_state_ready", "hg_o_done", "hg_o_copied", "hg_o_scaled", "hg_o_turned"))
        sq_ready, ms_ready = sem("hg_squares_ready"), sem("hg_square_sums_ready")
        with nc.Block(no_gpsimd_drain=True) as block:
            @block.tensor
            def _(pe):
                for t in range(NT):
                    for h in range(HH):
                        i = t * HH + h
                        mm = pe.transpose(by4(0, 4)[:, i, :], fk[:, h * T + t * P:h * T + (t + 1) * P], ident[:, :])
                mm.then_inc(ke_turned, 1)
                for t in range(NT):
                    for h in range(HH):
                        at = slice(h * T + t * P, h * T + (t + 1) * P)
                        mm = pe.matmul(by4(4, 4)[:, t * HH + h, :], fk[:, at], qe[:, at], start=True, stop=True)
                mm.then_inc(sc_done, 1)
                pe.wait_ge(keN_ready, 1)
                for c in range(3):
                    if c == 2:
                        pe.wait_ge(scT_ready, 1)
                    t, b = c // 2, (c % 2) * HCHUNK
                    for h in range(HH):
                        mm = pe.matmul(by4(2 * c, 2)[:, h, :], keN[b:b + HCHUNK, t * HH + h, :],
                                       V(t, h)[b:b + HCHUNK, :], start=True, stop=True)
                    mm.then_inc(dS_done, 1)
                pe.wait_ge(scT_ready, 1)
                for t in range(NT):
                    if t == 0:
                        pe.wait_ge(Sp_ready, 1)
                    else:
                        pe.wait_ge(Sp_ready, 3)
                    for h in range(HH):
                        o = by4(6 if t == 0 else 0, 2)[:, h, :]
                        pe.matmul(o, scT[:, t * HH + h, :], V(t, h), start=True, stop=True)
                        for c in ((1,) if t == 0 else (2, 3)):
                            b = (c % 2) * HCHUNK
                            mm = pe.matmul(o[b:b + HCHUNK, :],
                                           qe[:, h * T + c * HCHUNK:h * T + (c + 1) * HCHUNK],
                                           hSp[c - 1][:, h, :], start=False, stop=True, skip_group_check=True)
                    mm.then_inc(o_done, 1)
                for t in range(NT):
                    pe.wait_ge(o_scaled, t + 1)
                    for h in range(HH):
                        mm = pe.transpose(by4(2, 4)[:, h * 2 + t, :], hO[:, t * HH + h, :], ident[:, :])
                mm.then_inc(o_turned, 1)

            @block.scalar
            def _(act):
                act.wait_ge(ke_turned, 1)
                act.activation(keN, by4(0, 4), ACT.Copy).then_inc(keN_ready, 1)
                for t in range(NT):
                    act.wait_ge(o_done, t + 1)
                    o = by4(6 if t == 0 else 0, 2)
                    act.activation(hSq[:, t * HH:(t + 1) * HH, :], o, ACT.Square,
                                   scale=HD ** -0.5).then_inc(sq_ready, 1)
                    act.activation(hO[:, t * HH:(t + 1) * HH, :], o, ACT.Copy).then_inc(o_copied, 1)

            @block.gpsimd
            def _(pool):
                for t in range(NT):
                    pool.wait_ge(ms_ready, t + 1)
                    inv_sqrt(pool, hms[:, t * HH:(t + 1) * HH], hms[:, t * HH:(t + 1) * HH])

            @block.vector
            def _(dve):
                dve.wait_ge(sc_done, 1)
                dve.copy_predicated(scT[:, :, :], hmask[:, :].bitcast(U32).unsqueeze(1).to_broadcast([P, NT * HH, P]),
                                    by4(4, 4)).then_inc(scT_ready, 1)
                wide = lambda k, c: dec[:, k, :].rearrange("p (h c) -> p h c", c=4)[:, :, c:c + 1] \
                    .to_broadcast([P, HH, P])
                tmp = hSp[2]
                for c in range(3):
                    dve.wait_ge(dS_done, c + 1)
                    if c == 0:
                        dve_chain.step(dve, dve.tensor_tensor(hS, by4(0, 2), wide(2, 0), ALU.mult))
                    else:
                        dve.tensor_tensor(tmp, by4(2 * c, 2), wide(2, c), ALU.mult)
                        dve_chain.step(dve, dve.tensor_tensor(hS, hS, wide(1, c), ALU.mult))
                        dve_chain.step(dve, dve.tensor_tensor(hS, hS, tmp, ALU.add))
                    dve.tensor_tensor(hSp[c], hS, wide(0, c + 1), ALU.mult).then_inc(Sp_ready, 1)
                for t in range(NT):
                    of_t = slice(t * HH, (t + 1) * HH)
                    dve.wait_ge(sq_ready, t + 1)
                    dve.tensor_reduce(hms[:, of_t], hSq[:, of_t, :], AX.X, ALU.add).then_inc(ms_ready, 1)
                    dve.wait_ge(rstd_ready, rstds["n"] - NT + t + 1)
                    dve.wait_ge(o_copied, t + 1)
                    dve.tensor_tensor(hO[:, of_t, :], hO[:, of_t, :],
                                      hms[:, of_t].unsqueeze(2).to_broadcast([P, HH, P]),
                                      ALU.mult).then_inc(o_scaled, 1)
                dve.wait_ge(o_turned, 1)
                for h in range(HH):
                    dve.scalar_tensor_tensor(
                        out=ohT[:, h, :], in0=psum[:, 2 + h // 2, (h % 2) * T:(h % 2 + 1) * T],
                        scalar=gains[:, 8, h:h + 1],
                        in1=proj[:, SIG_HG + h // 2, (h % 2) * T:(h % 2 + 1) * T], op0=ALU.mult, op1=ALU.mult)
        hg.close()

        sbx = ExitStack()
        osT = sb("osT", [P, SH // 2, T], ctx=sbx)
        sbk = ExitStack()
        qT = sb("qT", [P, SH // 2, T], ctx=sbk)
        kT = sb("kT", [P, SH // 2, T], ctx=sbk)
        q_gain = sb("q_gain", [P, KD], ctx=sbk)
        qk_turned = sem("qk_turned")
        split_oh = Split(ohT, src_in)
        with nc.Block(no_gpsimd_drain=True) as block:
            @block.scalar
            def _(act):
                split_oh.hi(act)

            @block.vector
            def _(dve):
                split_oh.lo(dve)
                dve_chain.step(dve, dve.tensor_scalar(q_gain[:, :], gains[:, 6, :], SD ** -0.5, None, ALU.mult))
                for i, (dst, g) in enumerate(((qT, q_gain[:, :]), (kT, gains[:, 7, :]))):
                    dve.wait_ge(qk_turned, i + 1)
                    dve.tensor_tensor(dst[:, :, :], psum[:, 4 * i:4 * i + 4, :].rearrange("p b (j t) -> p (b j) t", t=T),
                                      g.unsqueeze(2).to_broadcast([P, KD, T]), ALU.mult)

            @block.tensor
            def _(pe):
                for i in range(2):
                    for ft in range(KD):
                        for t in range(NT):
                            mm = pe.transpose(
                                psum[:, 4 * i + ft // 2, (ft % 2) * T + t * P:(ft % 2) * T + (t + 1) * P],
                                proj[:, QK_AT + 4 * i + ft // 2, t * 256 + (ft % 2) * P:t * 256 + (ft % 2 + 1) * P],
                                ident[:, :])
                    mm.then_inc(qk_turned, 1)

        sba = ExitStack()
        C3 = 3 * P
        za = sb("za", [P, 2, 4, C3], ctx=sba)
        by_group = lambda v: v.rearrange("p a n -> p (a n)").rearrange("p (g h c) -> p g h c", g=2, h=4)
        sp_m = by_group(proj[:, QK_AT:QK_AT + 6, :])
        wa = by_group(proj[:, 0:6, :])
        z_done, l_ready, spm_ready, r_done, w_ready, a_ready, so_done, so_out = (
            sem(n) for n in ("sb_z_done", "sb_log_ready", "sb_softplus_ready", "sb_logw_done", "sb_logw_ready",
                             "sb_weights_ready", "sb_o_done", "sb_o_out"))
        NGRP = SH // 4
        with nc.Block(no_gpsimd_drain=True) as block:
            @block.tensor
            def _(pe):
                def z(g):
                    if g >= 2:
                        pe.wait_ge(so_out, g - 1)
                    for j in range(4):
                        h = 4 * g + j
                        b, r = 4 * (g % 2) + j, slice((h % 2) * SD, (h % 2 + 1) * SD)
                        pe.matmul(psum[:, b, 0:T], kT[r, h // 2, 0:P], qT[r, h // 2, :], start=True, stop=True)
                        mm = pe.matmul(psum[:, b, T:C3], kT[r, h // 2, P:T], qT[r, h // 2, P:T],
                                       start=False, stop=True, skip_group_check=True)
                    mm.then_inc(z_done, 1)

                def r(g):
                    pe.wait_ge(spm_ready, g + 1)
                    for j in range(4):
                        b, m = 4 * (g % 2) + j, sp_m[:, g % 2, j, :]
                        pe.matmul(psum[:, b, 0:C3], neg_upper[:, :], m, start=False, stop=True,
                                  skip_group_check=True)
                        mm = pe.matmul(psum[:, b, P:T], neg_ones[:, :], m[:, T:C3], start=False, stop=True,
                                       skip_group_check=True)
                    mm.then_inc(r_done, 1)

                def o(g):
                    pe.wait_ge(a_ready, g + 1)
                    for j in range(4):
                        h = 4 * g + j
                        ob = psum[(h % 2) * SD:(h % 2 + 1) * SD, 4 * (g % 2) + j // 2, 0:T]
                        v = lambda kt: proj[:, SV_AT + h // 4, kt * 256 + (h % 4) * SD:kt * 256 + (h % 4 + 1) * SD]
                        pe.matmul(ob, v(0), wa[:, g % 2, j, 0:T], start=True, stop=True)
                        mm = pe.matmul(ob[:, P:T], v(1), wa[:, g % 2, j, T:C3], start=False, stop=True,
                                       skip_group_check=True)
                    mm.then_inc(so_done, 1)

                z(0)
                for g in range(NGRP):
                    if g + 1 < NGRP:
                        z(g + 1)
                    r(g)
                    o(g)

            @block.scalar
            def _(act):
                def logs(g):
                    act.wait_ge(z_done, g + 1)
                    a, zz = za[:, g % 2, :, :], psum[:, 4 * (g % 2):4 * (g % 2) + 4, 0:C3]
                    if g >= 2:
                        act.wait_ge(spm_ready, g - 1)
                    act_chain.step(act, act.activation(a, zz, ACT.Abs))
                    act_chain.step(act, act.activation(a, a, ACT.Exp, scale=-1.0))
                    act.activation(a, a, ACT.Ln, bias=1.0).then_inc(l_ready, 1)

                def weights(g):
                    act.wait_ge(w_ready, g + 1)
                    a = wa[:, g % 2, :, :]
                    act.activation(a, a, ACT.Exp).then_inc(a_ready, 1)
                    act.wait_ge(so_done, g + 1)
                    act.activation(osT[:, 2 * g:2 * g + 2, :], psum[:, 4 * (g % 2):4 * (g % 2) + 2, 0:T],
                                   ACT.Copy).then_inc(so_out, 1)

                logs(0)
                for g in range(NGRP):
                    if g + 1 < NGRP:
                        logs(g + 1)
                    weights(g)

            @block.vector
            def _(dve):
                def soft(g):
                    dve.wait_ge(l_ready, g + 1)
                    m, zz = sp_m[:, g % 2, :, :], psum[:, 4 * (g % 2):4 * (g % 2) + 4, 0:C3]
                    if g >= 2:
                        dve.wait_ge(r_done, g - 1)
                    dve_chain.step(dve, dve.scalar_tensor_tensor(
                        out=m, in0=zz, scalar=0.0, in1=za[:, g % 2, :, :], op0=ALU.max, op1=ALU.add))
                    dve.tensor_tensor(m, m, strict[:, :].unsqueeze(1).to_broadcast([P, 4, C3]),
                                      ALU.mult).then_inc(spm_ready, 1)

                def masked(g):
                    dve.wait_ge(r_done, g + 1)
                    if g >= 2:
                        dve.wait_ge(so_done, g - 1)
                    dve.tensor_tensor(wa[:, g % 2, :, :], psum[:, 4 * (g % 2):4 * (g % 2) + 4, 0:C3],
                                      strict_add[:, :].unsqueeze(1).to_broadcast([P, 4, C3]),
                                      ALU.add).then_inc(w_ready, 1)

                soft(0)
                for g in range(NGRP):
                    masked(g)
                    if g + 1 < NGRP:
                        soft(g + 1)
        sba.close()
        sbk.close()

        mx = ExitStack()
        mix = sb("mix", [P, KD, T], ctx=mx)
        mix_ready, mix_hi = sem("mix_ready"), sem("mix_rounded")
        s_hg, s_sb, s_wo = FIRST_SLAB["hg_out"], FIRST_SLAB["sb_out"], FIRST_SLAB["w_o"]
        flat = lambda t, i: t[:, 2 * i:2 * i + 2, :].rearrange("p a t -> p (a t)")
        nat_cols = lambda t, i: t[:, :, 256 * i:256 * (i + 1)]
        bank_nat = lambda b: psum[:, b, :].rearrange("p (n c) -> p n c", n=NT)
        part = lambda i: proj[:, SIG_GB + i, :]
        src_b = [sb(n, [P, KD, T], F32R, ctx=mx) for n in ("inH2", "inL2")]
        split_os = Split(osT, src_b)
        os_split = sem("sb_output_split")
        with nc.Block(no_gpsimd_drain=True) as block:
            @block.sync
            def _(sp):
                feed(sp, s_wo)

            @block.tensor
            def _(pe):
                project(pe, s_hg, 4, turned_slab, src_in)
                pe.wait_ge(os_split, 1)
                project(pe, s_sb, 4, turned_slab, src_b, before=4)

            @block.scalar
            def _(act):
                for s in range(s_hg, s_wo):
                    split_hi(act, s + 1)
                    if s == s_hg:
                        split_os.hi(act)
                    if s >= s_sb:
                        i = s - s_sb
                        act.wait_ge(mix_ready, i + 1)
                        act.activation(flat(inH, i), flat(mix, i), ACT.Copy).then_inc(mix_hi, 1)

            @block.vector
            def _(dve):
                for i in range(4):
                    split_lo(dve, s_hg + i + 1)
                    if i == 0:
                        split_os.lo(dve).then_inc(os_split, 1)
                    dve.wait_ge(slab_used, s_hg + i + 1)
                    dve.tensor_tensor(flat(mix, i), psum[:, (s_hg + i) % BANKS, :], proj[:, SIG_GA + i, :],
                                      ALU.mult).then_inc(bank_read, 1)
                for i in range(4):
                    split_lo(dve, s_sb + i + 1)
                    dve.wait_ge(slab_used, s_sb + i + 1)
                    dve_chain.step(dve, dve.tensor_tensor(part(i), psum[:, (s_sb + i) % BANKS, :],
                                                          part(i), ALU.mult))
                    dve.tensor_tensor(flat(mix, i), flat(mix, i), part(i), ALU.add).then_inc(mix_ready, 1)
                    dve.sem_inc(bank_read, 1)
                    dve.wait_ge(mix_hi, i + 1)
                    dve.tensor_tensor(flat(inL, i), flat(mix, i), flat(inH, i).bitcast(F32), ALU.subtract)
        end_slabs(8)

        x_added = sem("residual_added")
        added = {"n": 0, "squares": 0}

        def onto_residual(s0, gain_at):
            own = ExitStack()
            norm = Norm(x, src_in, gain_at, own)
            parts = sb(f"square_sums{norm.n}", [P, NT, 4], ctx=own)
            first_add = added["n"]
            added["n"] += 4
            first_square = added["squares"]
            added["squares"] += 4 * NT
            with nc.Block(no_gpsimd_drain=True) as block:
                @block.sync
                def _(sp):
                    feed(sp, s0 + 4)

                @block.tensor
                def _(pe):
                    project(pe, s0, 4, natural_slab, src_in)
                    norm.turn(pe)

                @block.scalar
                def _(act):
                    for i in range(4):
                        split_hi(act, s0 + i + 1)
                        act.wait_ge(x_added, first_add + i + 1)
                        for n in range(NT):
                            act.activation(norm.junk[:, (NT * i + n) % 4 * 256:((NT * i + n) % 4 + 1) * 256],
                                           x[:, n, 256 * i:256 * (i + 1)], ACT.Square, scale=D ** -0.5,
                                           accum_out=parts[:, n, i:i + 1]).then_inc(square_summed, 1)
                        act.wait_ge(square_summed, first_square + NT * (i + 1))
                    norm.hi(act)

                @block.gpsimd
                def _(pool):
                    norm.roots(pool)

                @block.vector
                def _(dve):
                    for i in range(4):
                        split_lo(dve, s0 + i + 1)
                        dve.wait_ge(slab_used, s0 + i + 1)
                        dve.tensor_tensor(nat_cols(x, i), nat_cols(x, i), bank_nat((s0 + i) % BANKS),
                                          ALU.add).then_inc(x_added, 1)
                        dve.sem_inc(bank_read, 1)
                    dve.wait_ge(square_summed, first_square + 4 * NT)
                    dve.tensor_reduce(mean_sq[:, 0:NT], parts[:, :, :], AX.X, ALU.add).then_inc(norm_ready, NT)
                    norm.diags(dve)
                    norm.lo(dve)
            own.close()
            end_slabs(4)

        square_summed = sem("squares_summed")
        onto_residual(s_wo, 1)
        mx.close()
        sbx.close()
        first.close()

        ff = ExitStack()
        act_H = sb("act_H", [P, FT, T], F32R, ctx=ff)
        act_L = sb("act_L", [P, FT, T], F32R, ctx=ff)
        gate = sb("gate", [P, BANKS, T], ctx=ff)
        both = sb("both", [P, BANKS, T], ctx=ff)
        silu_ready, both_ready = sem("silu_ready"), sem("ffn_both_ready")
        s_in, s_out = FIRST_SLAB["ffn_in"], FIRST_SLAB["ffn_out"]
        row = lambda t, i: t[:, bass.ds(i, 1), :].rearrange("p a t -> p (a t)")
        norm2 = Norm(x, src_in, 2, ff)
        with nc.Block(no_gpsimd_drain=True) as block:
            @block.sync
            def _(sp):
                feed(sp, s_out + N_FFN_OUT)

            @block.gpsimd
            def _(pool):
                norm2.roots(pool)

            @block.tensor
            def _(pe):
                project(pe, s_in, N_FFN_IN, turned_slab, src_in)
                for i in range(N_FFN_OUT):
                    s = s_out + i
                    pe.wait_ge(split_ready, s + 1)
                    pe.wait_ge(bank_read, state["banks"] + min(2 * i + 2, FT))
                    w = weights_of(s % RING, 2)
                    for kk in range(2):
                        for n in range(NT):
                            for c in range(2):
                                mm = three(pe, psum[:, 4 + 2 * n + c, :],
                                           [v[:, 2 * i + kk, n * P:(n + 1) * P] for v in (act_H, act_L)],
                                           [v[:, kk, c * 512:(c + 1) * 512] for v in w],
                                           i == 0 and kk == 0, i == N_FFN_OUT - 1 and kk == 1)
                    mm.then_inc(slab_used, 1)
                norm2.turn(pe)

            @block.scalar
            def _(act):
                def body(s, it):
                    split_hi(act, s + 1, it)
                    act.wait_ge(slab_used, at(it, s + 1))
                    act.wait_ge(bank_read, at(it, state["banks"] + s - s_in - BANKS + 1))
                    act.activation(gate[:, s % BANKS, :], psum[:, s % BANKS, 0:T], ACT.Silu).then_inc(silu_ready, 1)
                per_slab(act, s_in, N_FFN_IN, body)
                for i in range(N_FFN_OUT):
                    split_hi(act, s_out + i + 1)
                for t in range(NT):
                    act.wait_ge(x_added, added["n"] + t + 1)
                    norm2.square(act, t)
                norm2.hi(act)

            @block.vector
            def _(dve):
                def body(s, it):
                    i, b = at(it, s - s_in), s % BANKS
                    split_lo(dve, s + 1, it)
                    dve.wait_ge(silu_ready, at(it, s - s_in + 1))
                    dve.tensor_tensor(both[:, b, :], gate[:, b, :], psum[:, b, T:2 * T],
                                      ALU.mult).then_inc(both_ready, 1)
                    dve.tensor_tensor(row(act_H, i), gate[:, b, :], psum[:, b, T:2 * T],
                                      ALU.mult).then_inc(both_ready, 1)
                    dve.wait_ge(both_ready, at(it, 2 * (s - s_in) + 2, 2 * GROUP))
                    dve.tensor_tensor(row(act_L, i), both[:, b, :], row(act_H, i).bitcast(F32),
                                      ALU.subtract).then_inc(bank_read, 1)
                per_slab(dve, s_in, N_FFN_IN, body)
                for i in range(N_FFN_OUT):
                    split_lo(dve, s_out + i + 1)
                dve.wait_ge(slab_used, s_out + N_FFN_OUT)
                for n in range(NT):
                    dve.tensor_tensor(x[:, n, :], x[:, n, :],
                                      psum[:, 4 + 2 * n:6 + 2 * n, :].rearrange("p b c -> p (b c)"),
                                      ALU.add).then_inc(x_added, 1)
                norm2.diags(dve)
                norm2.lo(dve)
        added["n"] += NT
        end_slabs(FT)
        ff.close()

        N_WIN2 = 12
        SL_GQ, SL_GK, SL_GR, SL_NQ, SL_C, SL_SW, SL_GV, SL_V, SL_SMALL = 0, 1, 2, 4, 6, 7, 8, 10, 11
        kv = ExitStack()
        xkv = sb("xkv", [P, 8, 512], ctx=kv)
        second = ExitStack()
        catT = sb("catT", [P, KD // 2, T], ctx=second)
        proj2 = sb("proj2", [P, N_WIN2, 512], ctx=second)
        src_mem = [sb(n, [P, KD, T], F32R, ctx=second) for n in ("memH", "memL")]
        mem = sb("mem", [P, NT, D], ctx=second)
        nsx = ExitStack()
        w1 = sb("w1", [P, 2, CB // 2, P], ctx=nsx)
        w2k = sb("w2k", [P, 2, ND], ctx=nsx)
        w2v = sb("w2v", [P, ND], ctx=nsx)
        pos = sb("pos", [P, 2, CB // 2], ctx=nsx)
        relx = sb("relx", [BUCKETS + 1, NH], ctx=nsx)
        buckets = sb("buckets", [BUCKETS + 1, 2, 2 * T - 1], ctx=nsx)
        gla_w2 = sb("gla_w2", [GRANK, T], ctx=nsx)
        gla_vec = sb("gla_vec", [P, 3], ctx=nsx)
        bias_c = sb("bias_c", [P, NT, NCMP, NH], ctx=nsx)
        bias_up = sb("bias_up", [P, NH, T], ctx=nsx)
        turn_over = sb("turn_over", [P, P], ctx=nsx)
        line = sb("line", [NH, 2 * T], ctx=nsx)
        bias_line = nc.dram_tensor("bias_line", [NH, 2 * T], F32, kind="Internal").ap()
        N_ = {n: sem("nsa_" + n) for n in (
            "line_done", "line_ready", "line_stored", "bias_landed", "cmp_bias_done", "kc_ready",
            "hid_ready", "cmp_done", "gate_ready", "seen_ready",
            "bias_done")}
        N_SMALL2 = 8
        small2, large2 = sem("small_weights_landed"), sem("memory_and_w1_landed")

        def small_slab(pe, slot, bank, src):
            w = weights_of(slot, KD)
            for k in range(KD):
                three(pe, psum[:, bank, 0:T], [v[:, k, 0:P] for v in w], [v[:, k, :] for v in src],
                      k == 0, k == KD - 1)
            for n in range(NT):
                for k in range(KD):
                    mm = three(pe, psum[:, bank, T + 24 * n:T + 24 * (n + 1)],
                               [v[:, k, n * P:(n + 1) * P] for v in src],
                               [v[:, k, GRANK:GRANK + 24] for v in w], k == 0, k == KD - 1)
            return mm

        s_w2 = FIRST_SLAB["win2_turned"]
        with nc.Block(no_gpsimd_drain=True) as block:
            @block.sync
            def _(sp):
                for h in range(2):
                    sp.dma_start(w2k[:, h, :], ins["cmp_k_w2"]).then_inc(small2, 16)
                sp.dma_start(w2v[:, :], ins["cmp_v_w2"]).then_inc(small2, 16)
                sp.dma_start(pos[:, :, :], ins["cmp_pos"]).then_inc(small2, 16)
                sp.dma_start(relx[0:BUCKETS, :], ins["rel_bias"]).then_inc(small2, 16)
                sp.dma_start(buckets[:, :, :], ins["buckets"]).then_inc(small2, 16)
                sp.dma_start(gla_w2[:, :], ins["gla_w2"]).then_inc(small2, 16)
                sp.dma_start(gla_vec[:, :], ins["gla_vec"]).then_inc(small2, 16)
                feed(sp, s_w2 + N_WIN2)
                sp.wait_ge(small2, 16 * N_SMALL2 + 1)
                sp.wait_ge(N_["bias_landed"], 16)
                sp.wait_ge(large2, 16 * 4)

            @block.gpsimd
            def _(pool):
                pool_chain.step(pool, pool.memset(relx[BUCKETS:BUCKETS + 1, :], MASKED))
                pool.sem_inc(small2, 1)
                pool_chain.step(pool, pool.memset(turn_over[:, :], 0.0))
                pool_chain.step(pool, pool.affine_select(
                    out=turn_over[:, :], in_=turn_over[:, :], compare_op=ALU.not_equal, fill=1.0,
                    base=-(P - 1), pattern=[[1, P]], channel_multiplier=1))

            @block.tensor
            def _(pe):
                project(pe, s_w2, 8, turned_slab, src_in)
                pe.wait_ge(small2, 16 * N_SMALL2 + 1)
                pe.matmul(psum[0:NH, 4, 0:2 * T - 1], relx[:, :], buckets[:, 1, :], start=True,
                          stop=True).then_inc(N_["line_done"], 1)
                for t in range(NT):
                    for n in range(NCMP):
                        at_ = T - 1 + t * P - CS * n - (CB - 1)
                        i = (t * NCMP + n) * NH
                        mm = pe.matmul(psum[:, 5, i:i + NH], buckets[:, 0, at_:at_ + P], relx[:, :],
                                       start=True, stop=True)
                mm.then_inc(N_["cmp_bias_done"], 1)
                project(pe, s_w2 + 8, 3, natural_slab, src_in, before=8)
                project(pe, s_w2 + 11, 1, small_slab, src_in, before=11)

            @block.scalar
            def _(act):
                for i in range(N_WIN2 - 1):
                    copy_step(act, proj2, s_w2, s_w2 + i)
                    if i in (0, 2):
                        act.dma_start(mem[:, i // 2, :], ins["mem"][0, i // 2 * P:(i // 2 + 1) * P, :])\
                           .then_inc(large2, 16)
                    if i in (4, 6):
                        act.dma_start(w1[:, i // 2 - 2, :, :], ins["cmp_w1"][:, i // 2 - 2, :, :])\
                           .then_inc(large2, 16)
                    if i == 8:
                        act.wait_ge(N_["line_done"], 1)
                        act.activation(line[:, 0:2 * T - 1], psum[0:NH, 4, 0:2 * T - 1], ACT.Copy)\
                           .then_inc(N_["line_ready"], 1)
                        act.wait_ge(N_["line_ready"], 1)
                        act.dma_start(bias_line[:, 0:2 * T - 1], line[:, 0:2 * T - 1]).then_inc(N_["line_stored"], 16)
                    elif i == 9:
                        act.wait_ge(N_["line_stored"], 16)
                        toeplitz = bass.AP(bias_line.tensor, 0, [[1, P], [2 * T, NH], [1, T]])
                        act.dma_start(bias_up[:, :, :], toeplitz).then_inc(N_["bias_landed"], 16)
                s = s_w2 + N_WIN2 - 1
                split_hi(act, s + 1)
                act.wait_ge(slab_used, s + 1)
                act.activation(proj2[0:GRANK, SL_SMALL, 0:T], psum[0:GRANK, s % BANKS, 0:T], ACT.Copy)
                act.activation(proj2[:, SL_SMALL, T:T + 48], psum[:, s % BANKS, T:T + 48],
                               ACT.Copy).then_inc(bank_read, 1)

            @block.vector
            def _(dve):
                for i in range(N_WIN2):
                    split_lo(dve, s_w2 + i + 1)
                    if i == 9:
                        dve.wait_ge(N_["cmp_bias_done"], 1)
                        dve.tensor_copy(bias_c[:, :, :, :].rearrange("p t n h -> p (t n h)"),
                                        psum[:, 5, 0:NT * NCMP * NH])
        end_slabs(N_WIN2)

        gl = ExitStack()
        GP = GH // 2
        CH = GP * NT
        gu = sb("gu", [P, GP * T], ctx=gl)
        ga_ = sb("ga_", [P, GP * T], ctx=gl)
        gcum = sb("gcum", [P, GP * T], ctx=gl)
        gmask = sb("gmask", [P, GP * T], ctx=gl)
        gdec = sb("gdec", [P, 3, CH], ctx=gl)
        gfac = sb("gfac", [P, GP], ctx=gl)
        gscT = sb("gscT", [P, NT * GH, P], ctx=gl)
        gkeN = sb("gkeN", [P, GP * P], ctx=gl)
        gS = sb("gS", [P, GP, GV], ctx=gl)
        gO = sb("gO", [P, NT * GH, GV], ctx=gl)
        gSq = mem[:, 0, :].rearrange("p (i v) -> p i v", v=GV)
        gms = sb("gms", [P, NT * GH], ctx=gl)
        gq = proj2[:, SL_GQ, :]
        gk = proj2[:, SL_GK, :]
        g_names = ("u_done", "u_ready", "l_ready", "mid_ready", "d_ready", "e_ready", "q_ready", "sc_done",
                   "turned", "keN_ready", "dS_done", "S_ready", "scT_ready", "o_done", "sq_ready", "ms_ready",
                   "o_scaled", "o_turned", "masks_ready")
        G = {n: sem("gla_" + n) for n in g_names}
        pairs_of = lambda v, s=P: v.rearrange("p (c s) -> p c s", s=s)
        gV = lambda t, h: proj2[:, SL_GV + h // 2, t * 256 + (h % 2) * GV:t * 256 + (h % 2 + 1) * GV]
        g_at = lambda c, h: (h % 2) * 4 + c * GP + h // 2
        rows = lambda h: slice((h % 2) * GD, (h % 2 + 1) * GD)
        mem_norm = Norm(mem, src_mem, 4, gl)
        kc2 = mem_norm.junk[:, :].rearrange("p (v g t) -> p v g t", v=2, g=NG)
        blocks = sb("blocks", [P, 2, CB // 2, NG, NCMP], ctx=gl)
        two = lambda r, sl: proj2[r, sl, :].rearrange("p (a t) -> p a t", a=2)

        def hidden(pe, kv_):
            for j in range(CB // 2):
                mm = pe.matmul(psum[:, kv_, 0:NG * NCMP], w1[:, kv_, j, :],
                               blocks[:, kv_, j, :, :].rearrange("p g b -> p (g b)"),
                               start=(j == 0), stop=(j == CB // 2 - 1))

        with nc.Block(no_gpsimd_drain=True) as block:
            @block.tensor
            def _(pe):
                for f in range(GP):
                    mm = pe.matmul(psum[:, 4, f * T:(f + 1) * T], gla_w2[:, f * P:(f + 1) * P],
                                   proj2[0:GRANK, SL_SMALL, 0:T], start=True, stop=True)
                mm.then_inc(G["u_done"], 1)
                mem_norm.turn(pe)
                pe.wait_ge(G["q_ready"], 1)
                for f in range(GP):
                    mm = pe.transpose(psum[:, 5, f * P:(f + 1) * P], gk[:, f * T:f * T + P], ident[:, :])
                mm.then_inc(G["turned"], 1)
                for c in range(NT):
                    for h in range(GH):
                        at_ = slice((h // 2) * T + c * P, (h // 2) * T + (c + 1) * P)
                        mm = pe.matmul(by4(6, 2)[:, g_at(c, h), :], gk[rows(h), at_], gq[rows(h), at_],
                                       start=True, stop=True)
                mm.then_inc(G["sc_done"], 1)
                pe.wait_ge(N_["kc_ready"], 1)
                hidden(pe, 0)
                pe.wait_ge(G["keN_ready"], 1)
                for h in range(GH):
                    mm = pe.matmul(psum[rows(h), 4, (h // 2) * GV:(h // 2 + 1) * GV], gkeN[:, h * GD:(h + 1) * GD],
                                   gV(0, h), start=True, stop=True)
                mm.then_inc(G["dS_done"], 1)
                hidden(pe, 1)
                pe.wait_ge(G["scT_ready"], 1)
                pe.wait_ge(G["S_ready"], 1)
                for c in range(NT):
                    for h in range(GH):
                        o = by4(4, 2)[:, g_at(c, h), :]
                        mm = pe.matmul(o, gscT[:, g_at(c, h), :], gV(c, h), start=True, stop=(c == 0))
                        if c == 1:
                            mm = pe.matmul(o, gq[rows(h), (h // 2) * T + P:(h // 2 + 1) * T], gS[rows(h), h // 2, :],
                                           start=False, stop=True)
                mm.then_inc(G["o_done"], 1)
                pe.wait_ge(G["o_scaled"], 1)
                for h in range(GH):
                    for c in range(NT):
                        mm = pe.transpose(by4(6, 2)[:, h * 2 + c, :], gO[:, g_at(c, h), :], ident[:, :])
                mm.then_inc(G["o_turned"], 1)

            @block.gpsimd
            def _(pool):
                mem_norm.roots(pool)
                pool_chain.step(pool, pool.memset(gmask[:, :], 1.0))
                pool_chain.step(pool, pool.memset(pairs_of(gmask[:, :])[:, :, 0:1], 0.0))
                pool.memset(gscT[:, :, :], 0.0).then_inc(G["masks_ready"], 1)
                pool.wait_ge(G["ms_ready"], 1)
                inv_sqrt(pool, gms[:, :], gms[:, :])

            @block.scalar
            def _(act):
                mem_norm.squares(act)
                act.wait_ge(G["u_ready"], 1)
                act_chain.step(act, act.activation(ga_[:, :], gu[:, :], ACT.Abs))
                act_chain.step(act, act.activation(ga_[:, :], ga_[:, :], ACT.Exp, scale=-1.0))
                act.activation(ga_[:, :], ga_[:, :], ACT.Ln, bias=1.0).then_inc(G["l_ready"], 1)
                mem_norm.hi(act)
                act.wait_ge(G["mid_ready"], 1)
                act.activation(gdec[:, :, :], gdec[:, :, :], ACT.Exp, scale=1 / GTAU).then_inc(G["e_ready"], 1)
                act.wait_ge(G["d_ready"], 1)
                act.activation(ga_[:, :], gu[:, :], ACT.Exp, scale=1 / GTAU).then_inc(G["e_ready"], 1)
                act.activation(gcum[:, :], gu[:, :], ACT.Exp, scale=-1 / GTAU).then_inc(G["e_ready"], 1)
                act.wait_ge(G["turned"], 1)
                act.activation(gkeN[:, :], psum[:, 5, 0:GP * P], ACT.Copy).then_inc(G["keN_ready"], 1)
                silu = proj2[:, SL_GR:SL_GR + 2, :]
                act_chain.step(act, act.activation(silu, silu, ACT.Silu))
                act.wait_ge(G["o_done"], 1)
                act.activation(gSq, by4(4, 2), ACT.Square, scale=GV ** -0.5).then_inc(G["sq_ready"], 1)
                act.activation(gO[:, :, :], by4(4, 2), ACT.Copy).then_inc(G["sq_ready"], 1)

            @block.vector
            def _(dve):
                dve.wait_ge(G["u_done"], 1)
                for f in range(GP):
                    o = dve.tensor_scalar(gu[:, f * T:(f + 1) * T], psum[:, 4, f * T:(f + 1) * T],
                                          gla_vec[:, f:f + 1], None, ALU.add)
                o.then_inc(G["u_ready"], 1)
                mem_norm.diags(dve)
                dve.wait_ge(G["l_ready"], 1)
                dve_chain.step(dve, dve.scalar_tensor_tensor(out=gu[:, :], in0=gu[:, :], scalar=0.0, in1=ga_[:, :],
                                                             op0=ALU.min, op1=ALU.subtract))
                dve.wait_ge(G["masks_ready"], 1)
                dve_chain.step(dve, dve.tensor_tensor_scan(gcum[:, :], gmask[:, :], gu[:, :], 0.0,
                                                           ALU.mult, ALU.add))
                mid = pairs_of(gcum[:, :])[:, :, P // 2 - 1:P // 2]
                last = pairs_of(gcum[:, :])[:, :, P - 1:P]
                dve.tensor_copy(gdec[:, 0, :].unsqueeze(2), mid)
                dve.tensor_copy(gdec[:, 1, :].unsqueeze(2), last)
                dve.tensor_tensor(gdec[:, 2, :].unsqueeze(2), last, mid, ALU.subtract).then_inc(G["mid_ready"], 1)
                dve_chain.step(dve, dve.tensor_tensor(pairs_of(gu[:, :]), pairs_of(gcum[:, :]),
                                                      mid.to_broadcast([P, CH, P]), ALU.subtract))
                dve.tensor_scalar(gu[:, :], gu[:, :], EXPO_CAP * GTAU, -EXPO_CAP * GTAU, ALU.min,
                                  ALU.max).then_inc(G["d_ready"], 1)
                mem_norm.lo(dve)
                dve.wait_ge(G["e_ready"], 3)
                dve.scalar_tensor_tensor(out=gq, in0=gq, scalar=GD ** -0.5, in1=ga_[:, :], op0=ALU.mult,
                                         op1=ALU.mult)
                dve.tensor_tensor(gk, gk, gcum[:, :], ALU.mult).then_inc(G["q_ready"], 1)
                for g in range(NG):
                    r = slice(g * ND, (g + 1) * ND)
                    dve.tensor_copy(kc2[0:ND, :, g, :], two(r, SL_C))
                    o = dve.tensor_copy(kc2[ND:P, :, g, 0:T - 1], two(r, SL_C)[:, :, 1:T])
                dve_chain.step(dve, o)
                for kv_ in range(2):
                    for hi_ in range(2):
                        js = slice(hi_ * CS // 2, (hi_ + 1) * CS // 2)
                        at_ = kc2[:, kv_, :, :].rearrange("p g (b s c) -> p s g b c", s=CS // 2, c=2)[
                            :, :, :, hi_:hi_ + NCMP, 0]
                        o = dve.tensor_tensor(blocks[:, kv_, js, :, :], at_,
                                              pos[:, kv_, js].unsqueeze(2).unsqueeze(2)
                                              .to_broadcast([P, CS // 2, NG, NCMP]), ALU.add)
                o.then_inc(N_["kc_ready"], 1)
                dve_chain.step(dve, dve.tensor_tensor(gfac[:, :].unsqueeze(2),
                                                      gdec[:, 2, :].rearrange("p (f c) -> p f c", c=NT)[:, :, 0:1],
                                                      gdec[:, 0, :].rearrange("p (f c) -> p f c", c=NT)[:, :, 1:2],
                                                      ALU.mult))
                dve.wait_ge(G["sc_done"], 1)
                dve.copy_predicated(gscT[:, :, :], causal[:, :].bitcast(U32).unsqueeze(1).to_broadcast([P, NT * GH, P]),
                                    by4(6, 2)).then_inc(G["scT_ready"], 1)
                dve.wait_ge(G["dS_done"], 1)
                dve.tensor_tensor(gS[:, :, :], psum[:, 4, 0:GP * GV].rearrange("p (f v) -> p f v", f=GP),
                                  gfac[:, :].unsqueeze(2).to_broadcast([P, GP, GV]), ALU.mult).then_inc(G["S_ready"], 1)
                dve.wait_ge(G["sq_ready"], 1)
                dve.tensor_reduce(gms[:, :], gSq, AX.X, ALU.add).then_inc(G["ms_ready"], 1)
                dve.wait_ge(rstd_ready, rstds["n"])
                dve.wait_ge(G["sq_ready"], 2)
                dve.tensor_tensor(gO[:, :, :], gO[:, :, :], gms[:, :].unsqueeze(2).to_broadcast([P, NT * GH, GV]),
                                  ALU.mult).then_inc(G["o_scaled"], 1)
                dve.wait_ge(G["o_turned"], 1)
                for h in range(GH):
                    dve.scalar_tensor_tensor(
                        out=catT[:, h, :], in0=psum[:, 6 + h // 2, (h % 2) * T:(h % 2 + 1) * T],
                        scalar=gla_vec[:, 2:3], in1=proj2[:, SL_GR + h // 2, (h % 2) * T:(h % 2 + 1) * T],
                        op0=ALU.mult, op1=ALU.mult)
        gl.close()

        nb = ExitStack()
        bias = sb("bias", [P, NH, T], ctx=nsx)
        kdup = sb("kdup", [P, 2, NG, T], ctx=nsx)
        kcmp = sb("kcmp", [P, NG, NCMP], ctx=nsx)
        vcmp = sb("vcmp", [NCMP, NG, ND], ctx=nsx)
        ngate = sb("ngate", [P, NT, 3 * NH], ctx=nsx)
        gsel = sb("gsel", [P, NH, 6], ctx=nsx)
        seen = sb("seen", [P, 1], ctx=nsx)
        hid = sb("hid", [P, 2, NG * NCMP], ctx=nb)
        s_mem = FIRST_SLAB["xa_wk"]
        split_gla = Split(catT, src_in, tiles=(0, KD // 2))
        with nc.Block(no_gpsimd_drain=True) as block:
            @block.tensor
            def _(pe):
                for b in range(4):
                    mm = pe.matmul(psum[:, 4 + b, :], turn_over[:, :],
                                   bias_up[:, 2 * b:2 * b + 2, :].rearrange("p h c -> p (h c)"),
                                   start=True, stop=True)
                mm.then_inc(N_["bias_done"], 1)
                pe.wait_ge(N_["hid_ready"], 2)
                pe.matmul(psum[:, 2, 0:NG * NCMP], w2k[:, :, :].rearrange("p a d -> p (a d)"), hid[:, 0, :],
                          start=True, stop=True).then_inc(N_["cmp_done"], 1)
                for g in range(NG):
                    mm = pe.matmul(psum[0:NCMP, 3, g * ND:(g + 1) * ND], hid[:, 1, g * NCMP:(g + 1) * NCMP],
                                   w2v[:, :], start=True, stop=True)
                mm.then_inc(N_["cmp_done"], 1)

            @block.scalar
            def _(act):
                split_gla.hi(act)
                split_hi(act, s_mem + 1)
                act.activation(ngate[:, :, :].rearrange("p n c -> p (n c)"), proj2[:, SL_SMALL, T:T + 3 * NT * NH],
                               ACT.Sigmoid).then_inc(N_["gate_ready"], 1)
                for kv_ in range(2):
                    act.activation(hid[:, kv_, :], psum[:, kv_, 0:NG * NCMP],
                                   ACT.Gelu_apprx_tanh).then_inc(N_["hid_ready"], 1)
                act.wait_ge(N_["cmp_done"], 2)
                act.activation(kcmp[:, :, :].rearrange("p g n -> p (g n)"), psum[:, 2, 0:NG * NCMP], ACT.Copy)
                act.activation(vcmp[:, :, :].rearrange("p g d -> p (g d)"), psum[0:NCMP, 3, 0:NG * ND], ACT.Copy)

            @block.gpsimd
            def _(pool):
                pool_chain.step(pool, pool.memset(seen[:, :], 1.0))
                pool.affine_select(out=seen[:, :], in_=seen[:, :], compare_op=ALU.is_ge, fill=0.0,
                                   base=-(CB - 1), pattern=[[1, 1]],
                                   channel_multiplier=1).then_inc(N_["seen_ready"], 1)

            @block.vector
            def _(dve):
                split_gla.lo(dve)
                split_lo(dve, s_mem + 1)
                two = lambda r, sl: proj2[r, sl, :].rearrange("p (a t) -> p a t", a=2)
                for g in range(NG):
                    r = slice(g * ND, (g + 1) * ND)
                    for half in range(2):
                        dve.tensor_copy(kdup[half * ND:(half + 1) * ND, :, g, :], two(r, SL_SW))
                dve.wait_ge(N_["gate_ready"], 1)
                ng3 = lambda t: ngate[:, t, :].rearrange("p (h i) -> p h i", i=3)
                dve.tensor_copy(gsel[:, :, 0:2], ng3(1)[:, :, 1:3])
                dve.tensor_copy(gsel[:, :, 2:4], ng3(0)[:, :, 1:3])
                dve.wait_ge(N_["seen_ready"], 1)
                dve.tensor_scalar(gsel[:, :, 4:5], ng3(0)[:, :, 0:1], seen[:, 0:1], None, ALU.mult)
                dve.tensor_copy(gsel[:, :, 5:6], ng3(1)[:, :, 0:1])
                dve.wait_ge(N_["bias_done"], 1)
                dve.tensor_copy(bias[:, :, :].rearrange("p (b h) c -> p b (h c)", b=4), psum[:, 4:8, :])
        nb.close()

        na = ExitStack()
        SC = 512 + 256 + NT * NCMP
        sc = sb("sc", [P, 2, SC + 2], ctx=na)
        negm = sb("negm", [P, 2, 6], ctx=na)
        den = sb("den", [P, 2, 6], ctx=na)
        coef = sb("coef", [P, 2, 6], ctx=na)
        pT = sb("pT", [P, 2, 2, 3 * P], ctx=na)
        pTc = sb("pTc", [NCMP, 2, T], ctx=na)
        A_ = {n: sem("na_" + n) for n in ("s_done", "scored", "max_ready", "exp_ready", "scaled", "t_done",
                                          "pT_ready", "o_done", "out_hi", "o_out")}
        SPANS = [(0, 256), (256, 512), (512, 640), (640, 768), (768, 768 + NCMP), (768 + NCMP, 768 + 2 * NCMP)]
        nqT = lambda h: proj2[(h % 2) * ND:(h % 2 + 1) * ND, SL_NQ + h // 4, ((h // 2) % 2) * T:((h // 2) % 2 + 1) * T]
        half = lambda h: slice((h % 2) * ND, (h % 2 + 1) * ND)
        with nc.Block(no_gpsimd_drain=True) as block:
            @block.sync
            def _(sp):
                feed(sp, s_mem + NH)

            @block.tensor
            def _(pe):
                def scores(h):
                    g, bA, bB = h // (NH // NG), 4, 5
                    if h >= 1:
                        pe.wait_ge(A_["scored"], h)
                    q = nqT(h)
                    for i in range(2):
                        pe.matmul(psum[:, bA, i * T:(i + 1) * T], q[:, P:T], kdup[half(h), i, g, :],
                                  start=True, stop=True)
                    for i in range(2):
                        pe.matmul(psum[:, bB, i * P:(i + 1) * P], q[:, 0:P], kdup[half(h), i, g, 0:P],
                                  start=True, stop=True)
                    for t in range(NT):
                        mm = pe.matmul(psum[:, bB, T + t * NCMP:T + (t + 1) * NCMP], q[:, t * P:(t + 1) * P],
                                       kcmp[half(h), g, :], start=True, stop=True)
                    mm.then_inc(A_["s_done"], 1)

                def turn(h):
                    pe.wait_ge(A_["scaled"], h + 1)
                    if h >= 1:
                        pe.wait_ge(A_["pT_ready"], h)
                    s = sc[:, h % 2, :]
                    for i in range(2):
                        b = 6 + i
                        pe.transpose(psum[:, b, 0:P], s[:, 512 + i * P:512 + (i + 1) * P], ident[:, :])
                        pe.transpose(psum[:, b, P:T], s[:, i * T:i * T + P], ident[:, :])
                        pe.transpose(psum[:, b, T:3 * P], s[:, i * T + P:(i + 1) * T], ident[:, :])
                        mm = pe.transpose(psum[0:NCMP, b, 3 * P:4 * P], s[:, 768 + i * NCMP:768 + (i + 1) * NCMP],
                                          ident[:, :])
                    mm.then_inc(A_["t_done"], 1)

                def outputs(h):
                    g = h // (NH // NG)
                    pe.wait_ge(A_["pT_ready"], h + 1)
                    if h % 2 == 0 and h >= 4:
                        pe.wait_ge(A_["o_out"], h // 2 - 1)
                    o = psum[half(h), 2 + (h // 2) % 2, 0:T]
                    for i in range(2):
                        v = lambda kt: proj2[:, SL_V, kt * 256 + i * P + g * ND:kt * 256 + i * P + (g + 1) * ND]
                        pe.matmul(o, v(0), pT[:, h % 2, i, 0:T], start=(i == 0), stop=True, skip_group_check=True)
                        pe.matmul(o[:, P:T], v(1), pT[:, h % 2, i, T:3 * P], start=False, stop=True,
                                  skip_group_check=True)
                    mm = pe.matmul(o, vcmp[:, g, :], pTc[:, h % 2, :], start=False, stop=True,
                                   skip_group_check=True)
                    mm.then_inc(A_["o_done"], 1)

                scores(0)
                for h in range(NH):
                    if h + 1 < NH:
                        scores(h + 1)
                    project(pe, s_mem + h, 1, turned_slab if h < 4 else natural_slab, src_mem, before=h, banks=2)
                    turn(h)
                    outputs(h)

            @block.scalar
            def _(act):
                def exps(h):
                    act.wait_ge(A_["max_ready"], h + 1)
                    for i, (a, b) in enumerate(SPANS):
                        e = act.activation(sc[:, h % 2, a:b], sc[:, h % 2, a:b], ACT.Exp,
                                           bias=negm[:, h % 2, i:i + 1], accum_out=den[:, h % 2, i:i + 1])
                    e.then_inc(A_["exp_ready"], 1)

                exps(0)
                for h in range(NH):
                    act.wait_ge(A_["t_done"], h + 1)
                    if h >= 2:
                        act.wait_ge(A_["o_done"], h - 1)
                    act.activation(pT[:, h % 2, :, :], psum[:, 6:8, 0:3 * P], ACT.Copy)
                    act.activation(pTc[:, h % 2, :].rearrange("p (t q) -> p t q", t=NT), psum[0:NCMP, 6:8, 3 * P:4 * P],
                                   ACT.Copy).then_inc(A_["pT_ready"], 1)
                    if h + 1 < NH:
                        exps(h + 1)
                    only_copy(act, xkv, s_mem, s_mem + h, banks=2)
                    if h + 1 < NH:
                        split_hi(act, s_mem + h + 2)
                    if h % 2 == 1:
                        act.wait_ge(A_["o_done"], h + 1)
                        act.activation(inH[:, 4 + h // 2, :], psum[:, 2 + (h // 2) % 2, 0:T],
                                       ACT.Copy).then_inc(A_["out_hi"], 1)

            @block.vector
            def _(dve):
                SCALE = ND ** -0.5

                def score(h):
                    dve.wait_ge(A_["s_done"], h + 1)
                    if h >= 2:
                        dve.wait_ge(A_["t_done"], h - 1)
                    s, bA, bB = sc[:, h % 2, :], 4, 5
                    wide = lambda v, n: v.rearrange("p (a c) -> p a c", a=n)
                    dve.scalar_tensor_tensor(out=wide(s[:, 0:512], 2), in0=wide(psum[:, bA, :], 2), scalar=SCALE,
                                             in1=bias[:, h:h + 1, :].to_broadcast([P, 2, T]),
                                             op0=ALU.mult, op1=ALU.add)
                    dve.scalar_tensor_tensor(out=wide(s[:, 512:768], 2), in0=wide(psum[:, bB, 0:256], 2), scalar=SCALE,
                                             in1=bias[:, h:h + 1, P:T].to_broadcast([P, 2, P]),
                                             op0=ALU.mult, op1=ALU.add)
                    o = dve.scalar_tensor_tensor(
                        out=s[:, 768:768 + 2 * NCMP], in0=psum[:, bB, T:T + 2 * NCMP], scalar=SCALE,
                        in1=bias_c[:, :, :, h].rearrange("p t n -> p (t n)"), op0=ALU.mult, op1=ALU.add)
                    o.then_inc(A_["scored"], 1)
                    dve.wait_ge(A_["scored"], h + 1)
                    nm = negm[:, h % 2, :]
                    dve.tensor_reduce(nm[:, 0:2], wide(s[:, 0:512], 2), AX.X, ALU.max, negate=True)
                    dve.tensor_reduce(nm[:, 2:4], wide(s[:, 512:768], 2), AX.X, ALU.max, negate=True)
                    dve.tensor_reduce(nm[:, 4:6], wide(s[:, 768:768 + 2 * NCMP], 2), AX.X, ALU.max,
                                      negate=True).then_inc(A_["max_ready"], 1)

                def scale(h):
                    dve.wait_ge(A_["exp_ready"], h + 1)
                    c = coef[:, h % 2, :]
                    dve_chain.step(dve, dve.reciprocal(c, den[:, h % 2, :]))
                    dve_chain.step(dve, dve.tensor_tensor(c, c, gsel[:, h, :], ALU.mult))
                    for i, (a, b) in enumerate(SPANS):
                        o = dve.tensor_scalar(sc[:, h % 2, a:b], sc[:, h % 2, a:b], c[:, i:i + 1], None, ALU.mult)
                    o.then_inc(A_["scaled"], 1)

                def out_lo(i):
                    dve.wait_ge(A_["out_hi"], i + 1)
                    dve.tensor_tensor(inL[:, 4 + i, :], psum[:, 2 + i % 2, 0:T], inH[:, 4 + i, :].bitcast(F32),
                                      ALU.subtract).then_inc(A_["o_out"], 1)

                score(0)
                for h in range(NH):
                    if h + 1 < NH:
                        score(h + 1)
                    scale(h)
                    if h + 1 < NH:
                        split_lo(dve, s_mem + h + 2)
                    if h % 2 == 0 and h > 0:
                        out_lo(h // 2 - 1)
                out_lo(NH // 2 - 1)
        end_slabs(8)
        na.close()
        nsx.close()

        onto_residual(FIRST_SLAB["w_out"], 3)
        second.close()

        xa = ExitStack()
        xq = sb("xq", [P, 4, 512], ctx=xa)
        xs = sb("xs", [P, NT * XH, T], ctx=xa)
        xpT = sb("xpT", [P, XH, NT, T], ctx=xa)
        xneg = sb("xneg", [P, NT * XH], ctx=xa)
        xden = sb("xden", [P, NT * XH], ctx=xa)
        X_ = {n: sem("xa_" + n) for n in ("s_done", "max_ready", "exp_ready", "scaled", "t_done",
                                          "pT_ready", "o_done", "out_hi")}
        s_xa = FIRST_SLAB["xa_wq"]
        with nc.Block(no_gpsimd_drain=True) as block:
            act_step, dve_step = copy_out(xq, s_xa, 4)

            @block.sync
            def _(sp):
                feed(sp, s_xa + 4)

            @block.tensor
            def _(pe):
                project(pe, s_xa, 4, turned_slab, src_in)

            @block.scalar
            def _(act):
                act_step(act)

            @block.vector
            def _(dve):
                dve_step(dve)
        end_slabs(4)
        tile_of = lambda v, f: v[:, f // 2, (f % 2) * T:(f % 2 + 1) * T]
        by2 = lambda b, n: psum[:, b:b + n, :].rearrange("p b (j c) -> p (b j) c", c=T)
        XT = XD // P
        with nc.Block(no_gpsimd_drain=True) as block:
            @block.tensor
            def _(pe):
                for h in range(XH):
                    for t in range(NT):
                        for j in range(XT):
                            mm = pe.matmul(by2(h, 1)[:, t, :], tile_of(xq, XT * h + j)[:, t * P:(t + 1) * P],
                                           tile_of(xkv, XT * h + j), start=(j == 0), stop=(j == XT - 1))
                    mm.then_inc(X_["s_done"], 1)

                def turn(h):
                    pe.wait_ge(X_["scaled"], h + 1)
                    for m in range(NT):
                        for t in range(NT):
                            mm = pe.transpose(by2(4, 4)[:, h * NT + m, t * P:(t + 1) * P],
                                              xs[:, h * NT + t, m * P:(m + 1) * P], ident[:, :])
                    mm.then_inc(X_["t_done"], 1)

                turn(0)
                for h in range(XH):
                    if h + 1 < XH:
                        turn(h + 1)
                    pe.wait_ge(X_["pT_ready"], h + 1)
                    for j in range(XT):
                        for m in range(NT):
                            v = xkv[:, 4 + h, m * 256 + j * P:m * 256 + (j + 1) * P]
                            mm = pe.matmul(by2(h, 1)[:, j, :], v, xpT[:, h, m, :],
                                           start=(m == 0), stop=(m == NT - 1))
                    mm.then_inc(X_["o_done"], 1)

            @block.scalar
            def _(act):
                def exps(h):
                    act.wait_ge(X_["max_ready"], h + 1)
                    for i in range(h * NT, (h + 1) * NT):
                        e = act.activation(xs[:, i, :], by2(h, 1)[:, i % NT, :], ACT.Exp, bias=xneg[:, i:i + 1],
                                           scale=XD ** -0.5, accum_out=xden[:, i:i + 1])
                    e.then_inc(X_["exp_ready"], 1)

                def out_hi(h):
                    act.wait_ge(X_["o_done"], h + 1)
                    act.activation(inH[:, 2 * h:2 * h + 2, :], by2(h, 1), ACT.Copy).then_inc(X_["out_hi"], 1)

                for h in range(XH):
                    exps(h)
                for h in range(XH):
                    act.wait_ge(X_["t_done"], h + 1)
                    act.activation(xpT[:, h, :, :], by2(4, 4)[:, h * NT:(h + 1) * NT, :],
                                   ACT.Copy).then_inc(X_["pT_ready"], 1)
                    if h > 0:
                        out_hi(h - 1)
                out_hi(XH - 1)

            @block.vector
            def _(dve):
                of = lambda v, h: v[:, h * NT:(h + 1) * NT]
                def maxima(h):
                    dve.wait_ge(X_["s_done"], h + 1)
                    dve_chain.step(dve, dve.tensor_reduce(of(xneg, h), by2(h, 1), AX.X, ALU.max, negate=True))
                    dve.tensor_scalar(of(xneg, h), of(xneg, h), XD ** -0.5, None, ALU.mult)\
                       .then_inc(X_["max_ready"], 1)

                def scale(h):
                    dve.wait_ge(X_["exp_ready"], h + 1)
                    dve_chain.step(dve, dve.reciprocal(of(xden, h), of(xden, h)))
                    for i in range(h * NT, (h + 1) * NT):
                        o = dve.tensor_scalar(xs[:, i, :], xs[:, i, :], xden[:, i:i + 1], None, ALU.mult)
                    o.then_inc(X_["scaled"], 1)

                maxima(0)
                for h in range(XH):
                    if h + 1 < XH:
                        maxima(h + 1)
                    scale(h)
                for h in range(XH):
                    dve.wait_ge(X_["out_hi"], h + 1)
                    dve.tensor_tensor(inL[:, 2 * h:2 * h + 2, :], by2(h, 1), inH[:, 2 * h:2 * h + 2, :].bitcast(F32),
                                      ALU.subtract)
        onto_residual(FIRST_SLAB["xa_wo"], 5)
        xa.close()
        kv.close()

        s_pq, s_down, s_up = FIRST_SLAB["peer_wq"], FIRST_SLAB["peer_down"], FIRST_SLAB["peer_up"]
        N_DOWN, N_UP = PK // 2, PK // 2
        KH = PH * PTOP
        assert KH == P and PK == P
        pr = ExitStack()
        HID = sb("hidden", [P, PK, T], ctx=pr)
        iota_e = sb("iota_e", [P, P], ctx=pr)
        gbx = ExitStack()
        IT, JT, GT = (sb(n, [P, T], ctx=gbx) for n in ("IT", "JT", "GT"))
        TAIL = 80
        room = HID[:, TAIL:PK, :].rearrange("p i t -> p (i t)")
        taken = {"words": 0}

        def in_room(*shape, dt=F32):
            n = int(np.prod(shape))
            lo = taken["words"]
            taken["words"] += n
            assert taken["words"] <= (PK - TAIL) * T
            v = room[:, lo:lo + n]
            v = v if dt is F32 else v.bitcast(dt)
            letters = "abcd"[:len(shape)]
            return v.rearrange(f"p ({' '.join(letters)}) -> p {' '.join(letters)}",
                               **dict(zip(letters[1:], shape[1:])))

        NHALF = 2 * PH
        pqT = in_room(PH, T)
        subk = in_room(PH, PK)
        work = in_room(NHALF, PK)
        cand = in_room(PH, PTOP * PTOP)
        cwork = in_room(PH, PTOP * PTOP)
        vals = in_room(NHALF, PTOP)
        idx_u = in_room(NHALF, PTOP, dt=U32)
        idx_f = in_room(NHALF, PTOP)
        ts_ = in_room(PH, PTOP)
        tpos = in_room(PH, PTOP, dt=U32)
        ab_u = in_room(2, PH, PTOP, dt=U32)
        ab_f = in_room(2, PH, PTOP)
        zsum = in_room(PH, 1)
        tables = in_room(3, NT, KH)
        R_ = {n: sem("peer_" + n) for n in (
            "loads", "iota_ready", "scored", "scores_read", "exp_in", "exp_out", "table_ready", "turned",
            "room_left", "j_near", "j_ready", "i_ready", "gi_ready", "g_done", "g_used", "tile_hi", "tile_ready", "half_used",
            "up_hi", "up_ready")}
        with nc.Block(no_gpsimd_drain=True) as block:
            act_step, dve_step = copy_out(pqT.rearrange("p (a c) t -> p a (c t)", c=2), s_pq, 4)

            @block.sync
            def _(sp):
                sp.dma_start(subk, ins["subkeys"]).then_inc(R_["loads"], 16)
                feed(sp, s_pq + 4)
                sp.wait_ge(R_["loads"], 16)

            @block.gpsimd
            def _(pool):
                pool.iota(iota_e[:, :], pattern=[[1, P]], base=0, channel_multiplier=0,
                          allow_small_or_imprecise_dtypes=True).then_inc(R_["iota_ready"], 1)

            @block.tensor
            def _(pe):
                project(pe, s_pq, 4, turned_slab, src_in)

            @block.scalar
            def _(act):
                act_step(act)

            @block.vector
            def _(dve):
                dve_step(dve)
        end_slabs(4)

        LOWEST = -3.0e38
        N_STEPS = 17
        EXP_STEP = 11
        SCORE_SLAB = 12
        TABLE_SLAB = NT * N_STEPS + 2
        assert 2 * (TABLE_SLAB + 4) <= TAIL and TABLE_SLAB % GROUP == 0
        s = by4(4, 4)

        def select(dve, t, step):
            def each_row(n, op):
                for i in range(n):
                    o = op(i)
                dve_chain.step(dve, o)

            wide = lambda v: v.rearrange("p h (k a) -> p h k a", k=PTOP)
            if step == 0:
                dve.wait_ge(R_["scored"], t + 1)
                each_row(NHALF, lambda i: dve.max(vals[:, i, 0:8], s[:, i, :]))
            elif step == 1:
                each_row(NHALF, lambda i: dve.max_index(idx_u[:, i, 0:8], vals[:, i, 0:8], s[:, i, :]))
            elif step == 2:
                each_row(NHALF, lambda i: dve.match_replace(work[:, i, :], vals[:, i, 0:8], s[:, i, :], LOWEST))
                dve.sem_inc(R_["scores_read"], 1)
            elif step == 3:
                each_row(NHALF, lambda i: dve.max(vals[:, i, 8:16], work[:, i, :]))
            elif step == 4:
                each_row(NHALF, lambda i: dve.max_index(idx_u[:, i, 8:16], vals[:, i, 8:16], work[:, i, :]))
            elif step == 5:
                dve.tensor_copy(idx_f, idx_u)
                dve_chain.step(dve, dve.tensor_tensor(
                    cand.rearrange("p h (a b) -> p h a b", a=PTOP),
                    vals[:, 0:PH, :].unsqueeze(3).to_broadcast([P, PH, PTOP, PTOP]),
                    vals[:, PH:NHALF, :].unsqueeze(2).to_broadcast([P, PH, PTOP, PTOP]), ALU.add))
            elif step == 6:
                each_row(PH, lambda h: dve.max(ts_[:, h, 0:8], cand[:, h, :]))
            elif step == 7:
                each_row(PH, lambda h: dve.max_index(tpos[:, h, 0:8], ts_[:, h, 0:8], cand[:, h, :]))
            elif step == 8:
                each_row(PH, lambda h: dve.match_replace(cwork[:, h, :], ts_[:, h, 0:8], cand[:, h, :], LOWEST))
            elif step == 9:
                each_row(PH, lambda h: dve.max(ts_[:, h, 8:16], cwork[:, h, :]))
            elif step == 10:
                each_row(PH, lambda h: dve.max_index(tpos[:, h, 8:16], ts_[:, h, 8:16], cwork[:, h, :]))
            elif step == EXP_STEP:
                dve_chain.step(dve, dve.tensor_copy(zsum, ts_[:, :, 0:1]))
                dve.tensor_tensor(ts_, ts_, zsum.to_broadcast([P, PH, PTOP]),
                                  ALU.subtract).then_inc(R_["exp_in"], 1)
                dve.tensor_single_scalar(ab_u[:, 0, :, :], tpos, 4, ALU.logical_shift_right)
                dve_chain.step(dve, dve.tensor_single_scalar(ab_u[:, 1, :, :], tpos, 15, ALU.bitwise_and))
                dve_chain.step(dve, dve.tensor_copy(ab_f, ab_u))
            elif step in (12, 14):
                c, eq = (0, cand) if step == 12 else (1, cwork)
                dve_chain.step(dve, dve.tensor_tensor(
                    wide(eq), ab_f[:, c, :, :].unsqueeze(3).to_broadcast([P, PH, PTOP, PTOP]),
                    iota_e[:, 0:PTOP].unsqueeze(1).unsqueeze(1).to_broadcast([P, PH, PTOP, PTOP]),
                    ALU.is_equal))
            elif step in (13, 15):
                c, eq = (0, cand) if step == 13 else (1, cwork)
                dve_chain.step(dve, dve.tensor_tensor(
                    wide(eq), wide(eq),
                    idx_f[:, c * PH:(c + 1) * PH, :].unsqueeze(2).to_broadcast([P, PH, PTOP, PTOP]), ALU.mult))
                dve_chain.step(dve, dve.tensor_reduce(
                    tables[:, c, t, :], eq.rearrange("p h (k a) -> p (h k) a", k=PTOP), AX.X, ALU.add))
            else:
                dve.wait_ge(R_["exp_out"], t + 1)
                dve_chain.step(dve, dve.tensor_reduce(zsum, ts_, AX.X, ALU.add))
                dve_chain.step(dve, dve.reciprocal(zsum, zsum))
                dve.tensor_tensor(tables[:, 2, t, :].rearrange("p (h k) -> p h k", k=PTOP), ts_,
                                  zsum.to_broadcast([P, PH, PTOP]), ALU.mult).then_inc(R_["table_ready"], 1)

        with nc.Block(no_gpsimd_drain=True) as block:
            @block.sync
            def _(sp):
                feed(sp, s_down + N_DOWN)

            @block.tensor
            def _(pe):
                def scores(t):
                    for half_ in range(2):
                        r = slice(half_ * 64, (half_ + 1) * 64)
                        for h in range(PH):
                            mm = pe.matmul(s[:, half_ * PH + h, :], pqT[r, h, t * P:(t + 1) * P],
                                           subk[r, h, :], start=True, stop=True)
                    mm.then_inc(R_["scored"], 1)

                scores(0)
                project(pe, s_down, SCORE_SLAB, turned_slab, src_in)
                pe.wait_ge(R_["scores_read"], 1)
                scores(1)
                project(pe, s_down + SCORE_SLAB, TABLE_SLAB - SCORE_SLAB, turned_slab, src_in, before=SCORE_SLAB)
                pe.wait_ge(R_["table_ready"], NT)
                for c in range(3):
                    for t in range(NT):
                        mm = pe.transpose(psum[:, 4 + c, t * P:(t + 1) * P], tables[:, c, t, :], ident[:, :])
                mm.then_inc(R_["turned"], 1)
                project(pe, s_down + TABLE_SLAB, N_DOWN - TABLE_SLAB, turned_slab, src_in, before=TABLE_SLAB)
                pe.wait_ge(R_["room_left"], 1)
                for n in range(NT):
                    for c in range(2):
                        pe.matmul(psum[:, 4 + 2 * n + c, :], ident[:, :], x[:, n, c * 512:(c + 1) * 512],
                                  start=True, stop=False)

            @block.scalar
            def _(act):
                def body(s, it):
                    split_hi(act, s + 1, it)
                    act.wait_ge(slab_used, at(it, s + 1))
                    act.activation(HID[:, bass.ds(at(it, 2 * (s - s_down), 2 * GROUP), 2), :]
                                   .rearrange("p i t -> p (i t)"),
                                   psum[:, s % BANKS, :], ACT.Gelu_apprx_tanh).then_inc(bank_read, 1)

                for i in range(TAIL // 2):
                    body(s_down + i, None)
                    if i < NT * N_STEPS and i % N_STEPS == EXP_STEP:
                        act.wait_ge(R_["exp_in"], i // N_STEPS + 1)
                        act.activation(ts_, ts_, ACT.Exp).then_inc(R_["exp_out"], 1)
                act.wait_ge(R_["room_left"], 1)
                with act.Fori(TAIL // 2 // GROUP, N_DOWN // GROUP) as it:
                    for j in range(GROUP):
                        body(s_down + j, it)

            @block.vector
            def _(dve):
                dve.wait_ge(R_["iota_ready"], 1)
                for i in range(TABLE_SLAB + 2):
                    split_lo(dve, s_down + i + 1)
                    if i < NT * N_STEPS:
                        select(dve, i // N_STEPS, i % N_STEPS)
                dve.wait_ge(R_["turned"], 1)
                for c, dst in enumerate((IT, JT, GT)):
                    o = dve.tensor_copy(dst[:, :], psum[:, 4 + c, 0:T])
                o.then_inc(R_["room_left"], 1)
                per_slab(dve, s_down + TABLE_SLAB + 2, N_DOWN - TABLE_SLAB - 2,
                         lambda s, it: split_lo(dve, s + 1, it))
        end_slabs(N_DOWN)

        QT = 2
        NBUF = 4
        NSTEP = T // QT
        hot = x[:, :, :].rearrange("p n d -> p (n d)").rearrange("p (q s k c) -> p q s k c", q=NBUF, s=2, k=QT)
        with nc.Block(no_gpsimd_drain=True) as block:
            step_of = lambda it, c: c if it is None else it * NBUF + c

            def steps(eng, body):
                for q in range(NBUF):
                    body(q, None)
                with eng.Fori(1, NSTEP // NBUF) as it:
                    for q in range(NBUF):
                        body(q, it)

            pair = lambda v, q, it: v[:, bass.ds(step_of(it, q) * QT, QT)].unsqueeze(2).to_broadcast([P, QT, P])

            by_scalar = lambda it, c: c if it is None else it * (NBUF - 1) + c

            @block.scalar
            def _(act):
                def body(q, it):
                    if q == NBUF - 1:
                        return
                    if it is not None:
                        act.wait_ge(R_["g_done"], step_of(it, q - NBUF + 1))
                    v = hot[:, q, 0, :, :]
                    for k in range(QT):
                        o = act.activation(v[:, k, :], iota_e[:, :], ACT.Abs, scale=-1.0,
                                           bias=JT[:, bass.ds(step_of(it, q) * QT + k, 1)])
                    o.then_inc(R_["j_near"], 1)
                    act.wait_ge(R_["j_near"], by_scalar(it, q + 1))
                    act.activation(v, v, ACT.Relu, scale=-1.0, bias=1.0).then_inc(R_["j_ready"], 1)
                steps(act, body)

            @block.gpsimd
            def _(pool):
                def body(q, it):
                    pool.wait_ge(R_["i_ready"], step_of(it, q + 1))
                    v = hot[:, q, 1, :, :]
                    pool.tensor_tensor(v, v, pair(GT, q, it), ALU.mult).then_inc(R_["gi_ready"], 1)
                steps(pool, body)
                pool.wait_ge(R_["gi_ready"], NSTEP)

            @block.tensor
            def _(pe):
                def body(q, it):
                    if q < NBUF - 1:
                        pe.wait_ge(R_["j_ready"], by_scalar(it, q + 1))
                    pe.wait_ge(R_["gi_ready"], step_of(it, q + 1))
                    if it is not None:
                        pe.wait_ge(R_["g_used"], step_of(it, q - NBUF + 1))
                    for k in range(QT):
                        mm = pe.matmul(psum[:, q, k * P:(k + 1) * P], hot[:, q, 0, k, :], hot[:, q, 1, k, :],
                                       start=True, stop=True)
                    mm.then_inc(R_["g_done"], 1)
                steps(pe, body)

            @block.vector
            def _(dve):
                def gated(q, step):
                    dve.wait_ge(R_["g_done"], step + 1)
                    v = HID[:, :, bass.ds(step * QT, QT)].rearrange("p i k -> p k i")
                    dve.tensor_tensor(v, v, psum[:, q, 0:QT * P].rearrange("p (k i) -> p k i", k=QT),
                                      ALU.mult).then_inc(R_["g_used"], 1)

                def one_hot(q, it):
                    if q == NBUF - 1:
                        dve.tensor_tensor(hot[:, q, 0, :, :], iota_e[:, :].unsqueeze(1).to_broadcast([P, QT, P]),
                                          pair(JT, q, it), ALU.is_equal)
                    dve.tensor_tensor(hot[:, q, 1, :, :], iota_e[:, :].unsqueeze(1).to_broadcast([P, QT, P]),
                                      pair(IT, q, it), ALU.is_equal).then_inc(R_["i_ready"], 1)

                for q in range(NBUF):
                    one_hot(q, None)
                with dve.Fori(1, NSTEP // NBUF) as it:
                    for q in range(NBUF):
                        gated(q, it * NBUF + (q - NBUF))
                        one_hot(q, it)
                for q in range(NBUF):
                    gated(q, NSTEP - NBUF + q)
        gbx.close()

        wgtH = sb("wgtH", [P, 2, T], F32R, ctx=pr)
        wgtL = sb("wgtL", [P, 2, T], F32R, ctx=pr)
        fin_gain = x[:, 0, :]
        with nc.Block(no_gpsimd_drain=True) as block:
            def up_slabs(eng, body):
                for j in range(GROUP):
                    body(s_up + j, None)
                with eng.Fori(1, N_UP // GROUP - 1) as it:
                    for j in range(GROUP):
                        body(s_up + j, it)
                for j in range(N_UP - GROUP, N_UP):
                    body(s_up + j, None)

            @block.sync
            def _(sp):
                sp.dma_start(fin_gain, ins["norm_final"].partition_broadcast(P)).then_inc(R_["loads"], 16)
                feed(sp, N_SLABS)
                sp.wait_ge(R_["loads"], 32)

            @block.tensor
            def _(pe):
                def body(s, it):
                    w = weights_of(s % RING, 2)
                    for a in range(2):
                        if a == 0 and (it is not None or s >= s_up + RING):
                            pe.wait_ge(R_["up_ready"], at(it, s - s_up - RING + 1))
                        else:
                            pe.wait_ge(split_ready, at(it, s + 1))
                        pe.wait_ge(R_["tile_ready"], at(it, 2 * (s - s_up) + a + 1, 2 * GROUP))
                        last = s == N_SLABS - 1 and a == 1
                        for n in range(NT):
                            for c in range(2):
                                mm = three(pe, psum[:, 4 + 2 * n + c, :],
                                           [v[:, a, n * P:(n + 1) * P] for v in (wgtH, wgtL)],
                                           [v[:, a, c * 512:(c + 1) * 512] for v in w], False, last)
                        mm.then_inc((R_["half_used"], slab_used)[a], 1)
                up_slabs(pe, body)

            half = lambda t, slot, a: t[:, slot, a * D:(a + 1) * D]

            @block.scalar
            def _(act):
                def tile_hi(i, a):
                    act.activation(wgtH[:, a, :], HID[:, bass.ds(i, 1), :].rearrange("p i t -> p (i t)"),
                                   ACT.Copy).then_inc(R_["tile_hi"], 1)

                def body(s, it):
                    slot = s % RING
                    for a in range(2):
                        act.wait_ge(*((R_["half_used"], at(it, s - s_up + 1)), (slab_used, at(it, s + 1)))[a])
                        if s + 1 < N_SLABS:
                            tile_hi(at(it, 2 * (s + 1 - s_up) + a, 2 * GROUP), a)
                        if s + RING < N_SLABS:
                            if a == 0:
                                act.wait_ge(slab_landed[slot], at(it, 16 * ((s + RING) // RING + 1), 16 * GROUP // RING))
                            act.activation(half(wH, slot, a), half(ring, slot, a),
                                           ACT.Copy).then_inc((R_["up_hi"], hi_ready)[a], 1)

                for a in range(2):
                    tile_hi(a, a)
                split_hi(act, s_up + 1)
                up_slabs(act, body)

            @block.vector
            def _(dve):
                def tile_lo(i, a):
                    dve.wait_ge(R_["tile_hi"], i + 1)
                    dve.tensor_tensor(wgtL[:, a, :], HID[:, bass.ds(i, 1), :].rearrange("p i t -> p (i t)"),
                                      wgtH[:, a, :].bitcast(F32), ALU.subtract).then_inc(R_["tile_ready"], 1)

                def body(s, it):
                    slot = s % RING
                    for a in range(2):
                        if s + 1 < N_SLABS:
                            tile_lo(at(it, 2 * (s + 1 - s_up) + a, 2 * GROUP), a)
                        if s + RING < N_SLABS:
                            dve.wait_ge(*((R_["up_hi"], at(it, s - s_up + 1)), (hi_ready, at(it, s + RING + 1)))[a])
                            dve.tensor_tensor(half(wL, slot, a), half(ring, slot, a), half(wH, slot, a).bitcast(F32),
                                              ALU.subtract).then_inc((R_["up_ready"], split_ready)[a], 1)

                for a in range(2):
                    tile_lo(a, a)
                split_lo(dve, s_up + 1)
                up_slabs(dve, body)

        fin_sq, fin_ready, out_stored = sem("final_squares"), sem("final_ready"), sem("out_stored")
        total = psum[:, 4:8, :].rearrange("p (n b) c -> p n (b c)", n=NT)
        result = HID[:, 0:NT * D // T, :].rearrange("p (n i) t -> p n (i t)", n=NT)
        squares = HID[:, NT * D // T:2 * NT * D // T, :].rearrange("p (n i) t -> p n (i t)", n=NT)
        with nc.Block(no_gpsimd_drain=True) as block:
            @block.scalar
            def _(act):
                for t in range(NT):
                    act.activation(squares[:, t, :], total[:, t, :], ACT.Square, scale=D ** -0.5,
                                   accum_out=mean_sq[:, t:t + 1]).then_inc(fin_sq, 1)

            @block.gpsimd
            def _(pool):
                pool.wait_ge(fin_sq, NT)
                inv_sqrt(pool, rstd[:, 0:NT], mean_sq[:, 0:NT])

            @block.vector
            def _(dve):
                dve.wait_ge(rstd_ready, rstds["n"])
                for t in range(NT):
                    dve.scalar_tensor_tensor(out=result[:, t, :], in0=total[:, t, :], scalar=rstd[:, t:t + 1],
                                             in1=fin_gain, op0=ALU.mult, op1=ALU.mult).then_inc(fin_ready, 1)

            @block.sync
            def _(sp):
                for t in range(NT):
                    sp.wait_ge(fin_ready, t + 1)
                    sp.dma_start(out[0, t * P:(t + 1) * P, :], result[:, t, :]).then_inc(out_stored, 16)
                sp.wait_ge(out_stored, 16 * NT)
        pr.close()


def lay_out(inputs):
    a = {k: np.asarray(v) for k, v in inputs.items()}

    def cols(w, order=None):
        w = w.reshape(KD, P, -1, 256)
        return w.transpose(2, 1, 0, 3).reshape(-1, P, SLAB)

    def vec(v):
        return v.reshape(KD, P).T

    w_in = a["w_in"][0]
    sec = lambda *n: np.concatenate([w_in[:, D * i:D * (i + 1)] for i in n], axis=1)
    parts = [cols(sec(0, 1, 3, 7, 8)), cols(sec(4, 5, 2, 6)),
             cols(a["w_hg_out"][0]), cols(a["w_sb_out"][0]), cols(a["w_o"][0])]
    fi = a["w_ffn_in"][0].reshape(KD, P, 2, FT, P)
    parts.append(fi.transpose(3, 1, 0, 2, 4).reshape(FT, P, SLAB))
    fo = a["w_ffn_out"][0].reshape(FT // 2, 2, P, D)
    parts.append(fo.transpose(0, 2, 1, 3).reshape(FT // 2, P, SLAB))
    w2 = a["w_in_2"][0]
    o = np.cumsum([0, 256, 256, 512, 512, 16, 512, 128, 128, 128, 128, 128, 128, 24])
    gq, gk, gv, gr, glr, nq, kc, vc, ks, vs, kw, vw, ng = (w2[:, o[i]:o[i + 1]] for i in range(13))
    pad = np.zeros((D, 256 - 40), np.float32)
    parts.append(cols(np.concatenate([gq, gk, gr, nq, kc, vc, ks, kw, gv, vs, vw, glr, ng, pad], axis=1)))
    for n in ("xa_wk_2", "xa_wv_2", "w_out_2", "xa_wq_2", "xa_wo_2", "peer_wq_2"):
        parts.append(cols(a[n][0]))
    parts.append(cols(a["peer_down_2"][0].T))
    up = a["peer_up_2"][0].reshape(PK // 2, 2, P, D)
    parts.append(up.transpose(0, 2, 1, 3).reshape(PK // 2, P, SLAB))
    w_stream = np.concatenate(parts, axis=0)
    assert w_stream.shape == (N_SLABS, P, SLAB)

    gains = np.stack([vec(a["norm1_gain"][0]), vec(a["norm2_gain"][0]), vec(a["norm_mix_2"][0]),
                      vec(a["norm_xattn_2"][0]), vec(a["norm_mem_2"][0]), vec(a["norm_ffn_2"][0]),
                      vec(a["sb_q_norm"][0]), vec(a["sb_k_norm"][0]), vec(a["hg_out_norm"][0])], axis=1)
    lb_logits = a["lb_logits"].reshape(2, KD, P).transpose(2, 0, 1)

    paired = lambda v: v.reshape(CB // 2, 2 * ND, -1).transpose(1, 0, 2)
    cmp_w1 = np.stack([paired(a["cmp_k_w1_2"][0]), paired(a["cmp_v_w1_2"][0])], axis=1)
    cmp_pos = np.stack([paired(a["cmp_pos_k_2"][0])[:, :, 0], paired(a["cmp_pos_v_2"][0])[:, :, 0]], axis=1)
    gla_vec = np.concatenate([a["gla_gate_b_2"][0].reshape(2, P).T, a["gla_out_norm_2"][0].reshape(P, 1)], axis=1)
    return {
        "x": a["x"], "w_stream": w_stream, "gains": gains, "lb_logits": lb_logits,
        "cmp_w1": cmp_w1, "cmp_pos": cmp_pos, "cmp_k_w2": a["cmp_k_w2_2"][0], "cmp_v_w2": a["cmp_v_w2_2"][0],
        "rel_bias": a["rel_bias_2"], "buckets": bucket_rows(), "gla_w2": a["gla_gate_w2_2"][0], "gla_vec": gla_vec,
        "mem": a["mem_2"], "norm_final": a["norm_final_2"],
        "subkeys": a["peer_subkeys_2"][0].transpose(1, 3, 0, 2).reshape(P, PH, PK),
    }


def bucket_rows():
    n = np.arange(T)
    exact = BUCKETS // 2
    log_ratio = np.log(np.maximum(n, 1).astype(np.float32) / np.float32(exact)) / np.float32(
        np.log(MAX_DIST / exact))
    large = np.minimum(exact + (log_ratio * (BUCKETS - exact)).astype(np.int32), BUCKETS - 1)
    bucket = np.where(n < exact, n, large)
    up = np.zeros((BUCKETS + 1, 2 * T - 1), np.float32)
    up[BUCKETS, :T - 1] = 1
    up[bucket, T - 1 + n] = 1
    return np.stack([up, up[:, ::-1]], axis=1)


_OUT = (1, T, D)


def kernel(**inputs):
    import concourse.bacc as _bacc
    from concourse.bass_utils import run_bass_kernel_spmd as _run

    nc = _bacc.Bacc("TRN2", target_bir_lowering=False, num_devices=1)
    arrays, args = {}, {}
    for name, v in lay_out(inputs).items():
        v = np.ascontiguousarray(v)
        arrays[f"in_{name}"] = v
        args[name] = nc.dram_tensor(f"in_{name}", v.shape, mybir.dt.from_np(v.dtype), kind="ExternalInput").ap()
    out = nc.dram_tensor("out_0", _OUT, F32, kind="ExternalOutput").ap()
    build(nc, args, out)
    r = _run(nc, [arrays], core_ids=[0])
    return r.results[0]["out_0"]
```
